# Optimizing a Trainium2 kernel written in Bass

```python
import math
import jax, jax.numpy as jnp
from jax import lax
import numpy as np

D_MODEL = 1024
BATCH = 1
SEQ = 256
DEPTH = 2

N_MIXERS = 2
Q_BLOCK = 128
ROPE_THETA = 10000.0
NORM_EPS = 1e-6

DIFF_HEAD_DIM = 64
DIFF_HEADS = D_MODEL // (2 * DIFF_HEAD_DIM)
DIFF_QK_WIDTH = DIFF_HEADS * 2 * DIFF_HEAD_DIM
DIFF_V_DIM = 2 * DIFF_HEAD_DIM
DIFF_V_WIDTH = DIFF_HEADS * DIFF_V_DIM

MLA_NOPE = 128
MLA_ROPE = 64
MLA_QK_DIM = MLA_NOPE + MLA_ROPE
MLA_V = 128
MLA_HEADS = D_MODEL // MLA_V
MLA_Q_LORA = 3 * D_MODEL // 8
MLA_KV_LORA = D_MODEL // 4
MLA_A_WIDTH = MLA_Q_LORA + MLA_KV_LORA + MLA_ROPE

N_GROUPS = 8
EXPERTS_PER_GROUP = 8
N_EXPERTS = N_GROUPS * EXPERTS_PER_GROUP
TOP_K = 2
EXPERT_FF = D_MODEL // 4


def rms_norm(x, gain):
    xf = x.astype(jnp.float32)
    y = xf * lax.rsqrt(jnp.mean(xf * xf, axis=-1, keepdims=True) + NORM_EPS)
    return (y * gain.astype(jnp.float32)).astype(x.dtype)

def rope(x, pos):
    d = x.shape[-1]
    half = d // 2
    inv_freq = 1.0 / (ROPE_THETA ** (jnp.arange(0, d, 2, dtype=jnp.float32) / d))
    ang = pos.astype(jnp.float32)[:, None] * inv_freq[None, :]
    shape = (pos.shape[0],) + (1,) * (x.ndim - 3) + (half,)
    cos = jnp.cos(ang).reshape(shape)
    sin = jnp.sin(ang).reshape(shape)
    xf = x.astype(jnp.float32)
    x1, x2 = xf[..., :half], xf[..., half:]
    return jnp.concatenate([x1 * cos - x2 * sin, x2 * cos + x1 * sin], axis=-1).astype(x.dtype)

def causal_softmax(scores, blk, seq):
    qpos = blk * Q_BLOCK + jnp.arange(Q_BLOCK)
    mask = jnp.arange(seq)[None, :] <= qpos[:, None]
    return jax.nn.softmax(jnp.where(mask, scores, -jnp.inf), axis=-1)

def query_block_map(fn, *qs):
    b, s = qs[0].shape[:2]
    nb = s // Q_BLOCK
    blocks = tuple(q.reshape(b, nb, Q_BLOCK, *q.shape[2:]).swapaxes(0, 1) for q in qs)
    out = lax.map(lambda a: fn(a[0], *a[1:]), (jnp.arange(nb), *blocks))
    return out.swapaxes(0, 1).reshape(b, s, *out.shape[3:])

def diff_attention(h, w_in, q_gain, k_gain, lq1, lk1, lq2, lk2, subln, w_out, lambda_init, pos):
    b, s, _ = h.shape
    qkv = h @ w_in
    q, k, v = jnp.split(qkv, [DIFF_QK_WIDTH, 2 * DIFF_QK_WIDTH], axis=-1)
    q = rope(rms_norm(q.reshape(b, s, DIFF_HEADS, 2, DIFF_HEAD_DIM), q_gain), pos)
    k = rope(rms_norm(k.reshape(b, s, DIFF_HEADS, 2, DIFF_HEAD_DIM), k_gain), pos)
    v = v.reshape(b, s, DIFF_HEADS, DIFF_V_DIM)
    q1, q2 = q[..., 0, :], q[..., 1, :]
    k1, k2 = k[..., 0, :], k[..., 1, :]
    lam = (jnp.exp(jnp.sum(lq1.astype(jnp.float32) * lk1.astype(jnp.float32)))
           - jnp.exp(jnp.sum(lq2.astype(jnp.float32) * lk2.astype(jnp.float32)))
           + lambda_init)
    scale = DIFF_HEAD_DIM ** -0.5

    def block(blk, qb1, qb2):
        s1 = jnp.einsum('bqhd,bkhd->bhqk', qb1, k1).astype(jnp.float32) * scale
        s2 = jnp.einsum('bqhd,bkhd->bhqk', qb2, k2).astype(jnp.float32) * scale
        a = causal_softmax(s1, blk, s) - lam * causal_softmax(s2, blk, s)
        return jnp.einsum('bhqk,bkhd->bqhd', a.astype(v.dtype), v)

    o = query_block_map(block, q1, q2)
    o = rms_norm(o, subln) * (1.0 - lambda_init)
    return o.reshape(b, s, DIFF_V_WIDTH) @ w_out

def mla_attention(h, w_a, q_a_gain, kv_a_gain, w_qb, w_kvb, q_gain, k_gain, w_out, pos):
    b, s, _ = h.shape
    a = h @ w_a
    cq, ckv, k_pe = jnp.split(a, [MLA_Q_LORA, MLA_Q_LORA + MLA_KV_LORA], axis=-1)
    q = (rms_norm(cq, q_a_gain) @ w_qb).reshape(b, s, MLA_HEADS, MLA_QK_DIM)
    kv = (rms_norm(ckv, kv_a_gain) @ w_kvb).reshape(b, s, MLA_HEADS, MLA_NOPE + MLA_V)
    k_nope, v = kv[..., :MLA_NOPE], kv[..., MLA_NOPE:]
    k_pe = jnp.broadcast_to(k_pe[:, :, None, :], (b, s, MLA_HEADS, MLA_ROPE))
    k = jnp.concatenate([k_nope, k_pe], axis=-1)
    q = rms_norm(q, q_gain)
    k = rms_norm(k, k_gain)
    q = jnp.concatenate([q[..., :MLA_NOPE], rope(q[..., MLA_NOPE:], pos)], axis=-1)
    k = jnp.concatenate([k[..., :MLA_NOPE], rope(k[..., MLA_NOPE:], pos)], axis=-1)
    scale = MLA_QK_DIM ** -0.5

    def block(blk, qb):
        sc = jnp.einsum('bqhd,bkhd->bhqk', qb, k).astype(jnp.float32) * scale
        p = causal_softmax(sc, blk, s)
        return jnp.einsum('bhqk,bkhd->bqhd', p.astype(v.dtype), v)

    o = query_block_map(block, q)
    return o.reshape(b, s, MLA_HEADS * MLA_V) @ w_out

def hier_moe(h, w_group, b_group, w_expert, b_expert, w_gate, w_up, w_down):
    b, s, d = h.shape
    t = h.reshape(-1, d)
    n_tok = t.shape[0]
    p_group = jax.nn.softmax((t @ w_group + b_group).astype(jnp.float32), axis=-1)
    g_w, g_idx = lax.top_k(p_group, 1)
    e_logits = (t @ w_expert + b_expert).astype(jnp.float32).reshape(n_tok, N_GROUPS, EXPERTS_PER_GROUP)
    e_logits = jnp.take_along_axis(e_logits, g_idx[:, :, None], axis=1)[:, 0]
    e_w, e_idx = lax.top_k(jax.nn.softmax(e_logits, axis=-1), TOP_K)
    weights = g_w * (e_w / jnp.sum(e_w, axis=-1, keepdims=True))
    expert_id = g_idx * EXPERTS_PER_GROUP + e_idx
    combine = jnp.einsum('tk,tke->te', weights,
                         jax.nn.one_hot(expert_id, N_EXPERTS, dtype=jnp.float32)).astype(t.dtype)

    def body(e, acc):
        hid = jax.nn.silu(t @ w_gate[e]) * (t @ w_up[e])
        return acc + combine[:, e, None] * (hid @ w_down[e])

    out = lax.fori_loop(0, N_EXPERTS, body, jnp.zeros_like(t))
    return out.reshape(b, s, d)

def first_inputs(seed: int = 0) -> dict:
    key = jax.random.key(seed)
    ks = iter(jax.random.split(key, 40))
    nd = (DEPTH + 1) // 2
    nm = DEPTH // 2

    def nrm(shape, scale):
        return jax.random.normal(next(ks), shape, jnp.float32) * scale

    def gain(shape):
        return 1.0 + nrm(shape, 0.05)

    D = D_MODEL
    return {
        "x": nrm((BATCH, SEQ, D), 1.0),
        "attn_norm": gain((DEPTH, D)),
        "ffn_norm": gain((DEPTH, D)),
        "diff_w_in": nrm((nd, D, 2 * DIFF_QK_WIDTH + DIFF_V_WIDTH), D ** -0.5),
        "diff_q_norm": gain((nd, DIFF_HEAD_DIM)),
        "diff_k_norm": gain((nd, DIFF_HEAD_DIM)),
        "diff_lambda_q1": nrm((nd, DIFF_HEAD_DIM), 0.1),
        "diff_lambda_k1": nrm((nd, DIFF_HEAD_DIM), 0.1),
        "diff_lambda_q2": nrm((nd, DIFF_HEAD_DIM), 0.1),
        "diff_lambda_k2": nrm((nd, DIFF_HEAD_DIM), 0.1),
        "diff_subln": gain((nd, DIFF_V_DIM)),
        "diff_w_out": nrm((nd, DIFF_V_WIDTH, D), DIFF_V_WIDTH ** -0.5),
        "mla_w_a": nrm((nm, D, MLA_A_WIDTH), D ** -0.5),
        "mla_q_a_norm": gain((nm, MLA_Q_LORA)),
        "mla_kv_a_norm": gain((nm, MLA_KV_LORA)),
        "mla_w_qb": nrm((nm, MLA_Q_LORA, MLA_HEADS * MLA_QK_DIM), MLA_Q_LORA ** -0.5),
        "mla_w_kvb": nrm((nm, MLA_KV_LORA, MLA_HEADS * (MLA_NOPE + MLA_V)), MLA_KV_LORA ** -0.5),
        "mla_q_norm": gain((nm, MLA_QK_DIM)),
        "mla_k_norm": gain((nm, MLA_QK_DIM)),
        "mla_w_out": nrm((nm, MLA_HEADS * MLA_V, D), (MLA_HEADS * MLA_V) ** -0.5),
        "moe_w_group": nrm((DEPTH, D, N_GROUPS), D ** -0.5),
        "moe_b_group": nrm((DEPTH, N_GROUPS), 0.01),
        "moe_w_expert": nrm((DEPTH, D, N_EXPERTS), D ** -0.5),
        "moe_b_expert": nrm((DEPTH, N_EXPERTS), 0.01),
        "moe_w_gate": nrm((DEPTH, N_EXPERTS, D, EXPERT_FF), D ** -0.5),
        "moe_w_up": nrm((DEPTH, N_EXPERTS, D, EXPERT_FF), D ** -0.5),
        "moe_w_down": nrm((DEPTH, N_EXPERTS, EXPERT_FF, D), EXPERT_FF ** -0.5),
    }

def first_block(x, attn_norm, ffn_norm, diff_w_in, diff_q_norm, diff_k_norm,
              diff_lambda_q1, diff_lambda_k1, diff_lambda_q2, diff_lambda_k2,
              diff_subln, diff_w_out, mla_w_a, mla_q_a_norm, mla_kv_a_norm,
              mla_w_qb, mla_w_kvb, mla_q_norm, mla_k_norm, mla_w_out,
              moe_w_group, moe_b_group, moe_w_expert, moe_b_expert,
              moe_w_gate, moe_w_up, moe_w_down):
    pos = jnp.arange(x.shape[1])
    for i in range(DEPTH):
        h = rms_norm(x, attn_norm[i])
        j = i // N_MIXERS
        if i % N_MIXERS == 0:
            lambda_init = 0.8 - 0.6 * math.exp(-0.3 * i)
            x = x + diff_attention(h, diff_w_in[j], diff_q_norm[j], diff_k_norm[j],
                                   diff_lambda_q1[j], diff_lambda_k1[j],
                                   diff_lambda_q2[j], diff_lambda_k2[j],
                                   diff_subln[j], diff_w_out[j], lambda_init, pos)
        else:
            x = x + mla_attention(h, mla_w_a[j], mla_q_a_norm[j], mla_kv_a_norm[j],
                                  mla_w_qb[j], mla_w_kvb[j], mla_q_norm[j], mla_k_norm[j],
                                  mla_w_out[j], pos)
        h = rms_norm(x, ffn_norm[i])
        x = x + hier_moe(h, moe_w_group[i], moe_b_group[i], moe_w_expert[i], moe_b_expert[i],
                         moe_w_gate[i], moe_w_up[i], moe_w_down[i])
    return x


DEPTH_2 = 1

HEAD_DIM = 64
N_HEADS_SWA = D_MODEL // (2 * HEAD_DIM)
N_KV_SWA = max(1, N_HEADS_SWA // 4)
N_HEADS_FOX = D_MODEL // (2 * HEAD_DIM)
WINDOW = 128
BLOCK = 128
D_FF = ((8 * D_MODEL // 3 + 127) // 128) * 128
CONV_WIDTH = 3
EPS = 1e-6
NEG = -1e30

Q_A = N_HEADS_SWA * HEAD_DIM
KV_A = N_KV_SWA * HEAD_DIM
Q_B = N_HEADS_FOX * HEAD_DIM
F_B = N_HEADS_FOX
D_IN = Q_A + 2 * KV_A + 3 * Q_B + F_B
D_MIX = Q_A + Q_B


def rms_norm_2(x, g):
    xf = x.astype(jnp.float32)
    y = xf * lax.rsqrt(jnp.mean(xf * xf, axis=-1, keepdims=True) + EPS)
    return (y * g.astype(jnp.float32)).astype(x.dtype)

def modulate(h, shift, scale):
    return h * (1 + scale[:, None, :]) + shift[:, None, :]

def alibi_slopes(n_heads):
    return jnp.exp2(-8.0 * (jnp.arange(n_heads, dtype=jnp.float32) + 1) / n_heads)

def swa_attention(q, k, v, sinks):
    B, S, H, D = q.shape
    Hkv = k.shape[2]
    G = H // Hkv
    nb = S // BLOCK
    qb = q.reshape(B, nb, BLOCK, Hkv, G, D)

    def band(t):
        prev = jnp.pad(t[:, :S - BLOCK], ((0, 0), (BLOCK, 0), (0, 0), (0, 0)))
        return jnp.concatenate([prev.reshape(B, nb, BLOCK, Hkv, D),
                                t.reshape(B, nb, BLOCK, Hkv, D)], axis=2)

    kb, vb = band(k), band(v)
    scores = jnp.einsum('bnqhgd,bnkhd->bnhgqk', qb, kb).astype(jnp.float32) * (HEAD_DIM ** -0.5)
    n_idx = jnp.arange(nb)[:, None, None]
    q_idx = jnp.arange(BLOCK)[None, :, None]
    k_idx = jnp.arange(2 * BLOCK)[None, None, :]
    dist = (BLOCK + q_idx) - k_idx
    key_abs = n_idx * BLOCK - BLOCK + k_idx
    valid = (dist >= 0) & (dist < WINDOW) & (key_abs >= 0)
    slopes = alibi_slopes(H).reshape(Hkv, G)[:, :, None, None]
    scores = scores - slopes * dist[0].astype(jnp.float32)
    scores = jnp.where(valid[None, :, None, None], scores, NEG)
    sink = sinks.astype(jnp.float32).reshape(Hkv, G)[:, :, None, None]
    m = jnp.maximum(scores.max(axis=-1, keepdims=True), sink)
    p = jnp.exp(scores - m)
    probs = p / (p.sum(axis=-1, keepdims=True) + jnp.exp(sink - m))
    out = jnp.einsum('bnhgqk,bnkhd->bnqhgd', probs.astype(v.dtype), vb)
    return out.reshape(B, S, H, D)

def forgetting_attention(q, k, v, f_logit):
    B, S, H, D = q.shape
    nb = S // BLOCK
    F = jnp.cumsum(jax.nn.log_sigmoid(f_logit.astype(jnp.float32)), axis=1)
    Fk = F.transpose(0, 2, 1)
    qb = q.reshape(B, nb, BLOCK, H, D).transpose(1, 0, 2, 3, 4)
    Fq = Fk.reshape(B, H, nb, BLOCK).transpose(2, 0, 1, 3)
    k_pos = jnp.arange(S)

    def one_block(args):
        qi, Fi, n = args
        s = jnp.einsum('bqhd,bkhd->bhqk', qi, k).astype(jnp.float32) * (HEAD_DIM ** -0.5)
        s = s + (Fi[..., None] - Fk[:, :, None, :])
        q_pos = n * BLOCK + jnp.arange(BLOCK)
        s = jnp.where(k_pos[None, :] <= q_pos[:, None], s, NEG)
        p = jax.nn.softmax(s, axis=-1)
        return jnp.einsum('bhqk,bkhd->bqhd', p.astype(v.dtype), v)

    out = lax.map(one_block, (qb, Fq, jnp.arange(nb)))
    return out.transpose(1, 0, 2, 3, 4).reshape(B, S, H, D)

def causal_dwconv(u, w, b):
    C = u.shape[-1]
    y = lax.conv_general_dilated(u, w[:, None, :], window_strides=(1,),
                                 padding=[(CONV_WIDTH - 1, 0)],
                                 dimension_numbers=('NWC', 'WIO', 'NWC'),
                                 feature_group_count=C)
    return y + b

def hybrid_mixer(h, w_in, b_f, sinks, w_out):
    B, S, _ = h.shape
    z = h @ w_in
    o = 0
    qa = z[..., o:o + Q_A].reshape(B, S, N_HEADS_SWA, HEAD_DIM); o += Q_A
    ka = z[..., o:o + KV_A].reshape(B, S, N_KV_SWA, HEAD_DIM); o += KV_A
    va = z[..., o:o + KV_A].reshape(B, S, N_KV_SWA, HEAD_DIM); o += KV_A
    qb = z[..., o:o + Q_B].reshape(B, S, N_HEADS_FOX, HEAD_DIM); o += Q_B
    kb = z[..., o:o + Q_B].reshape(B, S, N_HEADS_FOX, HEAD_DIM); o += Q_B
    vb = z[..., o:o + Q_B].reshape(B, S, N_HEADS_FOX, HEAD_DIM); o += Q_B
    fb = z[..., o:o + F_B] + b_f
    ya = swa_attention(qa, ka, va, sinks).reshape(B, S, Q_A)
    yb = forgetting_attention(qb, kb, vb, fb).reshape(B, S, Q_B)
    return jnp.concatenate([ya, yb], axis=-1) @ w_out

def conv_glu_mlp(h, w_up, conv_w, conv_b, w_down):
    u = causal_dwconv(h @ w_up, conv_w, conv_b)
    a, g = jnp.split(u, 2, axis=-1)
    return (jax.nn.silu(g) * a) @ w_down

def second_inputs(seed: int = 0) -> dict:
    key = jax.random.key(seed)
    ks = jax.random.split(key, 16)
    f32 = jnp.float32
    nrm = lambda k, shp, s: jax.random.normal(k, shp, f32) * s
    return {
        "x": nrm(ks[0], (BATCH, SEQ, D_MODEL), 1.0),
        "c": nrm(ks[1], (BATCH, D_MODEL), 1.0),
        "w_ada": nrm(ks[2], (D_MODEL, 6 * D_MODEL), 0.5 * D_MODEL ** -0.5),
        "b_ada": nrm(ks[3], (6 * D_MODEL,), 0.02),
        "g_attn": 1.0 + nrm(ks[4], (D_MODEL,), 0.05),
        "w_in": nrm(ks[5], (D_MODEL, D_IN), D_MODEL ** -0.5),
        "b_f": 2.0 + nrm(ks[6], (N_HEADS_FOX,), 0.5),
        "sinks": nrm(ks[7], (N_HEADS_SWA,), 0.5),
        "w_out": nrm(ks[8], (D_MIX, D_MODEL), D_MIX ** -0.5),
        "g_mlp": 1.0 + nrm(ks[9], (D_MODEL,), 0.05),
        "w_up": nrm(ks[10], (D_MODEL, 2 * D_FF), D_MODEL ** -0.5),
        "conv_w": nrm(ks[11], (CONV_WIDTH, 2 * D_FF), CONV_WIDTH ** -0.5),
        "conv_b": nrm(ks[12], (2 * D_FF,), 0.02),
        "w_down": nrm(ks[13], (D_FF, D_MODEL), D_FF ** -0.5),
        "g_final": 1.0 + nrm(ks[14], (D_MODEL,), 0.05),
    }

def second_block(x, c, w_ada, b_ada, g_attn, w_in, b_f, sinks, w_out,
              g_mlp, w_up, conv_w, conv_b, w_down, g_final):
    mod = jax.nn.silu(c) @ w_ada + b_ada
    sh1, sc1, ga1, sh2, sc2, ga2 = jnp.split(mod, 6, axis=-1)
    for _ in range(DEPTH_2):
        h = modulate(rms_norm_2(x, g_attn), sh1, sc1)
        x = x + ga1[:, None, :] * hybrid_mixer(h, w_in, b_f, sinks, w_out)
        h2 = modulate(rms_norm_2(x, g_mlp), sh2, sc2)
        x = x + ga2[:, None, :] * conv_glu_mlp(h2, w_up, conv_w, conv_b, w_down)
    return rms_norm_2(x, g_final)


def setup_inputs(seed=0):
    out = dict(first_inputs(seed))
    for name, value in second_inputs(seed + 1).items():
        if name != "x":
            out[name + "_2"] = value
    return out


def reference(
    x, attn_norm, ffn_norm, diff_w_in, diff_q_norm, diff_k_norm, diff_lambda_q1, diff_lambda_k1,
    diff_lambda_q2, diff_lambda_k2, diff_subln, diff_w_out, mla_w_a, mla_q_a_norm,
    mla_kv_a_norm, mla_w_qb, mla_w_kvb, mla_q_norm, mla_k_norm, mla_w_out, moe_w_group,
    moe_b_group, moe_w_expert, moe_b_expert, moe_w_gate, moe_w_up, moe_w_down, c_2, w_ada_2,
    b_ada_2, g_attn_2, w_in_2, b_f_2, sinks_2, w_out_2, g_mlp_2, w_up_2, conv_w_2, conv_b_2,
    w_down_2, g_final_2,
):
    x = first_block(
        x, attn_norm, ffn_norm, diff_w_in, diff_q_norm, diff_k_norm, diff_lambda_q1,
        diff_lambda_k1, diff_lambda_q2, diff_lambda_k2, diff_subln, diff_w_out, mla_w_a,
        mla_q_a_norm, mla_kv_a_norm, mla_w_qb, mla_w_kvb, mla_q_norm, mla_k_norm, mla_w_out,
        moe_w_group, moe_b_group, moe_w_expert, moe_b_expert, moe_w_gate, moe_w_up, moe_w_down,
    )
    return second_block(
        x, c_2, w_ada_2, b_ada_2, g_attn_2, w_in_2, b_f_2, sinks_2, w_out_2, g_mlp_2, w_up_2,
        conv_w_2, conv_b_2, w_down_2, g_final_2,
    )


_drawn_inputs = setup_inputs


def setup_inputs(seed=0):
    import zlib

    import numpy as np

    out = dict(_drawn_inputs(seed))
    spreads = {}
    factors = {'diff_lambda_k2': 4.106,
     'mla_q_a_norm': 5.603,
     'mla_kv_a_norm': 2.992,
     'mla_q_norm': 7.694,
     'mla_k_norm': 5.313,
     'moe_b_group': 3.882,
     'moe_b_expert': 3.93,
     'b_ada_2': 3.371,
     'g_attn_2': 7.717,
     'b_f_2': 3.42,
     'sinks_2': 170.309,
     'g_mlp_2': 4.803,
     'conv_b_2': 8.0}
    for name, (base, spread) in spreads.items():
        noise = np.random.default_rng([zlib.crc32(name.encode()), seed]).standard_normal(out[name].shape)
        drawn = base * np.exp(spread * noise) if base else spread * noise
        out[name] = __import__('jax').numpy.asarray(drawn.astype(out[name].dtype))
    for name, factor in factors.items():
        out[name] = (out[name] * factor).astype(out[name].dtype)
    return out
```

```python
import math
from contextlib import ExitStack

import numpy as np

import concourse.bass as bass
from concourse import mybir

ALU = mybir.AluOpType
ACT = mybir.ActivationFunctionType
F32 = mybir.dt.float32
I32 = mybir.dt.int32
AX = mybir.AxisListType.X

P = 128
S = 256
TT = S // P
D = 1024
DC = D // P
EPS = 1e-6
NEG = -1e30
NB = 512

RING = 12
UNIT = 2048

E = 64
GROUPS = 8
FF = 256
CAP = 64
SLOTS = 2 * S
TRASH = SLOTS + CAP
WIDE = TRASH + CAP
PER = 4
PASSES = S // CAP

HEADS = 8
ROT = 64
MLA_Q, MLA_KV, MLA_QK, NOPE = 384, 256, 192, 128
DFF = 2816
LAMBDA_INIT = 0.8 - 0.6 * math.exp(0.0)
WINDOW = 128
HYB_IN = 2312
SPAN = 3 * P

GATE_AT, UP_AT, DOWN_AT = (0, 1, 4, 5), (2, 3, 6, 7), (8, 9, 10, 11)


def shape_constants():
    pos = np.arange(S, dtype=np.float32)
    inv = (1.0 / (np.float32(10000.0) ** (np.arange(0, ROT, 2, dtype=np.float32) / np.float32(ROT)))).astype(np.float32)
    ang = pos[:, None] * inv[None, :]
    cos = np.concatenate([np.cos(ang), np.cos(ang)], 1)
    sin = np.concatenate([-np.sin(ang), np.sin(ang)], 1)
    rope = np.stack([cos, sin], 0).astype(np.float32)
    rope = rope.reshape(2, TT, P, ROT).transpose(2, 0, 1, 3).reshape(P, -1)
    q = np.arange(P)[:, None]
    k = np.arange(P)[None, :]
    tri = np.where(k <= q, 0.0, NEG)
    causal = np.concatenate([tri, np.zeros((P, P)), tri], 1)
    window = np.concatenate([tri, np.where(q + P - k < WINDOW, 0.0, NEG), tri], 1)
    dist = np.concatenate([q - k, q + P - k, q - k], 1)
    before = (np.arange(P)[:, None] < np.arange(P)[None, :]).astype(np.float32)
    upto = (np.arange(P)[:, None] <= np.arange(P)[None, :]).astype(np.float32)
    iota = np.tile(np.arange(SLOTS), (P, 1))
    parts = [np.eye(P), before, np.ones((P, P)), rope, causal, upto, window, dist, iota]
    return np.concatenate([p.astype(np.float32) for p in parts], 1)


KEPT = dict(ident=P, before=P, ones=P, rope=2 * TT * ROT, causal=SPAN)
LATER = dict(upto=P, window=SPAN, dist=SPAN, iota=SLOTS)


def build(nc, t, out):
    with ExitStack() as ctx:
        def sb(name, shape, dt=F32):
            return ctx.enter_context(nc.sbuf_tensor(name, shape, dt))

        class Signal:

            def __init__(self, handle, base=0):
                self.sem, self.base = handle, base

            def __call__(self, n):
                return self.sem, n + self.base

        def sem(name):
            return Signal(ctx.enter_context(nc.semaphore(name)))

        counted_up = {}

        def shared(kind, total):
            if kind not in counted_up:
                counted_up[kind] = [ctx.enter_context(nc.semaphore(kind)), 0]
            signal = Signal(*counted_up[kind])
            counted_up[kind][1] += total
            return signal

        X = sb("X", [P, TT, D])
        hn = sb("hn", [P, TT, D])
        hT = sb("hT", [P, DC, S])
        ring = sb("ring", [P, RING, UNIT])
        A = sb("A", [P, 8192])
        BC = sb("BC", [P, 10240])
        konst = sb("konst", [P, sum(KEPT.values())])
        pT = sb("pT", [P, 2, SPAN])
        stat = sb("stat", [P, 512])
        at = {}
        offset = 0
        for name, width in KEPT.items():
            at[name] = konst[:, offset:offset + width]
            offset += width
        ident, ones, before = at["ident"], at["ones"], at["before"]
        later = {}
        for name, width in LATER.items():
            later[name] = t["constants"][:, offset:offset + width]
            offset += width
        rope_tab = at["rope"].rearrange("p (a t d) -> p a t d", a=2, t=TT)

        gains = sb("gains", [P, 2, 2, DC])
        gains2 = sb("gains2", [P, 2, DC])
        small = sb("small", [P, 64])
        subln, mla_gain = small[:, 0:1], small[:, 1:6]
        ccol, csig = small[:, 8:16], small[:, 16:24]
        sinks = small[:, 24:32]
        f_bias = small[:, 32:40]
        lam = small[:, 40:44]
        cond_c = small[:, 44:52]
        router_w = A[:, 4608:4608 + DC * 72].rearrange("p (c n) -> p c n", c=DC)
        iota = A[:, 2560:2560 + SLOTS]
        router_b = sb("router_b", [P, 2, 72])
        qk_gain = sb("qk_gain", [P, 2, 192])
        gtab = sb("gtab", [P, 2, 2, TT, ROT])
        modc = sb("modc", [P, 4, DC])
        eb = pT[:, :, :].rearrange("p a s -> p (a s)")[:, 0:2 * FF].rearrange("p (b n) -> p b n", b=2)
        modrow = sb("modrow", [1, NB])
        pos_i = A[:, 7168:7168 + (PASSES + 1) * E].bitcast(I32)
        half = sb("half", [P, 16])

        bank = [ctx.enter_context(nc.psum_tensor(f"bank{i}", [P, NB], F32)) for i in range(8)]
        mod_dram = nc.dram_tensor("mod_scratch", (6 * D,), F32, kind="Internal").ap()

        loaded = sem("loaded")
        unit_full = [sem(f"unit_full{i}") for i in range(RING)]
        unit_done = sem("unit_done")
        dve_step, act_step, pool_step = sem("dve_step"), sem("act_step"), sem("pool_step")

        class Steps:

            def __init__(self, signal):
                self.count_sem, self.n, self.eng = signal, 0, None

            def done(self, ins):
                self.n += 1
                ins.then_inc(self.count_sem.sem, 1)
                self.eng.wait_ge(*self.count_sem(self.n))

        dv, ac, po = Steps(dve_step), Steps(act_step), Steps(pool_step)

        units = []

        def plan(view, src):
            units.append((view, src))
            return len(units) - 1

        def slot(u):
            return ring[:, u % RING, :]

        def load_unit(sp, u):
            if u >= RING:
                sp.wait_ge(*unit_done(u - RING + 1))
            view, src = units[u]
            sp.dma_start(view(slot(u)), src).then_inc(unit_full[u % RING].sem, 16)

        def unit_here(pe, u):
            pe.wait_ge(*unit_full[u % RING](16 * (u // RING + 1)))

        class Stage:
            tensor = vector = scalar = gpsimd = sync = staticmethod(lambda eng: None)

        def norm_stage(name, before_stage, gain, shift=None, extra=()):
            st = Stage()
            squares, rooted, scaled = shared("norm_squares", TT), shared("norm_rooted", 1), shared("norm_scaled", TT)
            turned, out_v, out_a = shared("norm_turned", 4), shared("norm_out_v", 4), shared("norm_out_a", 4)
            ssq, rstd = stat[:, 0:TT], stat[:, 2:2 + TT]

            def scalar(act):
                before_stage(act)
                for tt in range(TT):
                    nc.scalar.activation(hT[:, :, :].rearrange("p c s -> p (c s)")[:, tt * D:(tt + 1) * D], X[:, tt, :],
                                         ACT.Square, accum_out=ssq[:, tt:tt + 1]).then_inc(squares.sem, 1)
                for s, v in extra:
                    act.wait_ge(*s(v))
                for f in (1, 3):
                    act.wait_ge(*turned(f + 1))
                    for k in range(2):
                        c = 2 * f + k
                        b = shift[:, c:c + 1] if shift is not None else 0.0
                        nc.scalar.activation(hT[:, c, :], bank[4 + f % 2][:, k * S:(k + 1) * S], ACT.Identity,
                                             scale=gain[:, c:c + 1], bias=b).then_inc(out_a.sem, 1)

            def gpsimd(pool):
                pool.wait_ge(*squares(TT))
                po.done(nc.gpsimd.tensor_scalar(rstd, ssq, 1.0 / D, EPS, ALU.mult, ALU.add))
                nc.gpsimd.tensor_tensor(rstd, rstd, half[:, 0:TT], ALU.pow).then_inc(rooted.sem, 1)

            def vector(dve):
                before_stage(dve)
                dve.wait_ge(*rooted(1))
                for tt in range(TT):
                    nc.vector.tensor_scalar(hn[:, tt, :], X[:, tt, :], rstd[:, tt:tt + 1], None,
                                            ALU.mult).then_inc(scaled.sem, 1)
                dve.wait_ge(*squares(TT))
                for s, v in extra:
                    dve.wait_ge(*s(v))
                for f in (0, 2):
                    dve.wait_ge(*turned(f + 1))
                    for k in range(2):
                        c = 2 * f + k
                        if shift is None:
                            i = nc.vector.tensor_scalar(hT[:, c, :], bank[4][:, k * S:(k + 1) * S],
                                                        gain[:, c:c + 1], None, ALU.mult)
                        else:
                            i = nc.vector.tensor_scalar(hT[:, c, :], bank[4][:, k * S:(k + 1) * S],
                                                        gain[:, c:c + 1], shift[:, c:c + 1], ALU.mult, ALU.add)
                        i.then_inc(out_v.sem, 1)

            def tensor(pe):
                pe.wait_ge(*scaled(TT))
                for f in range(4):
                    if f == 2:
                        pe.wait_ge(*out_v(2))
                    if f == 3:
                        pe.wait_ge(*out_a(2))
                    for k in range(2):
                        for tt in range(TT):
                            i = nc.tensor.transpose(bank[4 + f % 2][:, k * S + tt * P:k * S + (tt + 1) * P],
                                                    hn[:, tt, 2 * f + k:D:DC], ident)
                    i.then_inc(turned.sem, 1)

            def ready(eng):
                eng.wait_ge(*out_v(4))
                eng.wait_ge(*out_a(4))
            st.scalar, st.gpsimd, st.vector, st.tensor, st.ready = scalar, gpsimd, vector, tensor, ready
            return st

        def project_stage(name, ready, lhs, blocks, evac, fold=None, sbanks=(0, 1, 2, 3), first_free=None):
            st = Stage()
            copied = shared("product_copied", TT * len(blocks))

            def ps(n, tt):
                return bank[sbanks[2 * (n % 2) + tt]]

            def last_unit(n):
                return blocks[n][1][-1][0]

            def tensor(pe):
                ready(pe)
                if first_free:
                    first_free(pe)
                for n, (w, parts) in enumerate(blocks):
                    if n >= 2:
                        pe.wait_ge(*copied(2 * (n - 1)))
                    total = sum(p[2] for p in parts)
                    seen = 0
                    for u, view, cn, keep in parts:
                        unit_here(pe, u)
                        for tt in range(TT):
                            for c in range(cn):
                                i = nc.tensor.matmul(ps(n, tt)[:, 0:w], lhs(seen + c, tt), view(slot(u))[:, c, :],
                                                     start=(seen + c == 0), stop=(seen + c == total - 1))
                        seen += cn
                        i.then_inc((unit_done if not keep else kept[0]).sem, 1)

            kept = [sem(name + "_kept")] if any(p[3] for b in blocks for p in b[1]) else [None]
            kept_of = {}
            count = 0
            for n, (w, parts) in enumerate(blocks):
                if parts[-1][3]:
                    count += 1
                    kept_of[n] = count

            def block_ready(eng, n):
                if n in kept_of:
                    eng.wait_ge(*kept[0](kept_of[n]))
                else:
                    eng.wait_ge(*unit_done(last_unit(n) + 1))

            def drain(eng):
                for n, (w, parts) in enumerate(blocks):
                    block_ready(eng, n)
                    for tt in range(TT):
                        evac(eng, n, tt, ps(n, tt)[:, 0:w]).then_inc(copied.sem, 1)
                    if fold:
                        fold(eng, n)
            st.tensor, st.drain, st.copied = tensor, drain, copied
            return st

        def square_units(w, ncols, order="(p c)", kc=DC, per=4, col0=0):
            src = w.rearrange("(p c) n -> p c n", c=kc) if order == "(p c)" else w.rearrange("(c p) n -> p c n", p=P)
            blocks = []
            for n0 in range(0, ncols, NB):
                wd = min(NB, ncols - n0)
                parts = []
                for c0 in range(0, kc, per):
                    cn = min(per, kc - c0)

                    def view(a, wd=wd, cn=cn):
                        return a[:, 0:cn * wd].rearrange("p (c n) -> p c n", c=cn)
                    u = plan(view, src[:, c0:c0 + cn, col0 + n0:col0 + n0 + wd])
                    parts.append((u, view, cn, False))
                blocks.append((wd, parts))
            return blocks

        def loads(first, last):
            def sync(sp):
                for u in range(first, last):
                    load_unit(sp, u)
            return sync

        def turn_stage(name, ready, jobs, free=None):
            st = Stage()
            fills = [jobs[i:i + 2] for i in range(0, len(jobs), 2)]
            turned, out_v, out_a = (shared("turn_done", len(fills)), shared("turn_out_v", (len(fills) + 1) // 2),
                                    shared("turn_out_a", len(fills) // 2))

            def tensor(pe):
                ready(pe)
                for f, fill in enumerate(fills):
                    if f >= 2:
                        pe.wait_ge(*(out_v if f % 2 == 0 else out_a)(f // 2))
                    for k, (src, w, dst, scale) in enumerate(fill):
                        for tt in range(TT):
                            i = nc.tensor.transpose(bank[4 + f % 2][0:w, k * S + tt * P:k * S + (tt + 1) * P],
                                                    src(tt), ident)
                    i.then_inc(turned.sem, 1)

            def evac(eng, odd):
                for f, fill in enumerate(fills):
                    if f % 2 != odd:
                        continue
                    eng.wait_ge(*turned(f + 1))
                    for k, (src, w, dst, scale) in enumerate(fill):
                        ps = bank[4 + f % 2][0:w, k * S:(k + 1) * S]
                        if odd and scale is not None:
                            i = nc.scalar.activation(dst, ps, ACT.Identity, scale=scale)
                        elif odd:
                            i = nc.scalar.activation(dst, ps, ACT.Copy)
                        elif scale is not None:
                            i = nc.vector.tensor_scalar(dst, ps, scale, None, ALU.mult)
                        else:
                            i = nc.vector.tensor_copy(dst, ps)
                    i.then_inc((out_a if odd else out_v).sem, 1)

            def vector(dve):
                if free:
                    free(dve)
                evac(dve, 0)

            def scalar(act):
                if free:
                    free(act)
                evac(act, 1)

            def done(eng):
                eng.wait_ge(*out_v((len(fills) + 1) // 2))
                if len(fills) > 1:
                    eng.wait_ge(*out_a(len(fills) // 2))
            st.tensor, st.vector, st.scalar, st.ready = tensor, vector, scalar, done
            return st

        SC = BC[:, 8192:8192 + 4 * SPAN].rearrange("p (b m s) -> p b m s", b=2, m=2)

        def attention_stage(name, ready, heads, scale, dv_w, bias, filler=None, mix=None, sink=False):
            st = Stage()
            n = len(heads)
            maps = len(heads[0][0])
            scored, masked, maxed = (shared("head_scored", maps * n), shared("head_masked", maps * n),
                                     shared("head_maxed", n))
            exped, mixed, turned = (shared("head_exped", n), shared("head_mixed", n if mix else 0),
                                    shared("head_turned", n))
            copied, summed, stored = shared("head_copied", n), shared("head_summed", n), shared("head_stored", n)
            sink_heads = heads if sink is True else []
            nmax = stat[:, 16:24].rearrange("p (b m t) -> p b m t", b=2, m=2)
            den = stat[:, 24:32].rearrange("p (b m t) -> p b m t", b=2, m=2)
            rden = stat[:, 32:40].rearrange("p (b m t) -> p b m t", b=2, m=2)
            dsink = stat[:, 40:44].rearrange("p (b t) -> p b t", b=2)
            obanks = 1 if mix else 2

            def obank(h):
                b = bank[6] if mix else bank[1 + 2 * (h % 2)]
                return b[:, 0:S].rearrange("p (t d) -> p t d", t=TT)
            ranges = [(0, P), (P, SPAN)]

            def tensor(pe):
                ready(pe)

                def score(h):
                    if h >= 2:
                        pe.wait_ge(*masked(maps * (h - 1)))
                    for m in range(maps):
                        ps = bank[(h % 2) * 2 + m]
                        pairs = heads[h][0][m]
                        for tt, (a, b) in enumerate(ranges):
                            for j, (q, k) in enumerate(pairs):
                                i = nc.tensor.matmul(ps[:, a:b], q(tt), k(0, b - a), start=(j == 0),
                                                     stop=(j == len(pairs) - 1))
                        i.then_inc(scored.sem, 1)

                def turn(h):
                    pe.wait_ge(*(mixed if mix else exped)(h + 1))
                    if h >= 2:
                        pe.wait_ge(*copied(h - 1))
                    for j in range(3):
                        i = nc.tensor.transpose(bank[4 + h % 2][:, j * P:(j + 1) * P],
                                                SC[:, h % 2, 0, j * P:(j + 1) * P], ident)
                    i.then_inc(turned.sem, 1)

                def sum_v(h):
                    pe.wait_ge(*copied(h + 1))
                    if h >= obanks:
                        pe.wait_ge(*stored(h - obanks + 1))
                    ps = obank(h)
                    v = heads[h][1]
                    p = pT[:, h % 2, :]
                    nc.tensor.matmul(ps[:, 0, 0:dv_w], p[:, 0:P], v(0), start=True, stop=True)
                    nc.tensor.matmul(ps[:, 1, 0:dv_w], p[:, P:2 * P], v(0), start=True, stop=False)
                    nc.tensor.matmul(ps[:, 1, 0:dv_w], p[:, 2 * P:SPAN], v(1), start=False,
                                     stop=True).then_inc(summed.sem, 1)
                score(0)
                for h in range(n + 1):
                    if h + 1 < n:
                        score(h + 1)
                    if filler and h < n:
                        filler.tensor(pe, h)
                    if h < n:
                        turn(h)
                    if h >= 1:
                        sum_v(h - 1)

            def vector(dve):
                def mask(h):
                    if h >= 2:
                        dve.wait_ge(*turned(h - 1))
                    for m in range(maps):
                        ps = bank[(h % 2) * 2 + m][:, 0:SPAN]
                        b = bias(h)
                        dve.wait_ge(*scored(maps * h + m + 1))
                        nc.vector.scalar_tensor_tensor(out=SC[:, h % 2, m, :], in0=ps, scalar=scale, in1=b,
                                                       op0=ALU.mult, op1=ALU.add).then_inc(masked.sem, 1)
                    dve.wait_ge(*masked(maps * (h + 1)))
                    for m in range(maps):
                        for tt, (a, b) in enumerate(ranges):
                            i = nc.vector.tensor_reduce(nmax[:, h % 2, m, tt:tt + 1], SC[:, h % 2, m, a:b], AX,
                                                        ALU.max, negate=True)
                    if sink and h < HEADS:
                        dv.done(i)
                        i = nc.vector.tensor_scalar(nmax[:, h % 2, 0, :], nmax[:, h % 2, 0, :], nsink[:, h:h + 1],
                                                    None, ALU.min)
                    i.then_inc(maxed.sem, 1)

                def weigh(h):
                    dve.wait_ge(*exped(h + 1))
                    if sink and h < HEADS:
                        dv.done(nc.vector.tensor_tensor(den[:, h % 2, 0, :], den[:, h % 2, 0, :], dsink[:, h % 2, :],
                                                        ALU.add))
                    if h >= 2:
                        dve.wait_ge(*stored(h - 1))
                    dv.done(nc.vector.reciprocal(rden[:, h % 2, 0:maps, :], den[:, h % 2, 0:maps, :]))
                    if mix:
                        dv.done(nc.vector.tensor_scalar(rden[:, h % 2, 1, :], rden[:, h % 2, 1, :], lam[:, 3:4], None,
                                                        ALU.mult))
                        for tt, (a, b) in enumerate(ranges):
                            dv.done(nc.vector.tensor_scalar(SC[:, h % 2, 0, a:b], SC[:, h % 2, 0, a:b],
                                                            rden[:, h % 2, 0, tt:tt + 1], None, ALU.mult))
                            i = nc.vector.scalar_tensor_tensor(out=SC[:, h % 2, 0, a:b], in0=SC[:, h % 2, 1, a:b],
                                                               scalar=rden[:, h % 2, 1, tt:tt + 1],
                                                               in1=SC[:, h % 2, 0, a:b], op0=ALU.mult, op1=ALU.add)
                            if tt == 0:
                                dv.done(i)
                        i.then_inc(mixed.sem, 1)

                def store(h):
                    dve.wait_ge(*summed(h + 1))
                    ps = obank(h)
                    for tt in range(TT):
                        if mix:
                            i = nc.vector.tensor_copy(heads[h][2](tt), ps[:, tt, 0:dv_w])
                        else:
                            i = nc.vector.tensor_scalar(heads[h][2](tt), ps[:, tt, 0:dv_w],
                                                        rden[:, h % 2, 0, tt:tt + 1], None, ALU.mult)
                    i.then_inc(stored.sem, 1)
                mask(0)
                for h in range(n + 1):
                    if h + 1 < n:
                        mask(h + 1)
                    if h < n:
                        weigh(h)
                    if h >= 1:
                        store(h - 1)

            def scalar(act):
                def exps(h):
                    act.wait_ge(*maxed(h + 1))
                    for m in range(maps):
                        for tt, (a, b) in enumerate(ranges):
                            i = nc.scalar.activation(SC[:, h % 2, m, a:b], SC[:, h % 2, m, a:b], ACT.Exp,
                                                     bias=nmax[:, h % 2, m, tt:tt + 1],
                                                     accum_out=den[:, h % 2, m, tt:tt + 1])
                    if sink and h < HEADS:
                        for tt in range(TT):
                            i = nc.scalar.activation(dsink[:, h % 2, tt:tt + 1], sinks[:, h:h + 1], ACT.Exp,
                                                     bias=nmax[:, h % 2, 0, tt:tt + 1])
                    i.then_inc(exped.sem, 1)

                def copy(h):
                    act.wait_ge(*turned(h + 1))
                    if h >= 2:
                        act.wait_ge(*summed(h - 1))
                    nc.scalar.activation(pT[:, h % 2, :], bank[4 + h % 2][:, 0:SPAN], ACT.Copy).then_inc(copied.sem, 1)
                exps(0)
                for h in range(n):
                    if h + 1 < n:
                        exps(h + 1)
                    if filler:
                        filler.scalar(act, h)
                    copy(h)

            def done(eng):
                eng.wait_ge(*stored(n))
            st.tensor, st.vector, st.scalar, st.ready = tensor, vector, scalar, done
            return st

        order = []

        n_loaded = [0]

        def start_gpsimd(pool):
            def ld(dst, src):
                pool.dma_start(dst, src).then_inc(loaded.sem, 16)
                n_loaded[0] += 16
            ld(gains[:, 0, :, :], t["attn_norm"].rearrange("l (p c) -> p l c", c=DC))
            ld(gains[:, 1, :, :], t["ffn_norm"].rearrange("l (p c) -> p l c", c=DC))
            ld(BC[:, 384:384 + ROT], t["diff_q_norm"][0].partition_broadcast(P))
            ld(BC[:, 448:448 + ROT], t["diff_k_norm"][0].partition_broadcast(P))
            ld(qk_gain[:, 0, :], t["mla_q_norm"][0].partition_broadcast(P))
            ld(qk_gain[:, 1, :], t["mla_k_norm"][0].partition_broadcast(P))
            for k, name in enumerate(("q1", "k1", "q2", "k2")):
                ld(BC[:, k * ROT:(k + 1) * ROT], t["diff_lambda_" + name][0].partition_broadcast(P))
            ld(subln, t["diff_subln"].rearrange("a p -> p a"))
            ld(mla_gain[:, 0:3], t["mla_q_a_norm"].rearrange("a (p c) -> p (a c)", c=3))
            ld(mla_gain[:, 3:5], t["mla_kv_a_norm"].rearrange("a (p c) -> p (a c)", c=2))
            for layer in range(2):
                ld(router_b[:, layer, 0:GROUPS], t["moe_b_group"][layer].partition_broadcast(P))
                ld(router_b[:, layer, GROUPS:], t["moe_b_expert"][layer].partition_broadcast(P))
            ld(gains2[:, 0, :], t["g_attn_2"].rearrange("(p c) -> p c", c=DC))
            ld(gains2[:, 1, :], t["g_mlp_2"].rearrange("(p c) -> p c", c=DC))
            ld(ccol, t["c_2"].rearrange("a (p c) -> p (a c)", c=DC))
            ld(sinks, t["sinks_2"].partition_broadcast(P))
            ld(f_bias, t["b_f_2"].partition_broadcast(P))
            assert n_loaded[0] == N_SMALL
            po.done(nc.gpsimd.memset(half[:, :], -0.5))

        N_SMALL = 16 * 22
        first = sem("first")

        def start_scalar(act):
            act.dma_start(X[:, :, :], t["x"][0].rearrange("(t p) d -> p t d", p=P)).then_inc(first.sem, 16)
            act.dma_start(konst[:, :], t["constants"][:, 0:sum(KEPT.values())]).then_inc(first.sem, 16)

        def have_first(eng):
            eng.wait_ge(*first(32))

        u0 = len(units)
        w_in = t["diff_w_in"][0]
        in_blocks = square_units(w_in, 3072)
        u1 = len(units)
        set_up = sem("set_up")
        lam_exp = sem("lam_exp")
        lam_dot = sem("lam_dot")

        def have_small(eng):
            eng.wait_ge(*loaded(N_SMALL))

        norm1_free = have_first
        n1 = norm_stage("n1", norm1_free, gains[:, 0, 0, :], extra=[(loaded, N_SMALL)])
        qkv = A[:, 0:TT * 3072].rearrange("p (t n) -> p t n", t=TT)

        def setup_vector(dve):
            have_small(dve)
            l = BC[:, 0:4 * ROT].rearrange("p (k d) -> p k d", k=4)
            pr = BC[:, 4 * ROT:6 * ROT].rearrange("p (k d) -> p k d", k=2)
            for k in range(2):
                dv.done(nc.vector.tensor_tensor(pr[:, k, :], l[:, 2 * k, :], l[:, 2 * k + 1, :], ALU.mult))
            nc.vector.tensor_reduce(lam[:, 0:2], pr, AX, ALU.add).then_inc(lam_dot.sem, 1)
            fold_rope(0)
            dve.wait_ge(*lam_exp(2))
            dv.done(nc.vector.tensor_tensor(lam[:, 2:3], lam[:, 1:2], lam[:, 0:1], ALU.subtract))
            dv.done(nc.vector.tensor_scalar(lam[:, 3:4], lam[:, 2:3], -LAMBDA_INIT, None, ALU.add))
            dv.done(nc.vector.tensor_scalar(csig, csig, 1.0, None, ALU.add))
            dv.done(nc.vector.reciprocal(csig, csig))
            dv.done(nc.vector.tensor_scalar(subln, subln, 1.0 - LAMBDA_INIT, None, ALU.mult))
            dv.done(nc.vector.tensor_scalar(nsink, sinks, -1.0, None, ALU.mult))
            nc.vector.tensor_tensor(cond_c, ccol, csig, ALU.mult).then_inc(set_up.sem, 1)

        nsink = stat[:, 48:56]

        def fold_rope(which):
            for qk in range(2):
                g = BC[:, 384 + 64 * qk:448 + 64 * qk] if which == 0 else qk_gain[:, qk, NOPE:MLA_QK]
                for tt in range(TT):
                    dv.done(nc.vector.tensor_tensor(gtab[:, qk, 0, tt, :], rope_tab[:, 0, tt, :], g, ALU.mult))
                    dv.done(nc.vector.tensor_tensor(gtab[:, qk, 1, tt, 0:32], rope_tab[:, 1, tt, 0:32], g[:, 32:64],
                                                    ALU.mult))
                    dv.done(nc.vector.tensor_tensor(gtab[:, qk, 1, tt, 32:64], rope_tab[:, 1, tt, 32:64], g[:, 0:32],
                                                    ALU.mult))

        def setup_scalar(act):
            have_small(act)
            act.wait_ge(*lam_dot(1))
            nc.scalar.activation(lam[:, 0:2], lam[:, 0:2], ACT.Exp).then_inc(lam_exp.sem, 1)
            nc.scalar.activation(csig, ccol, ACT.Exp, scale=-1.0).then_inc(lam_exp.sem, 1)

        def copy_qkv(eng, n, tt, ps):
            return nc.scalar.activation(qkv[:, tt, n * NB:(n + 1) * NB], ps, ACT.Copy)

        p1_sq, p1_ss, p1_rs = sem("p1_sq"), sem("p1_ss"), sem("p1_rs")
        p1_used = sem("p1_used")
        sq1 = hn[:, 0, :].rearrange("p (b n) -> p b n", b=2)
        rot1 = hn[:, 1, :].rearrange("p (b n) -> p b n", b=2)

        def square_qk(act, n):
            if n >= 4:
                return
            for tt in range(TT):
                j = 2 * n + tt
                act.wait_ge(*p1.copied(j + 1))
                if j >= 2:
                    act.wait_ge(*p1_ss(j - 1))
                nc.scalar.activation(sq1[:, j % 2, :], qkv[:, tt, n * NB:(n + 1) * NB], ACT.Square).then_inc(p1_sq.sem, 1)

        p1 = project_stage("p1", n1.ready, lambda c, tt: hT[:, c, tt * P:(tt + 1) * P], in_blocks, copy_qkv,
                           square_qk)

        def rotate(dve, x, g, w, n_groups, qk, tt, t1, t2):
            cs = gtab[:, qk, 0, tt, :].unsqueeze(1).broadcast_to([P, n_groups, ROT])
            sn0 = gtab[:, qk, 1, tt, 0:32].unsqueeze(1).broadcast_to([P, n_groups, 32])
            sn1 = gtab[:, qk, 1, tt, 32:64].unsqueeze(1).broadcast_to([P, n_groups, 32])
            nc.vector.tensor_tensor(t1, x, cs, ALU.mult)
            nc.vector.tensor_tensor(t2[:, :, 0:32], x[:, :, 32:64], sn0, ALU.mult)
            dv.done(nc.vector.tensor_tensor(t2[:, :, 32:64], x[:, :, 0:32], sn1, ALU.mult))
            dv.done(nc.vector.tensor_tensor(t1, t1, t2, ALU.add))

        p1_qk = sem("p1_qk")

        def rope_vector(dve):
            for n in range(4):
                for tt in range(TT):
                    j = 2 * n + tt
                    x = qkv[:, tt, n * NB:(n + 1) * NB].rearrange("p (g d) -> p g d", d=ROT)
                    dve.wait_ge(*p1_sq(j + 1))
                    nc.vector.tensor_reduce(stat[:, 64 + 8 * (j % 2):72 + 8 * (j % 2)],
                                            sq1[:, j % 2, :].rearrange("p (g d) -> p g d", d=ROT), AX,
                                            ALU.add).then_inc(p1_ss.sem, 1)
                    t1 = rot1[:, 0, :].rearrange("p (g d) -> p g d", d=ROT)
                    t2 = rot1[:, 1, :].rearrange("p (g d) -> p g d", d=ROT)
                    rotate(dve, x, None, ROT, 8, n // 2, tt, t1, t2)
                    dve.wait_ge(*p1_rs(j + 1))
                    r = stat[:, 80 + 8 * (j % 2):88 + 8 * (j % 2)].unsqueeze(2).broadcast_to([P, 8, ROT])
                    dv.done(nc.vector.tensor_tensor(x, t1, r, ALU.mult))
            nc.vector.tensor_copy(stat[:, 8:9], stat[:, 64:65]).then_inc(p1_qk.sem, 1)

        def rope_gpsimd(pool):
            for j in range(8):
                pool.wait_ge(*p1_ss(j + 1))
                a, b = 64 + 8 * (j % 2), 80 + 8 * (j % 2)
                po.done(nc.gpsimd.tensor_scalar(stat[:, 96:104], stat[:, a:a + 8], 1.0 / ROT, EPS, ALU.mult, ALU.add))
                nc.gpsimd.tensor_tensor(stat[:, b:b + 8], stat[:, 96:104], half[:, 0:8], ALU.pow).then_inc(p1_rs.sem, 1)

        qkT = BC[:, 0:8192].rearrange("p (j s) -> p j s", s=S)
        jobs = []
        for h in range(HEADS):
            for qk in range(2):
                jobs.append((lambda tt, c0=qk * D + h * P: qkv[:, tt, c0:c0 + P], P, qkT[:, 2 * h + qk, :], None))

        def t1_ready(pe):
            pe.wait_ge(*p1_qk(1))
        t1 = turn_stage("t1", t1_ready, jobs)

        class Conditioning:

            def __init__(self, name, n0, n1, heads):
                w = t["w_ada_2"].rearrange("(p c) n -> p c n", c=DC)
                self.n0 = n0
                self.jobs = [[] for _ in range(heads)]
                self.copied = shared("mod_copied", n1 - n0)
                self.stored = shared("mod_stored", 16 * (n1 - n0))
                self.total = n1 - n0
                k = 0

                def view(a):
                    return a.rearrange("p (c n) -> p c n", c=4)
                for n in range(n0, n1):
                    for c0 in (0, 4):
                        h = k * heads // (2 * (n1 - n0))
                        self.jobs[h].append((n, c0, plan(view, w[:, c0:c0 + 4, n * NB:(n + 1) * NB]), view))
                        k += 1

            def tensor(self, pe, h):
                for n, c0, u, view in self.jobs[h]:
                    j = n - self.n0
                    if c0 == 0 and n >= 1:
                        pe.wait_ge(*self.copied(j))
                    unit_here(pe, u)
                    for c in range(4):
                        i = nc.tensor.matmul(bank[7][0:1, :], cond_c[:, c0 + c:c0 + c + 1], view(slot(u))[:, c, :],
                                             start=(c0 + c == 0), stop=(c0 + c == DC - 1))
                    i.then_inc(unit_done.sem, 1)

            def scalar(self, act, h):
                for n, c0, u, view in self.jobs[h]:
                    if c0 == 0:
                        continue
                    j = n - self.n0
                    act.wait_ge(*unit_done(u + 1))
                    if n >= 1:
                        act.wait_ge(*self.stored(16 * j))
                    nc.scalar.activation(modrow[0:1, :], bank[7][0:1, :], ACT.Copy).then_inc(self.copied.sem, 1)
                    act.wait_ge(*self.copied(j + 1))
                    act.dma_start(mod_dram[n * NB:(n + 1) * NB].rearrange("(a n) -> a n", a=1),
                                  modrow[0:1, :]).then_inc(self.stored.sem, 16)

            def ready(self, eng):
                eng.wait_ge(*self.stored(16 * self.total))

        cond1 = Conditioning("cond1", 0, 6, HEADS)
        u2 = len(units)

        def diff_head(h):
            def part(m):
                a, b = m * ROT, (m + 1) * ROT
                return [(lambda tt: qkT[a:b, 2 * h, tt * P:(tt + 1) * P], lambda k0, k1: qkT[a:b, 2 * h + 1, k0:k1])]
            return ([part(0), part(1)], lambda kt: qkv[:, kt, 2 * D + h * P:2 * D + (h + 1) * P],
                    lambda tt: hn[:, tt, h * P:(h + 1) * P])

        def a1_ready(pe):
            t1.ready(pe)
            pe.wait_ge(*set_up(1))
            pe.wait_ge(*p1.copied(12))
        a1 = attention_stage("a1", a1_ready, [diff_head(h) for h in range(HEADS)], ROT ** -0.5, P,
                             lambda h: at["causal"], filler=cond1, mix=True)

        n_sq, n_ss, n_rs, n_out = sem("sub_sq"), sem("sub_ss"), sem("sub_rs"), sem("sub_out")
        sub_sq = BC[:, 0:TT * D].rearrange("p (t h d) -> p t h d", t=TT, h=HEADS)

        def sub_scalar(act):
            a1.ready(act)
            nc.scalar.activation(sub_sq.rearrange("p t h d -> p (t h d)"), hn[:, :, :].rearrange("p t d -> p (t d)"),
                                 ACT.Square).then_inc(n_sq.sem, 1)

        def sub_vector(dve):
            dve.wait_ge(*n_sq(1))
            nc.vector.tensor_reduce(stat[:, 64:80], BC[:, 0:TT * D].rearrange("p (g d) -> p g d", d=P), AX,
                                    ALU.add).then_inc(n_ss.sem, 1)
            dve.wait_ge(*n_rs(1))
            o = hn[:, :, :].rearrange("p t (h d) -> p (t h) d", d=P)
            nc.vector.tensor_tensor(o, o, stat[:, 80:96].unsqueeze(2).broadcast_to([P, 16, P]),
                                    ALU.mult).then_inc(n_out.sem, 1)

        def sub_gpsimd(pool):
            pool.wait_ge(*n_ss(1))
            po.done(nc.gpsimd.tensor_scalar(stat[:, 64:80], stat[:, 64:80], 1.0 / P, EPS, ALU.mult, ALU.add))
            nc.gpsimd.tensor_tensor(stat[:, 80:96], stat[:, 64:80], half[:, 0:16], ALU.pow).then_inc(n_rs.sem, 1)

        def heads_turned(name, ready, scale=None):
            return turn_stage(name, ready, [(lambda tt, c=c: hn[:, tt, c * P:(c + 1) * P], P, hT[:, c, :], scale)
                                            for c in range(DC)])

        def sub_ready(pe):
            pe.wait_ge(*n_out(1))
        t2 = heads_turned("t2", sub_ready, subln)

        def add_x(eng, n, tt, ps):
            xs = X[:, tt, n * NB:(n + 1) * NB]
            return nc.vector.tensor_tensor(xs, xs, ps, ALU.add)

        def hT_lhs(c, tt):
            return hT[:, c, tt * P:(tt + 1) * P]
        out1 = square_units(t["diff_w_out"][0], D, order="(c p)")
        o1 = project_stage("o1", t2.ready, hT_lhs, out1, add_x)

        def o1_done(eng):
            eng.wait_ge(*o1.copied(4))

        def moe(layer, name, x_ready, x_free):
            st = Stage()
            pairs = E // 2
            nrm = norm_stage(name + "_n", x_ready, gains[:, 1, layer, :])
            table_in, logits, gexp, gexp_in = (shared("table_in", 48), shared("logits", 1), shared("gexp", 2 * TT),
                                               shared("gexp_in", TT))
            picked, counted, placed, gathered = (shared("picked", 1), shared("counted", 1), shared("placed", 1),
                                                 shared("gathered", DC))
            spread, spread_a = shared("spread_v", DC // 2), shared("spread_a", DC // 2)
            cwt_ready, cw_turned, cw_ready = shared("cwt_ready", 1), shared("cw_turned", 1), shared("cw_ready", 1)
            exped, hid_ready, h_turned = (shared("gate_exped", pairs), shared("hid_ready", pairs),
                                          shared("hid_turned", pairs))
            x_ready_, hT_ready = shared("tokens_ready", pairs + 2), shared("hidT_ready", pairs)
            rows_v, rows_a, rows_turned = shared("rows_v", pairs), shared("rows_a", pairs), shared("rows_turned", pairs)
            first_stored, pair_stored = shared("first_stored", pairs), shared("pair_stored", pairs + 1)
            y_turned, y_out_v, y_out_a = shared("y_turned", 8), shared("y_out_v", 4), shared("y_out_a", 4)
            summed, added, vstep = shared("moe_summed", 4), shared("moe_added", 4), shared("hidden_step", 3 * pairs)
            f_full, f_up, f_exp, f_hid = sem(name + "_f_full"), sem(name + "_f_up"), sem(name + "_f_exp"), sem(name + "_f_hid")
            f_down, f_stored, f_v = sem(name + "_f_down"), sem(name + "_f_stored"), sem(name + "_f_v")
            f_x, f_turned, f_hT = sem(name + "_f_x"), sem(name + "_f_turned"), sem(name + "_f_hT")
            f_rows, f_rturned = sem(name + "_f_rows"), sem(name + "_f_rturned")

            gate_w, up_w, down_w = (t["moe_w_gate"][layer], t["moe_w_up"][layer], t["moe_w_down"][layer])
            base = len(units)
            for _ in range(3 * E):
                units.append(None)
            xsT = BC[:, 0:DC * WIDE].rearrange("p (c s) -> p c s", c=DC)
            ysT = BC[:, DC * WIDE:2 * DC * WIDE].rearrange("p (c s) -> p c s", c=DC)
            place = A[:, 0:TT * SLOTS].rearrange("p (t s) -> p t s", t=TT)
            cwt = A[:, 1024:1024 + TT * SLOTS].rearrange("p (t s) -> p t s", t=TT)
            tmp = A[:, 2048:2560]
            cw = A[:, 6144:6144 + 4 * S].rearrange("p (b s) -> p b s", b=4)
            ys = A[:, 0:4 * D].rearrange("p (b n) -> p b n", b=4)
            lg = A[:, 3072:3072 + TT * 72].rearrange("p (t n) -> p t n", t=TT)
            oh = A[:, 3328:3328 + 2 * TT * E].rearrange("p (k t e) -> p k t e", k=2, t=TT)
            both = A[:, 3584:3584 + TT * E].rearrange("p (t e) -> p t e", t=TT)
            prod = A[:, 3712:3776]
            cnt = A[:, 3776:3840]
            off = A[:, 3840:3904]
            cum = A[:, 3904:3968]
            posf = A[:, 4096:4096 + (PASSES + 1) * E].rearrange("p (j e) -> p j e", j=PASSES + 1)
            r = stat[:, 128:256]
            hid = A[:, 7488:7488 + 2 * FF].rearrange("p (b n) -> p b n", b=2)
            hidT = gtab[:, :, :, :, :].rearrange("p a b t d -> p (a b t d)")[:, 0:2 * 2 * P].rearrange(
                "p (b c n) -> p b c n", b=2, c=2)
            xg = hT[:, :, :].rearrange("p c s -> p (c s)").rearrange("p (b c n) -> p b c n", b=2, c=DC)
            yrow = hn[:, :, :]
            turn_banks = ((6, 7), (4, 5))

            def first_of(dve, dst, values, top, work):
                dv.done(nc.vector.tensor_scalar(work[:, 0:8], values, top, None, ALU.is_equal))
                dv.done(nc.vector.tensor_tensor_scan(work[:, 8:16], work[:, 0:8], zero8, 0.0, ALU.add, ALU.add))
                dv.done(nc.vector.scalar_tensor_tensor(out=dst, in0=work[:, 8:16], scalar=1.0, in1=work[:, 0:8],
                                                       op0=ALU.is_equal, op1=ALU.mult))

            def tensor(pe):
                nrm.tensor(pe)
                nrm.ready(pe)
                pe.wait_ge(*table_in(48))
                for tt in range(TT):
                    for c in range(DC):
                        i = nc.tensor.matmul(bank[0][:, tt * 72:(tt + 1) * 72], hT_lhs(c, tt),
                                             router_w[:, c, :], start=(c == 0), stop=(c == DC - 1))
                i.then_inc(logits.sem, 1)
                pe.wait_ge(*picked(1))
                nc.tensor.matmul(bank[1][:, 0:E], before, both[:, 0, :], start=True, stop=True)
                nc.tensor.matmul(bank[1][:, E:2 * E], ones, both[:, 0, :], start=True, stop=False)
                nc.tensor.matmul(bank[1][:, E:2 * E], before, both[:, 1, :], start=False, stop=True)
                nc.tensor.matmul(bank[1][:, 2 * E:3 * E], ones, both[:, 0, :], start=True, stop=False)
                nc.tensor.matmul(bank[1][:, 2 * E:3 * E], ones, both[:, 1, :], start=False,
                                 stop=True).then_inc(counted.sem, 1)
                pe.wait_ge(*placed(1))
                for c in range(DC):
                    if c >= 4:
                        pe.wait_ge(*(spread if c % 2 == 0 else spread_a)((c - 4) // 2 + 1))
                    for tt in range(TT):
                        i = nc.tensor.matmul(bank[c % 4][:, :], hn[:, tt, c:D:DC], place[:, tt, :], start=(tt == 0),
                                             stop=(tt == TT - 1))
                    i.then_inc(gathered.sem, 1)
                pe.wait_ge(*cwt_ready(1))
                for b in range(4):
                    for tt in range(TT):
                        i = nc.tensor.transpose(bank[4 + b // 2][:, (b % 2) * S + tt * P:(b % 2) * S + (tt + 1) * P],
                                                cwt[:, tt, b * P:(b + 1) * P], ident)
                i.then_inc(cw_turned.sem, 1)
                pe.wait_ge(*cw_ready(1))
                pe.wait_ge(*spread(4))
                pe.wait_ge(*spread_a(4))

                def gate_up(k, experts):
                    ps = bank[4 + k]
                    for part in range(2):
                        ws = [slots[part].rearrange("p (c f) -> p c f", c=DC) for slots in experts]
                        for c in range(DC):
                            for q, w in enumerate(ws):
                                i = nc.tensor.matmul(ps[q * CAP:(q + 1) * CAP, part * FF:(part + 1) * FF],
                                                     xg[:, k, c, q * CAP:(q + 1) * CAP], w[:, c, :],
                                                     start=(c == 0), stop=(c == DC - 1))
                        yield i

                def turn_hidden(k, rows):
                    for c in range(2):
                        i = nc.tensor.transpose(bank[6][:, c * P:c * P + rows], hid[0:rows, k, c:FF:2],
                                                ident[0:rows, 0:rows])
                    return i

                def down(k, experts):
                    ws = [w.rearrange("p (c n) -> p c n", c=2) for w in experts]
                    for nb in range(2):
                        for c in range(2):
                            for q, w in enumerate(ws):
                                i = nc.tensor.matmul(bank[2 * k + nb][q * CAP:(q + 1) * CAP, :],
                                                     hidT[:, k, c, q * CAP:(q + 1) * CAP],
                                                     w[:, c, nb * NB:(nb + 1) * NB], start=(c == 0), stop=(c == 1))
                    return i

                def turn_rows(k, rows):
                    for m in range(DC):
                        i = nc.tensor.transpose(bank[turn_banks[k][m // 4]][:, (m % 4) * P:(m % 4) * P + rows],
                                                yrow[0:rows, k, m * P:(m + 1) * P], ident[0:rows, 0:rows])
                    return i

                with pe.Fori(0, E // PER) as turn:
                    def here(k):
                        u = base + k
                        pe.wait_ge(*unit_full[u % RING](turn * 16 + 16 * (u // RING + 1)))

                    for k in range(2):
                        pe.wait_ge(*x_ready_(turn * 2 + k + 1))
                        if k == 0:
                            pe.wait_ge(*pair_stored(turn * 2 + 1))
                        g = gate_up(k, [(slot(base + GATE_AT[2 * k + q]), slot(base + UP_AT[2 * k + q]))
                                        for q in range(2)])
                        here(GATE_AT[2 * k])
                        here(GATE_AT[2 * k + 1])
                        next(g).then_inc(unit_done.sem, 2)
                        here(UP_AT[2 * k])
                        here(UP_AT[2 * k + 1])
                        next(g).then_inc(unit_done.sem, 2)
                    for k in range(2):
                        pe.wait_ge(*hid_ready(turn * 2 + k + 1))
                        turn_hidden(k, P).then_inc(h_turned.sem, 1)
                        pe.wait_ge(*hT_ready(turn * 2 + k + 1))
                        here(DOWN_AT[2 * k])
                        here(DOWN_AT[2 * k + 1])
                        down(k, [slot(base + DOWN_AT[2 * k + q]) for q in range(2)]).then_inc(unit_done.sem, 2)
                    for k in range(2):
                        pe.wait_ge(*rows_v(turn * 2 + k + 1))
                        pe.wait_ge(*rows_a(turn * 2 + k + 1))
                        turn_rows(k, P).then_inc(rows_turned.sem, 1)

                over = pe.value_load(pos_i[0:1, PASSES * E:PASSES * E + 1], min_val=0, max_val=S)
                pe.wait_ge(*pair_stored(E // 2 + 1))
                with pe.If(over > CAP):
                    with pe.Fori(0, (PASSES - 1) * E) as n:
                        pe.wait_ge(*f_x(n + 1))
                        pe.wait_ge(*f_full(n * 48 + 48))
                        g = gate_up(0, [(A[:, 0:2048], A[:, 2048:4096])])
                        next(g)
                        next(g).then_inc(f_up.sem, 1)
                        pe.wait_ge(*f_hid(n + 1))
                        turn_hidden(0, P).then_inc(f_turned.sem, 1)
                        pe.wait_ge(*f_hT(n + 1))
                        down(0, [A[:, 4096:6144]]).then_inc(f_down.sem, 1)
                        pe.wait_ge(*f_rows(n + 1))
                        turn_rows(0, P).then_inc(f_rturned.sem, 1)
                    pe.wait_ge(*f_stored((PASSES - 1) * E + 1))
                for b in range(4):
                    for hf in range(2):
                        j = 2 * b + hf
                        if j >= 2:
                            pe.wait_ge(*(y_out_v if j % 2 == 0 else y_out_a)(j // 2))
                        for m in range(4):
                            i = nc.tensor.transpose(bank[4 + j % 2][:, m * P:(m + 1) * P],
                                                    ysT[:, 4 * hf + m, b * P:(b + 1) * P], ident)
                        i.then_inc(y_turned.sem, 1)
                pe.wait_ge(*y_out_v(4))
                pe.wait_ge(*y_out_a(4))
                for tt in range(TT):
                    for nb in range(2):
                        for b in range(4):
                            i = nc.tensor.matmul(bank[2 * tt + nb][:, :], cw[:, b, tt * P:(tt + 1) * P],
                                                 ys[:, b, nb * NB:(nb + 1) * NB], start=(b == 0), stop=(b == 3))
                        i.then_inc(summed.sem, 1)

            zero8, zero64 = stat[:, 448:456], stat[:, 448:512]

            def vector(dve):
                nrm.vector(dve)
                have_small(dve)
                dv.done(nc.vector.memset(zero64, 0.0))
                dve.wait_ge(*table_in(48))
                dve.wait_ge(*logits(1))
                for tt in range(TT):
                    dv.done(nc.vector.tensor_tensor(lg[:, tt, :], bank[0][:, tt * 72:(tt + 1) * 72],
                                                    router_b[:, layer, :], ALU.add))
                w = A[:, 3968:4096]
                for tt in range(TT):
                    o = 40 * tt
                    dv.done(nc.vector.max(out=r[:, o:o + 8], in_=lg[:, tt, 0:8]))
                    first_of(dve, r[:, o + 8:o + 16], lg[:, tt, 0:8], r[:, o:o + 1], w)
                    dv.done(nc.vector.tensor_scalar(r[:, o + 16:o + 24], lg[:, tt, 0:8], r[:, o:o + 1], None,
                                                    ALU.subtract))
                    g3 = r[:, o + 8:o + 16].unsqueeze(2).broadcast_to([P, 8, 8])
                    dv.done(nc.vector.tensor_tensor(prod.rearrange("p (g e) -> p g e", g=8),
                                                    lg[:, tt, 8:72].rearrange("p (g e) -> p g e", g=8), g3, ALU.mult))
                    dv.done(nc.vector.tensor_reduce(w[:, 16:24], prod.rearrange("p (g e) -> p e g", g=8), AX, ALU.add))
                    dv.done(nc.vector.max(out=w[:, 24:32], in_=w[:, 16:24]))
                    for k in range(2):
                        if k == 1:
                            dv.done(nc.vector.scalar_tensor_tensor(out=w[:, 16:24], in0=w[:, 40:48], scalar=-3e38,
                                                                   in1=w[:, 16:24], op0=ALU.mult, op1=ALU.add))
                        first_of(dve, w[:, 40:48], w[:, 16:24], w[:, 24 + k:25 + k], w)
                        dv.done(nc.vector.tensor_tensor(oh[:, k, tt, :].rearrange("p (g e) -> p g e", g=8), g3,
                                                        w[:, 40:48].unsqueeze(1).broadcast_to([P, 8, 8]), ALU.mult))
                    i = nc.vector.tensor_tensor(r[:, o + 24:o + 25], w[:, 25:26], w[:, 24:25], ALU.subtract)
                    i.then_inc(gexp_in.sem, 1)
                    dve.wait_ge(*gexp_in(tt + 1))
                nc.vector.tensor_tensor(both, oh[:, 0, :, :], oh[:, 1, :, :], ALU.add).then_inc(picked.sem, 1)
                dve.wait_ge(*gexp(2 * TT))
                for tt in range(TT):
                    o = 40 * tt
                    dv.done(nc.vector.tensor_reduce(r[:, o + 26:o + 27], r[:, o + 16:o + 24], AX, ALU.add))
                    dv.done(nc.vector.tensor_scalar(r[:, o + 27:o + 28], r[:, o + 25:o + 26], 1.0, None, ALU.add))
                    dv.done(nc.vector.tensor_tensor(r[:, o + 28:o + 29], r[:, o + 26:o + 27], r[:, o + 27:o + 28],
                                                    ALU.mult))
                    dv.done(nc.vector.reciprocal(r[:, o + 29:o + 30], r[:, o + 28:o + 29]))
                    dv.done(nc.vector.tensor_tensor(r[:, o + 30:o + 31], r[:, o + 29:o + 30], r[:, o + 25:o + 26],
                                                    ALU.mult))
                dve.wait_ge(*counted(1))
                dv.done(nc.vector.tensor_copy(cnt, bank[1][:, 2 * E:3 * E]))
                dv.done(nc.vector.tensor_tensor_scan(cum, cnt, zero64, 0.0, ALU.add, ALU.add))
                dv.done(nc.vector.tensor_tensor(off, cum, cnt, ALU.subtract))
                for tt in range(TT):
                    o = 40 * tt
                    dv.done(nc.vector.tensor_tensor(w[:, 0:E], bank[1][:, tt * E:(tt + 1) * E], off, ALU.add))
                    for k in range(2):
                        dv.done(nc.vector.tensor_tensor(w[:, E:2 * E], w[:, 0:E], oh[:, k, tt, :], ALU.mult))
                        dv.done(nc.vector.tensor_reduce(r[:, o + 32 + k:o + 33 + k], w[:, E:2 * E], AX, ALU.add))
                    dv.done(nc.vector.tensor_scalar(tmp, iota, r[:, o + 32:o + 33], None, ALU.is_equal))
                    dv.done(nc.vector.scalar_tensor_tensor(out=place[:, tt, :], in0=iota, scalar=r[:, o + 33:o + 34],
                                                           in1=tmp, op0=ALU.is_equal, op1=ALU.add))
                dv.done(nc.vector.tensor_copy(posf[:, 0, :], off))
                for j in range(1, PASSES):
                    dv.done(nc.vector.tensor_scalar(posf[:, j, :], cnt, float(-CAP), float(j * CAP), ALU.add, ALU.min))
                    dv.done(nc.vector.tensor_tensor(posf[:, j, :], posf[:, j, :], off, ALU.add))
                    dv.done(nc.vector.tensor_scalar(posf[:, j, :], posf[:, j, :], float(-TRASH), None, ALU.add))
                    dv.done(nc.vector.scalar_tensor_tensor(out=posf[:, j, :], in0=cnt, scalar=float(j * CAP),
                                                           in1=posf[:, j, :], op0=ALU.is_gt, op1=ALU.mult))
                    dv.done(nc.vector.tensor_scalar(posf[:, j, :], posf[:, j, :], float(TRASH), None, ALU.add))
                dv.done(nc.vector.tensor_reduce(posf[:, PASSES, 0:1], cnt, AX, ALU.max))
                dv.done(nc.vector.tensor_copy(posf[:, PASSES, 1:E], posf[:, 0, 1:E]))
                dv.done(nc.vector.tensor_copy(pos_i[0:1, :], A[0:1, 4096:4096 + (PASSES + 1) * E]))
                nc.vector.memset(xsT[:, :, SLOTS:WIDE], 0.0).then_inc(placed.sem, 1)
                for c in range(0, DC, 2):
                    dve.wait_ge(*gathered(c + 1))
                    nc.vector.tensor_scalar(xsT[:, c, 0:SLOTS], bank[c % 4][:, :], gains[:, 1, layer, c:c + 1], None,
                                            ALU.mult).then_inc(spread.sem, 1)
                for tt in range(TT):
                    o = 40 * tt
                    dv.done(nc.vector.tensor_scalar(cwt[:, tt, :], iota, r[:, o + 32:o + 33], r[:, o + 29:o + 30],
                                                    ALU.is_equal, ALU.mult))
                    dv.done(nc.vector.tensor_scalar(tmp, iota, r[:, o + 33:o + 34], r[:, o + 30:o + 31],
                                                    ALU.is_equal, ALU.mult))
                    i = nc.vector.tensor_tensor(cwt[:, tt, :], cwt[:, tt, :], tmp, ALU.add)
                    if tt == 0:
                        dv.done(i)
                i.then_inc(cwt_ready.sem, 1)
                dve.wait_ge(*cw_turned(1))
                for b in range(2):
                    i = nc.vector.tensor_copy(cw[:, 2 * b:2 * b + 2, :],
                                              bank[4 + b][:, :].rearrange("p (b s) -> p b s", b=2))
                i.then_inc(cw_ready.sem, 1)
                def tokens(index, dst):
                    where = dve.value_load(pos_i[0:1, index], min_val=0, max_val=TRASH)
                    return nc.vector.tensor_copy(dst, xsT[:, :, bass.ds(where, CAP)])

                def hidden(k, rows, wait):
                    g, u, e = bank[4 + k][0:rows, 0:FF], bank[4 + k][0:rows, FF:2 * FF], eb[0:rows, k, :]
                    wait(nc.vector.tensor_scalar(e, e, 1.0, None, ALU.add))
                    wait(nc.vector.reciprocal(e, e))
                    wait(nc.vector.tensor_tensor(e, g, e, ALU.mult))
                    return nc.vector.tensor_tensor(hid[0:rows, k, :], u, e, ALU.mult)

                dve.wait_ge(*spread(4))
                dve.wait_ge(*spread_a(4))
                dve.wait_ge(*logits(1))
                for k in range(2):
                    for q in range(2):
                        i = tokens(slice(2 * k + q, 2 * k + q + 1), xg[:, k, :, q * CAP:(q + 1) * CAP])
                    i.then_inc(x_ready_.sem, 1)
                with dve.Fori(0, E // PER) as turn:
                    for k in range(2):
                        steps = [3 * k]

                        def wait(ins):
                            steps[0] += 1
                            ins.then_inc(vstep.sem, 1)
                            dve.wait_ge(*vstep(turn * 6 + steps[0]))
                        dve.wait_ge(*exped(turn * 2 + k + 1))
                        hidden(k, P, wait).then_inc(hid_ready.sem, 1)
                        dve.wait_ge(*unit_done(turn * 12 + base + 4 * k + 4))
                        for q in range(2):
                            i = tokens(bass.ds(turn * PER + (PER + 2 * k + q), 1), xg[:, k, :, q * CAP:(q + 1) * CAP])
                        i.then_inc(x_ready_.sem, 1)
                    for k in range(2):
                        dve.wait_ge(*unit_done(turn * 12 + base + 10 + 2 * k))
                        nc.vector.tensor_copy(yrow[:, k, 0:NB], bank[2 * k][:, :]).then_inc(rows_v.sem, 1)

                over = dve.value_load(pos_i[0:1, PASSES * E:PASSES * E + 1], min_val=0, max_val=S)
                with dve.If(over > CAP):
                    with dve.Fori(0, (PASSES - 1) * E) as n:
                        steps = [0]

                        def wait(ins):
                            steps[0] += 1
                            ins.then_inc(f_v.sem, 1)
                            dve.wait_ge(*f_v(n * 3 + steps[0]))
                        dve.wait_ge(*f_stored(n + 1))
                        dve.wait_ge(*pair_stored(E // 2 + 1))
                        tokens(bass.ds(n + E, 1), xg[:, 0, :, 0:CAP]).then_inc(f_x.sem, 1)
                        dve.wait_ge(*f_exp(n + 1))
                        hidden(0, CAP, wait).then_inc(f_hid.sem, 1)
                for j in range(0, 8, 2):
                    dve.wait_ge(*y_turned(j + 1))
                    nc.vector.tensor_copy(ys[:, j // 2, 0:NB], bank[4][:, :]).then_inc(y_out_v.sem, 1)
                for tt in range(TT):
                    for nb in range(2):
                        dve.wait_ge(*summed(2 * tt + nb + 1))
                        xs = X[:, tt, nb * NB:(nb + 1) * NB]
                        nc.vector.tensor_tensor(xs, xs, bank[2 * tt + nb][:, :], ALU.add).then_inc(added.sem, 1)


            def scalar(act):
                nrm.scalar(act)
                for tt in range(TT):
                    o = 40 * tt
                    act.wait_ge(*gexp_in(tt + 1))
                    nc.scalar.activation(r[:, o + 16:o + 24], r[:, o + 16:o + 24], ACT.Exp).then_inc(gexp.sem, 1)
                    nc.scalar.activation(r[:, o + 25:o + 26], r[:, o + 24:o + 25], ACT.Exp).then_inc(gexp.sem, 1)
                for c in range(1, DC, 2):
                    act.wait_ge(*gathered(c + 1))
                    nc.scalar.activation(xsT[:, c, 0:SLOTS], bank[c % 4][:, :], ACT.Identity,
                                         scale=gains[:, 1, layer, c:c + 1]).then_inc(spread_a.sem, 1)
                act.wait_ge(*placed(1))
                nc.scalar.activation(stat[:, 9:10], half[:, 0:1], ACT.Copy).then_inc(pair_stored.sem, 1)
                nc.scalar.activation(stat[:, 11:12], half[:, 0:1], ACT.Copy).then_inc(f_stored.sem, 1)

                def store(index, k, q):
                    where = act.value_load(pos_i[0:1, index], min_val=0, max_val=TRASH)
                    for hf in range(2):
                        i = nc.scalar.activation(
                            ysT[:, 4 * hf:4 * hf + 4, bass.ds(where, CAP)],
                            bank[turn_banks[k][hf]][:, :].rearrange("p (m s) -> p m s", m=4)[:, :, q * CAP:(q + 1) * CAP],
                            ACT.Copy)
                    return i

                def copy_hidden(k, rows):
                    return nc.scalar.activation(hidT[:, k, :, 0:rows],
                                                bank[6][:, 0:2 * P].rearrange("p (c n) -> p c n", c=2)[:, :, 0:rows],
                                                ACT.Copy)

                with act.Fori(0, E // PER) as turn:
                    for k in range(2):
                        act.wait_ge(*unit_done(turn * 12 + base + 4 * k + 4))
                        nc.scalar.activation(eb[:, k, :], bank[4 + k][:, 0:FF], ACT.Exp, scale=-1.0).then_inc(exped.sem, 1)
                    for k in range(2):
                        act.wait_ge(*h_turned(turn * 2 + k + 1))
                        copy_hidden(k, P).then_inc(hT_ready.sem, 1)
                        act.wait_ge(*unit_done(turn * 12 + base + 10 + 2 * k))
                        nc.scalar.activation(yrow[:, k, NB:D], bank[2 * k + 1][:, :], ACT.Copy).then_inc(rows_a.sem, 1)
                    for k in range(2):
                        act.wait_ge(*rows_turned(turn * 2 + k + 1))
                        act.wait_ge(*pair_stored(turn * 2 + k + 1))
                        store(bass.ds(turn * PER + 2 * k, 1), k, 0).then_inc(first_stored.sem, 1)
                        act.wait_ge(*first_stored(turn * 2 + k + 1))
                        store(bass.ds(turn * PER + 2 * k + 1, 1), k, 1).then_inc(pair_stored.sem, 1)
                over = act.value_load(pos_i[0:1, PASSES * E:PASSES * E + 1], min_val=0, max_val=S)
                with act.If(over > CAP):
                    with act.Fori(0, (PASSES - 1) * E) as n:
                        act.wait_ge(*pair_stored(E // 2 + 1))
                        act.wait_ge(*f_stored(n + 1))
                        act.wait_ge(*f_up(n + 1))
                        nc.scalar.activation(eb[0:CAP, 0, :], bank[4][0:CAP, 0:FF], ACT.Exp,
                                             scale=-1.0).then_inc(f_exp.sem, 1)
                        act.wait_ge(*f_turned(n + 1))
                        copy_hidden(0, CAP).then_inc(f_hT.sem, 1)
                        act.wait_ge(*f_down(n + 1))
                        nc.scalar.activation(yrow[0:CAP, 0, 0:NB], bank[0][0:CAP, :], ACT.Copy)
                        nc.scalar.activation(yrow[0:CAP, 0, NB:D], bank[1][0:CAP, :], ACT.Copy).then_inc(f_rows.sem, 1)
                        act.wait_ge(*f_rturned(n + 1))
                        store(bass.ds(n + E, 1), 0, 0).then_inc(f_stored.sem, 1)
                for j in range(1, 8, 2):
                    act.wait_ge(*y_turned(j + 1))
                    nc.scalar.activation(ys[:, j // 2, NB:D], bank[5][:, :], ACT.Copy).then_inc(y_out_a.sem, 1)

            def sync(sp):
                with sp.Fori(0, E // PER) as turn:
                    for k in range(3 * PER):
                        u = base + k
                        sp.wait_ge(*unit_done(turn * 12 + u - RING + 1))
                        w, at_ = next((w, at_) for w, at_ in ((gate_w, GATE_AT), (up_w, UP_AT), (down_w, DOWN_AT))
                                      if k in at_)
                        e = turn * PER + at_.index(k)
                        src = w[bass.ds(e, 1), :, :].rearrange("e (p c) n -> p (e c n)", p=P)
                        sp.dma_start(slot(u), src).then_inc(unit_full[u % RING].sem, 16)

            def gpsimd(pool):
                x_free(pool)
                pool.dma_start(router_w[:, :, 0:GROUPS],
                               t["moe_w_group"][layer].rearrange("(p c) n -> p c n", c=DC)).then_inc(table_in.sem, 16)
                pool.dma_start(router_w[:, :, GROUPS:],
                               t["moe_w_expert"][layer].rearrange("(p c) n -> p c n", c=DC)).then_inc(table_in.sem, 16)
                pool.dma_start(iota, later["iota"]).then_inc(table_in.sem, 16)
                nrm.gpsimd(pool)
                pool.wait_ge(*pair_stored(E // 2 + 1))
                over = pool.value_load(pos_i[0:1, PASSES * E:PASSES * E + 1], min_val=0, max_val=S)
                with pool.If(over > CAP):
                    with pool.Fori(0, PASSES - 1) as ps_:
                        with pool.Fori(0, E) as e:
                            pool.wait_ge(*f_stored(ps_ * E + e + 1))
                            for k, w in enumerate((gate_w, up_w, down_w)):
                                pool.dma_start(A[:, k * 2048:(k + 1) * 2048],
                                               w[bass.ds(e, 1), :, :].rearrange("e (p c) n -> p (e c n)", p=P)
                                               ).then_inc(f_full.sem, 16)

            def done(eng):
                eng.wait_ge(*added(4))
            st.tensor, st.vector, st.scalar, st.gpsimd, st.sync, st.ready = tensor, vector, scalar, gpsimd, sync, done
            return st

        m1_base = len(units)
        m1 = moe(0, "m1", o1_done, a1.ready)
        m1_units = (m1_base, m1_base + 3 * E)

        n2 = norm_stage("n2", m1.ready, gains[:, 0, 1, :])
        A_WIDTH = MLA_Q + MLA_KV + ROT

        def copy_a(eng, n, tt, ps):
            return nc.scalar.activation(hn[:, tt, n * NB:n * NB + ps.shape[1]], ps, ACT.Copy)
        pa = project_stage("pa", n2.ready, hT_lhs, square_units(t["mla_w_a"][0], A_WIDTH), copy_a)
        a_sq, a_rs, a_scaled = sem("a_sq"), sem("a_rs"), sem("a_scaled")
        a_parts = [(0, MLA_Q), (MLA_Q, MLA_Q + MLA_KV)]

        def latent_scalar(act):
            act.wait_ge(*pa.copied(4))
            for k, (a, b) in enumerate(a_parts):
                for tt in range(TT):
                    nc.scalar.activation(BC[:, k * 1024 + tt * 512:k * 1024 + tt * 512 + b - a], hn[:, tt, a:b], ACT.Square,
                                         accum_out=stat[:, 64 + 2 * k + tt:65 + 2 * k + tt]).then_inc(a_sq.sem, 1)

        def latent_gpsimd(pool):
            pool.wait_ge(*a_sq(4))
            for k, (a, b) in enumerate(a_parts):
                po.done(nc.gpsimd.tensor_scalar(stat[:, 68 + 2 * k:70 + 2 * k], stat[:, 64 + 2 * k:66 + 2 * k],
                                                1.0 / (b - a), EPS, ALU.mult, ALU.add))
            nc.gpsimd.tensor_tensor(stat[:, 72:76], stat[:, 68:72], half[:, 0:4], ALU.pow).then_inc(a_rs.sem, 1)

        def latent_vector(dve):
            dve.wait_ge(*a_rs(1))
            for k, (a, b) in enumerate(a_parts):
                for tt in range(TT):
                    i = nc.vector.tensor_scalar(hn[:, tt, a:b], hn[:, tt, a:b], stat[:, 72 + 2 * k + tt:73 + 2 * k + tt],
                                                None, ALU.mult)
            i.then_inc(a_scaled.sem, 1)

        def latent_ready(pe):
            pe.wait_ge(*a_scaled(1))
        cT = BC[:, 8192:8192 + 5 * S].rearrange("p (c s) -> p c s", c=5)
        t3 = turn_stage("t3", latent_ready,
                        [(lambda tt, c=c: hn[:, tt, c:MLA_Q:3], P, cT[:, c, :], mla_gain[:, c:c + 1]) for c in range(3)] +
                        [(lambda tt, c=c: hn[:, tt, MLA_Q + c:MLA_Q + MLA_KV:2], P, cT[:, 3 + c, :],
                          mla_gain[:, 3 + c:4 + c]) for c in range(2)])
        q_l = A[:, 0:3072].rearrange("p (t h d) -> p t h d", t=TT, h=HEADS)
        k_l = A[:, 3072:6144].rearrange("p (t h d) -> p t h d", t=TT, h=HEADS)
        v_l = A[:, 6144:8192].rearrange("p (t h d) -> p t h d", t=TT, h=HEADS)

        def copy_q(eng, n, tt, ps):
            return nc.scalar.activation(A[:, tt * 1536 + n * NB:tt * 1536 + (n + 1) * NB], ps, ACT.Copy)

        def copy_kv(eng, n, tt, ps):
            kv = ps.rearrange("p (h d) -> p h d", h=2)
            nc.scalar.activation(k_l[:, tt, 2 * n:2 * n + 2, 0:NOPE], kv[:, :, 0:NOPE], ACT.Copy)
            return nc.scalar.activation(v_l[:, tt, 2 * n:2 * n + 2, :], kv[:, :, NOPE:], ACT.Copy)
        pq = project_stage("pq", t3.ready, lambda c, tt: cT[:, c, tt * P:(tt + 1) * P],
                           square_units(t["mla_w_qb"][0], 1536, kc=3, per=3), copy_q)
        kv_src = t["mla_w_kvb"][0].rearrange("(p c) n -> p c n", c=2)
        kv_blocks = []
        for n in range(2):
            u = plan(lambda a: a.rearrange("p (c n) -> p c n", c=2), kv_src[:, :, n * 1024:(n + 1) * 1024])
            for hf in range(2):
                kv_blocks.append((NB, [(u, lambda a, hf=hf: a.rearrange("p (c n) -> p c n", c=2)[:, :, hf * NB:(hf + 1) * NB],
                                        2, hf == 0)]))

        def q_left(pe):
            pe.wait_ge(*pq.copied(6))
        pkv = project_stage("pkv", q_left, lambda c, tt: cT[:, 3 + c, tt * P:(tt + 1) * P], kv_blocks, copy_kv)
        l_sq, l_ss, l_rs, l_pe, l_qk = sem("l_sq"), sem("l_ss"), sem("l_rs"), sem("l_pe"), sem("l_qk")
        l_items = [(q_l, 0, 0), (q_l, 0, 1), (k_l, 1, 0), (k_l, 1, 1)]

        def l_squares(j):
            return BC[:, (j % 2) * 1536:(j % 2 + 1) * 1536]

        def heads_scalar(act):
            for j, (x, qk, tt) in enumerate(l_items):
                if j < 2:
                    act.wait_ge(*pq.copied(6))
                else:
                    act.wait_ge(*pkv.copied(8))
                    act.wait_ge(*l_pe(j - 1))
                    act.wait_ge(*l_ss(j - 1))
                nc.scalar.activation(l_squares(j), x[:, tt, :, :].rearrange("p h d -> p (h d)"),
                                     ACT.Square).then_inc(l_sq.sem, 1)

        def heads_gpsimd(pool):
            for j in range(4):
                pool.wait_ge(*l_ss(j + 1))
                a, b = 64 + 8 * (j % 2), 80 + 8 * (j % 2)
                po.done(nc.gpsimd.tensor_scalar(stat[:, 96:104], stat[:, a:a + 8], 1.0 / MLA_QK, EPS, ALU.mult, ALU.add))
                nc.gpsimd.tensor_tensor(stat[:, b:b + 8], stat[:, 96:104], half[:, 0:8], ALU.pow).then_inc(l_rs.sem, 1)

        def heads_vector(dve):
            fold_rope(1)
            for j, (x, qk, tt) in enumerate(l_items):
                if qk == 1:
                    dve.wait_ge(*pkv.copied(8))
                    nc.vector.tensor_copy(k_l[:, tt, :, NOPE:], hn[:, tt, MLA_Q + MLA_KV:A_WIDTH].unsqueeze(1)
                                          .broadcast_to([P, HEADS, ROT])).then_inc(l_pe.sem, 1)
                dve.wait_ge(*l_sq(j + 1))
                if j >= 2:
                    dve.wait_ge(*l_rs(j))
                nc.vector.tensor_reduce(stat[:, 64 + 8 * (j % 2):72 + 8 * (j % 2)],
                                        l_squares(j).rearrange("p (h d) -> p h d", h=HEADS), AX, ALU.add).then_inc(l_ss.sem, 1)
                t1_ = BC[:, 3072:3584].rearrange("p (h d) -> p h d", h=HEADS)
                t2_ = BC[:, 3584:4096].rearrange("p (h d) -> p h d", h=HEADS)
                rotate(dve, x[:, tt, :, NOPE:], None, ROT, HEADS, qk, tt, t1_, t2_)
                g = qk_gain[:, qk, 0:NOPE].unsqueeze(1).broadcast_to([P, HEADS, NOPE])
                dv.done(nc.vector.tensor_tensor(x[:, tt, :, 0:NOPE], x[:, tt, :, 0:NOPE], g, ALU.mult))
                dve.wait_ge(*l_rs(j + 1))
                r = stat[:, 80 + 8 * (j % 2):88 + 8 * (j % 2)].unsqueeze(2)
                nc.vector.tensor_tensor(x[:, tt, :, 0:NOPE], x[:, tt, :, 0:NOPE], r.broadcast_to([P, HEADS, NOPE]),
                                        ALU.mult)
                dv.done(nc.vector.tensor_tensor(x[:, tt, :, NOPE:], t1_, r.broadcast_to([P, HEADS, ROT]), ALU.mult))
            nc.vector.tensor_copy(stat[:, 8:9], stat[:, 64:65]).then_inc(l_qk.sem, 1)

        def l_ready(pe):
            pe.wait_ge(*l_qk(1))
        nopeT = BC[:, 0:16 * S].rearrange("p (h k s) -> p h k s", h=HEADS, k=2)
        peT = BC[:, 16 * S:32 * S].rearrange("p (h k s) -> p h k s", h=HEADS, k=2)
        l_jobs = []
        for h in range(HEADS):
            for k, x in enumerate((q_l, k_l)):
                l_jobs.append((lambda tt, x=x, h=h: x[:, tt, h, 0:NOPE], P, nopeT[:, h, k, :], None))
            for k, x in enumerate((q_l, k_l)):
                l_jobs.append((lambda tt, x=x, h=h: x[:, tt, h, NOPE:], ROT, peT[0:ROT, h, k, :], None))
        t4 = turn_stage("t4", l_ready, l_jobs)
        cond2 = Conditioning("cond2", 6, 12, HEADS)

        def latent_head(h):
            pairs = [(lambda tt: nopeT[:, h, 0, tt * P:(tt + 1) * P], lambda k0, k1: nopeT[:, h, 1, k0:k1]),
                     (lambda tt: peT[0:ROT, h, 0, tt * P:(tt + 1) * P], lambda k0, k1: peT[0:ROT, h, 1, k0:k1])]
            return ([pairs], lambda kt: v_l[:, kt, h, :], lambda tt: hn[:, tt, h * P:(h + 1) * P])
        a2 = attention_stage("a2", t4.ready, [latent_head(h) for h in range(HEADS)], MLA_QK ** -0.5, P,
                             lambda h: at["causal"], filler=cond2)
        t5 = heads_turned("t5", a2.ready)
        o2 = project_stage("o2", t5.ready, hT_lhs, square_units(t["mla_w_out"][0], D, order="(c p)"), add_x)

        def o2_done(eng):
            eng.wait_ge(*o2.copied(4))
        u3 = len(units)
        m2 = moe(1, "m2", o2_done, a2.ready)
        u4 = len(units)

        mod_in, mod_ready = sem("mod_in"), sem("mod_ready")
        b_cols = stat[:, 256:288].rearrange("p (k c) -> p k c", k=4)
        MOD = (0, 1, 3, 4)

        def conditioning_gpsimd(pool):
            cond1.ready(pool)
            cond2.ready(pool)
            for k, m in enumerate(MOD):
                pool.dma_start(modc[:, k, :], mod_dram[m * D:(m + 1) * D].rearrange("(p c) -> p c", c=DC)
                               ).then_inc(mod_in.sem, 16)
                pool.dma_start(b_cols[:, k, :], t["b_ada_2"][m * D:(m + 1) * D].rearrange("(p c) -> p c", c=DC)
                               ).then_inc(mod_in.sem, 16)

        def conditioning_vector(dve):
            dve.wait_ge(*mod_in(16 * 8))
            dv.done(nc.vector.tensor_tensor(modc[:, :, :], modc[:, :, :], b_cols, ALU.add))
            for k in range(2):
                dv.done(nc.vector.tensor_scalar(modc[:, 2 * k + 1, :], modc[:, 2 * k + 1, :], 1.0, None, ALU.add))
                i = nc.vector.tensor_tensor(modc[:, 2 * k + 1, :], modc[:, 2 * k + 1, :], gains2[:, k, :], ALU.mult)
            i.then_inc(mod_ready.sem, 1)
            dve.wait_ge(*mod_ready(1))

        n3 = norm_stage("n3", m2.ready, modc[:, 1, :], shift=modc[:, 0, :], extra=[(mod_ready, 1)])
        z = A[:, 0:TT * HYB_IN].rearrange("p (t n) -> p t n", t=TT)
        QA, KA, VA, QB, KB, VB, FB = 0, 512, 640, 768, 1280, 1792, 2304
        z_blocks = square_units(t["w_in_2"], HYB_IN - 4 * NB, col0=4 * NB) + square_units(t["w_in_2"], 4 * NB)
        z_at = (4, 0, 1, 2, 3)

        def copy_z(eng, n, tt, ps):
            c0 = z_at[n] * NB
            return nc.scalar.activation(z[:, tt, c0:c0 + ps.shape[1]], ps, ACT.Copy)
        pz = project_stage("pz", n3.ready, hT_lhs, z_blocks, copy_z)
        table = A[:, 4624:4624 + P + 2 * SPAN]
        upto, window, dist = table[:, 0:P], table[:, P:P + SPAN], table[:, P + SPAN:]
        fk = A[:, 5520:5520 + HEADS * S].rearrange("p (h s) -> p h s", h=HEADS)
        hbias = A[:, 7568:7568 + SPAN]
        fox = stat[:, 288:288 + 5 * TT * HEADS].rearrange("p (k t h) -> p k t h", k=5, t=TT)
        f_raw, f_abs, f_log, f_sum, f_low = (fox[:, k, :, :] for k in range(5))
        table3, fx = sem("table3"), sem("fx")
        fx_exp, fx_log, fx_ready, fx_sum, fx_col = sem("fx_exp"), sem("fx_log"), sem("fx_ready"), sem("fx_sum"), sem("fx_col")
        fx_turned, fx_rows, fx_spread, fx_out = sem("fx_turned"), sem("fx_rows"), sem("fx_spread"), sem("fx_out")
        fT = hT[0:HEADS, 0, :]

        def tables_gpsimd(pool):
            m2.ready(pool)
            pool.dma_start(upto, later["upto"]).then_inc(table3.sem, 16)
            pool.dma_start(window, later["window"]).then_inc(table3.sem, 16)
            pool.dma_start(dist, later["dist"]).then_inc(table3.sem, 16)

        def forget_vector(dve):
            dve.wait_ge(*pz.copied(2))
            dv.done(nc.vector.tensor_tensor(f_raw, z[:, :, FB:FB + HEADS],
                                            f_bias.unsqueeze(1).broadcast_to([P, TT, HEADS]), ALU.add))
            nc.vector.tensor_scalar(f_low, f_raw, 0.0, None, ALU.min)
            dv.done(nc.vector.tensor_scalar(f_abs, f_raw, -1.0, None, ALU.mult))
            nc.vector.tensor_tensor(f_abs, f_abs, f_raw, ALU.max).then_inc(fx.sem, 1)
            dve.wait_ge(*fx_exp(1))
            nc.vector.tensor_scalar(f_abs, f_abs, 1.0, None, ALU.add).then_inc(fx.sem, 1)
            dve.wait_ge(*fx_log(1))
            nc.vector.tensor_tensor(f_log, f_low, f_abs, ALU.subtract).then_inc(fx_ready.sem, 1)
            dve.wait_ge(*fx_sum(1))
            nc.vector.tensor_copy(f_sum, bank[7][:, 0:TT * HEADS].rearrange("p (t h) -> p t h", t=TT)).then_inc(fx_col.sem, 1)
            dve.wait_ge(*fx_turned(1))
            nc.vector.tensor_copy(fT, bank[7][0:HEADS, 0:S]).then_inc(fx_rows.sem, 1)
            for b in range(4):
                dve.wait_ge(*fx_spread(b + 1))
                nc.vector.tensor_copy(fk[:, 2 * b:2 * b + 2, :], bank[4 + b][:, :].rearrange("p (h s) -> p h s", h=2)
                                      ).then_inc(fx_out.sem, 1)

        def forget_scalar(act):
            act.wait_ge(*fx(1))
            nc.scalar.activation(f_abs, f_abs, ACT.Exp, scale=-1.0).then_inc(fx_exp.sem, 1)
            act.wait_ge(*fx(2))
            nc.scalar.activation(f_abs, f_abs, ACT.Ln).then_inc(fx_log.sem, 1)

        def forget_tensor(pe):
            pe.wait_ge(*table3(48))
            pe.wait_ge(*fx_ready(1))
            nc.tensor.matmul(bank[7][:, 0:HEADS], upto, f_log[:, 0, :], start=True, stop=True)
            nc.tensor.matmul(bank[7][:, HEADS:2 * HEADS], ones, f_log[:, 0, :], start=True, stop=False)
            nc.tensor.matmul(bank[7][:, HEADS:2 * HEADS], upto, f_log[:, 1, :], start=False,
                             stop=True).then_inc(fx_sum.sem, 1)
            pe.wait_ge(*fx_col(1))
            for tt in range(TT):
                i = nc.tensor.transpose(bank[7][0:HEADS, tt * P:(tt + 1) * P], f_sum[:, tt, :], ident)
            i.then_inc(fx_turned.sem, 1)
            pe.wait_ge(*fx_rows(1))
            for h in range(HEADS):
                i = nc.tensor.matmul(bank[4 + h // 2][:, (h % 2) * S:(h % 2 + 1) * S],
                                     ident[0:HEADS, h:h + 1].broadcast_to([HEADS, P]), fT, start=True, stop=True)
                if h % 2:
                    i.then_inc(fx_spread.sem, 1)

        def z_ready(pe):
            pe.wait_ge(*pz.copied(10))
            pe.wait_ge(*fx_out(4))
        zT = BC[0:ROT, 0:26 * S].rearrange("p (j s) -> p j s", s=S)
        cols = [QA + 64 * h for h in range(8)] + [KA, KA + 64] + [QB + 64 * h for h in range(8)] + \
               [KB + 64 * h for h in range(8)]
        t6 = turn_stage("t6", z_ready, [(lambda tt, c0=c0: z[:, tt, c0:c0 + ROT], ROT, zT[:, j, :], None)
                                        for j, c0 in enumerate(cols)])

        def head3(h):
            if h < HEADS:
                qj, kj, vc, oc = h, 8 + h // 4, VA + 64 * (h // 4), 64 * h
            else:
                qj, kj, vc, oc = 10 + h - 8, 18 + h - 8, VB + 64 * (h - 8), 64 * h
            return ([[(lambda tt: zT[:, qj, tt * P:(tt + 1) * P], lambda k0, k1: zT[:, kj, k0:k1])]],
                    lambda kt: z[:, kt, vc:vc + ROT], lambda tt: hn[:, tt, oc:oc + ROT])

        def bias3(h):
            if h < HEADS:
                slope = 2.0 ** (-8.0 * (h + 1) / HEADS)
                dv.done(nc.vector.scalar_tensor_tensor(out=hbias, in0=dist, scalar=-slope, in1=window, op0=ALU.mult,
                                                       op1=ALU.add))
                return hbias
            for tt, (a, b) in enumerate([(0, P), (P, SPAN)]):
                i = nc.vector.tensor_scalar(hbias[:, a:b], fk[:, h - HEADS, 0:b - a], -1.0,
                                            f_sum[:, tt, h - HEADS:h - HEADS + 1], ALU.mult, ALU.add)
            dv.done(i)
            dv.done(nc.vector.tensor_tensor(hbias, hbias, at["causal"], ALU.add))
            return hbias
        a3 = attention_stage("a3", t6.ready, [head3(h) for h in range(2 * HEADS)], ROT ** -0.5, ROT, bias3, sink=True)
        t7 = heads_turned("t7", a3.ready)

        gate_in = [sem("gate1_in"), sem("gate2_in")]
        gate_rows = [A[:, 0:D], A[:, 5632:5632 + D]]
        gate_bias = [A[:, D:2 * D], A[:, 6656:6656 + D]]
        scratch = [A[:, 2048:3072], BC[:, 7168:8192]]
        gate_ready = [sem("gate1_ready"), sem("gate2_ready")]
        g_fin = A[:, 0:D]
        fin_in = sem("fin_in")

        def gate_gpsimd(pool, k):
            m = (2, 5)[k]
            pool.dma_start(gate_rows[k], mod_dram[m * D:(m + 1) * D].partition_broadcast(P)).then_inc(gate_in[k].sem, 16)
            pool.dma_start(gate_bias[k], t["b_ada_2"][m * D:(m + 1) * D].partition_broadcast(P)).then_inc(gate_in[k].sem, 16)

        def gate_vector(dve, k):
            dve.wait_ge(*gate_in[k](32))
            dv.done(nc.vector.tensor_tensor(gate_rows[k], gate_rows[k], gate_bias[k], ALU.add))

        def gated(k):
            def add(eng, n, tt, ps):
                xs = X[:, tt, n * NB:(n + 1) * NB]
                product = scratch[k][:, tt * NB:(tt + 1) * NB]
                dv.done(nc.vector.tensor_tensor(product, ps, gate_rows[k][:, n * NB:(n + 1) * NB], ALU.mult))
                return nc.vector.tensor_tensor(xs, xs, product, ALU.add)
            return add
        o3 = project_stage("o3", t7.ready, hT_lhs, square_units(t["w_out_2"], D, order="(c p)"), gated(0))

        def o3_done(eng):
            eng.wait_ge(*o3.copied(4))

        n4 = norm_stage("n4", o3_done, modc[:, 3, :], shift=modc[:, 2, :])
        FB_ = DFF // P
        PAIRS = FB_ // 2
        up_src = t["w_up_2"].rearrange("(p c) n -> p c n", c=DC)
        down_src = t["w_down_2"].rearrange("(c p) n -> p c n", p=P)
        up_units = [[plan(lambda a: a.rearrange("p (c n) -> p c n", c=DC), up_src[:, :, c0 + j * 256:c0 + (j + 1) * 256])
                     for c0 in (DFF, 0)] for j in range(PAIRS)]
        down_units = [plan(lambda a: a.rearrange("p (c n) -> p c n", c=2), down_src[:, 2 * j:2 * j + 2, :])
                      for j in range(PAIRS)]
        hidT3 = BC[:, 0:FB_ * S].rearrange("p (b s) -> p b s", b=FB_)
        cw3 = BC[:, 5632:5632 + 4 * 2 * FB_].rearrange("p (k b) -> p k b", k=4)
        cw_rows = BC[0:2 * FB_, 6144:6144 + 4 * P].rearrange("p (k c) -> p k c", k=4)
        cw_in, cw_turned3, cw_out = sem("cw_in"), sem("cw_turned3"), sem("cw_out")
        raw = A[:, 2048:4096].rearrange("p (j h n) -> p j h n", j=2, h=2)
        yv = A[:, 4096:5120].rearrange("p (h b s) -> p h b s", h=2, b=2)
        ev = A[:, 5120:5632].rearrange("p (b s) -> p b s", b=2)
        raw_copied, raw_used, g_conv, g_exp, hid3 = (sem("raw_copied"), sem("raw_used"), sem("g_conv"), sem("g_exp"),
                                                     sem("hid3"))
        down_done, out_added = sem("down_done"), sem("out_added")

        def mlp_gpsimd(pool):
            a3.ready(pool)
            gate_gpsimd(pool, 0)
            for k in range(3):
                pool.dma_start(cw_rows[:, k, :], t["conv_w_2"][k].rearrange("(b p) -> b p", p=P)).then_inc(cw_in.sem, 16)
            pool.dma_start(cw_rows[:, 3, :], t["conv_b_2"].rearrange("(b p) -> b p", p=P)).then_inc(cw_in.sem, 16)
            o3_done(pool)
            gate_gpsimd(pool, 1)
            pool.dma_start(g_fin, t["g_final_2"].partition_broadcast(P)).then_inc(fin_in.sem, 16)

        def mlp_tensor(pe):
            pe.wait_ge(*cw_in(64))
            for k in range(4):
                i = nc.tensor.transpose(bank[6][:, k * 64:k * 64 + 2 * FB_], cw_rows[:, k, :], ident[0:2 * FB_, 0:2 * FB_])
            i.then_inc(cw_turned3.sem, 1)
            n4.ready(pe)
            for j in range(PAIRS):
                for h in range(2):
                    n = 2 * j + h
                    if n >= 4:
                        pe.wait_ge(*raw_copied(n - 3))
                    u = up_units[j][h]
                    unit_here(pe, u)
                    w = units[u][0](slot(u))
                    for b in range(2):
                        for c in range(DC):
                            i = nc.tensor.matmul(bank[n % 4][:, b * S:(b + 1) * S], w[:, c, b * P:(b + 1) * P],
                                                 hT[:, c, :], start=(c == 0), stop=(c == DC - 1))
                    i.then_inc(unit_done.sem, 1)
            pe.wait_ge(*cw_out(1))
            for j in range(PAIRS):
                u = down_units[j]
                pe.wait_ge(*hid3(j + 1))
                unit_here(pe, u)
                w = units[u][0](slot(u))
                for c in range(2):
                    for tt in range(TT):
                        for nb in range(2):
                            i = nc.tensor.matmul(bank[4 + 2 * tt + nb][:, :], hidT3[:, 2 * j + c, tt * P:(tt + 1) * P],
                                                 w[:, c, nb * NB:(nb + 1) * NB], start=(j == 0 and c == 0),
                                                 stop=(j == PAIRS - 1 and c == 1))
                i.then_inc(unit_done.sem, 1)

        def mlp_scalar(act):
            for j in range(PAIRS):
                for h in range(2):
                    n = 2 * j + h
                    act.wait_ge(*unit_done(up_units[j][h] + 1))
                    if j >= 2:
                        act.wait_ge(*raw_used(n - 3))
                    nc.scalar.activation(raw[:, j % 2, h, :], bank[n % 4][:, :], ACT.Copy).then_inc(raw_copied.sem, 1)
                act.wait_ge(*g_conv(j + 1))
                nc.scalar.activation(ev, yv[:, 0, :, :], ACT.Exp, scale=-1.0).then_inc(g_exp.sem, 1)

        def mlp_vector(dve):
            dve.wait_ge(*cw_turned3(1))
            nc.vector.tensor_copy(cw3, bank[6][:, 0:256].rearrange("p (k b) -> p k b", k=4)[:, :, 0:2 * FB_]
                                  ).then_inc(cw_out.sem, 1)
            dve.wait_ge(*cw_out(1))
            for j in range(PAIRS):
                for h in range(2):
                    dve.wait_ge(*raw_copied(2 * j + h + 1))
                    blocks = [((FB_ if h == 0 else 0) + 2 * j + b, raw[:, j % 2, h, b * S:(b + 1) * S], yv[:, h, b, :])
                              for b in range(2)]
                    for ch, x, y in blocks:
                        i = nc.vector.tensor_scalar(y, x, cw3[:, 2, ch:ch + 1], cw3[:, 3, ch:ch + 1], ALU.mult, ALU.add)
                    dv.done(i)
                    for back in (1, 2):
                        for ch, x, y in blocks:
                            i = nc.vector.scalar_tensor_tensor(out=y[:, back:], in0=x[:, 0:S - back],
                                                               scalar=cw3[:, 2 - back, ch:ch + 1], in1=y[:, back:],
                                                               op0=ALU.mult, op1=ALU.add)
                        if back == 1:
                            dv.done(i)
                    i.then_inc(raw_used.sem, 1)
                    if h == 0:
                        dve.wait_ge(*raw_used(2 * j + 1))
                        nc.vector.tensor_copy(stat[:, 14:15], stat[:, 64:65]).then_inc(g_conv.sem, 1)
                dve.wait_ge(*g_exp(j + 1))
                dve.wait_ge(*raw_used(2 * j + 2))
                dv.done(nc.vector.tensor_scalar(ev, ev, 1.0, None, ALU.add))
                dv.done(nc.vector.reciprocal(ev, ev))
                dv.done(nc.vector.tensor_tensor(ev, ev, yv[:, 0, :, :], ALU.mult))
                nc.vector.tensor_tensor(hidT3[:, 2 * j:2 * j + 2, :], ev, yv[:, 1, :, :], ALU.mult).then_inc(hid3.sem, 1)
            gate_vector(dve, 1)
            dve.wait_ge(*unit_done(down_units[-1] + 1))
            for nb in range(2):
                for tt in range(TT):
                    gated(1)(dve, nb, tt, bank[4 + 2 * tt + nb][:, :]).then_inc(out_added.sem, 1)

        last_sq, last_rs, result = sem("last_sq"), sem("last_rs"), sem("result")

        def last_scalar(act):
            act.wait_ge(*out_added(4))
            for tt in range(TT):
                nc.scalar.activation(hT[:, :, :].rearrange("p c s -> p (c s)")[:, tt * D:(tt + 1) * D], X[:, tt, :],
                                     ACT.Square, accum_out=stat[:, tt:tt + 1]).then_inc(last_sq.sem, 1)

        def last_gpsimd(pool):
            pool.wait_ge(*last_sq(TT))
            po.done(nc.gpsimd.tensor_scalar(stat[:, 2:4], stat[:, 0:2], 1.0 / D, EPS, ALU.mult, ALU.add))
            nc.gpsimd.tensor_tensor(stat[:, 2:4], stat[:, 2:4], half[:, 0:TT], ALU.pow).then_inc(last_rs.sem, 1)

        def last_vector(dve):
            dve.wait_ge(*last_rs(1))
            dve.wait_ge(*fin_in(16))
            for tt in range(TT):
                nc.vector.scalar_tensor_tensor(out=hn[:, tt, :], in0=X[:, tt, :], scalar=stat[:, 2 + tt:3 + tt], in1=g_fin,
                                               op0=ALU.mult, op1=ALU.mult).then_inc(result.sem, 1)

        block = ctx.enter_context(nc.Block())
        final_out = sem("final_out")

        @block.sync
        def _(sp):
            def load(first, last):
                for u in range(first, last):
                    load_unit(sp, u)
            load(0, m1_units[0])
            m1.sync(sp)
            load(m1_units[1], u3)
            m2.sync(sp)
            load(u4, len(units))
            for tt in range(TT):
                sp.wait_ge(*result(tt + 1))
                sp.dma_start(out[0, tt * P:(tt + 1) * P, :], hn[:, tt, :]).then_inc(final_out.sem, 16)
            sp.wait_ge(*final_out(16 * TT))

        @block.gpsimd
        def _(pool):
            po.eng = pool
            start_gpsimd(pool)
            n1.gpsimd(pool)
            rope_gpsimd(pool)
            sub_gpsimd(pool)
            m1.gpsimd(pool)
            n2.gpsimd(pool)
            latent_gpsimd(pool)
            heads_gpsimd(pool)
            conditioning_gpsimd(pool)
            m2.gpsimd(pool)
            tables_gpsimd(pool)
            n3.gpsimd(pool)
            mlp_gpsimd(pool)
            n4.gpsimd(pool)
            last_gpsimd(pool)

        @block.scalar
        def _(act):
            start_scalar(act)
            n1.scalar(act)
            setup_scalar(act)
            p1.drain(act)
            t1.scalar(act)
            a1.scalar(act)
            sub_scalar(act)
            t2.scalar(act)
            m1.scalar(act)
            n2.scalar(act)
            pa.drain(act)
            latent_scalar(act)
            t3.scalar(act)
            pq.drain(act)
            pkv.drain(act)
            heads_scalar(act)
            t4.scalar(act)
            a2.scalar(act)
            t5.scalar(act)
            m2.scalar(act)
            n3.scalar(act)
            pz.drain(act)
            forget_scalar(act)
            t6.scalar(act)
            a3.scalar(act)
            t7.scalar(act)
            n4.scalar(act)
            mlp_scalar(act)
            last_scalar(act)

        @block.vector
        def _(dve):
            dv.eng = dve
            n1.vector(dve)
            setup_vector(dve)
            rope_vector(dve)
            t1.vector(dve)
            a1.vector(dve)
            sub_vector(dve)
            t2.vector(dve)
            o1.drain(dve)
            m1.vector(dve)
            n2.vector(dve)
            latent_vector(dve)
            t3.vector(dve)
            heads_vector(dve)
            t4.vector(dve)
            a2.vector(dve)
            t5.vector(dve)
            o2.drain(dve)
            m2.vector(dve)
            conditioning_vector(dve)
            n3.vector(dve)
            forget_vector(dve)
            t6.vector(dve)
            a3.vector(dve)
            t7.vector(dve)
            gate_vector(dve, 0)
            o3.drain(dve)
            n4.vector(dve)
            mlp_vector(dve)
            last_vector(dve)

        @block.tensor
        def _(pe):
            n1.tensor(pe)
            p1.tensor(pe)
            t1.tensor(pe)
            a1.tensor(pe)
            t2.tensor(pe)
            o1.tensor(pe)
            m1.tensor(pe)
            n2.tensor(pe)
            pa.tensor(pe)
            t3.tensor(pe)
            pq.tensor(pe)
            pkv.tensor(pe)
            t4.tensor(pe)
            a2.tensor(pe)
            t5.tensor(pe)
            o2.tensor(pe)
            m2.tensor(pe)
            n3.tensor(pe)
            pz.tensor(pe)
            forget_tensor(pe)
            t6.tensor(pe)
            a3.tensor(pe)
            t7.tensor(pe)
            o3.tensor(pe)
            n4.tensor(pe)
            mlp_tensor(pe)


INPUTS = ["x", "attn_norm", "ffn_norm", "diff_w_in", "diff_q_norm", "diff_k_norm", "diff_lambda_q1",
          "diff_lambda_k1", "diff_lambda_q2", "diff_lambda_k2", "diff_subln", "diff_w_out", "mla_w_a",
          "mla_q_a_norm", "mla_kv_a_norm", "mla_w_qb", "mla_w_kvb", "mla_q_norm", "mla_k_norm", "mla_w_out",
          "moe_w_group", "moe_b_group", "moe_w_expert", "moe_b_expert", "moe_w_gate", "moe_w_up", "moe_w_down",
          "c_2", "w_ada_2", "b_ada_2", "g_attn_2", "w_in_2", "b_f_2", "sinks_2", "w_out_2", "g_mlp_2", "w_up_2",
          "conv_w_2", "conv_b_2", "w_down_2", "g_final_2"]


def kernel(**inputs):
    import concourse.bacc as bacc
    from concourse.bass_utils import run_bass_kernel_spmd

    nc = bacc.Bacc("TRN2", target_bir_lowering=False, num_devices=1)
    arrays, tensors = {}, {}
    for name in INPUTS:
        a = np.ascontiguousarray(inputs[name])
        arrays["in_" + name] = a
        tensors[name] = nc.dram_tensor("in_" + name, a.shape, mybir.dt.from_np(a.dtype), kind="ExternalInput").ap()
    arrays["in_constants"] = shape_constants()
    tensors["constants"] = nc.dram_tensor("in_constants", arrays["in_constants"].shape, F32,
                                          kind="ExternalInput").ap()
    out = nc.dram_tensor("out_0", (1, S, D), F32, kind="ExternalOutput").ap()
    build(nc, tensors, out)
    r = run_bass_kernel_spmd(nc, [arrays], core_ids=[0])
    return r.results[0]["out_0"]
```

```python
import math
from contextlib import ExitStack

import numpy as np

import concourse.bass as bass
from concourse import mybir

ALU = mybir.AluOpType
ACT = mybir.ActivationFunctionType
F32 = mybir.dt.float32
I32 = mybir.dt.int32
AX = mybir.AxisListType.X

P = 128
S = 256
TT = S // P
D = 1024
DC = D // P
EPS = 1e-6
NEG = -1e30
NB = 512

RING = 12
UNIT = 2048

E = 64
GROUPS = 8
FF = 256
CAP = 64
SLOTS = 2 * S
TRASH = SLOTS + CAP
WIDE = TRASH + CAP
PER = 4
PASSES = S // CAP

HEADS = 8
ROT = 64
MLA_Q, MLA_KV, MLA_QK, NOPE = 384, 256, 192, 128
DFF = 2816
LAMBDA_INIT = 0.8 - 0.6 * math.exp(0.0)
WINDOW = 128
HYB_IN = 2312
SPAN = 3 * P

GATE_AT, UP_AT, DOWN_AT = (0, 1, 4, 5), (2, 3, 6, 7), (8, 9, 10, 11)


def shape_constants():
    pos = np.arange(S, dtype=np.float32)
    inv = (1.0 / (np.float32(10000.0) ** (np.arange(0, ROT, 2, dtype=np.float32) / np.float32(ROT)))).astype(np.float32)
    ang = pos[:, None] * inv[None, :]
    cos = np.concatenate([np.cos(ang), np.cos(ang)], 1)
    sin = np.concatenate([-np.sin(ang), np.sin(ang)], 1)
    rope = np.stack([cos, sin], 0).astype(np.float32)
    rope = rope.reshape(2, TT, P, ROT).transpose(2, 0, 1, 3).reshape(P, -1)
    q = np.arange(P)[:, None]
    k = np.arange(P)[None, :]
    tri = np.where(k <= q, 0.0, NEG)
    causal = np.concatenate([tri, np.zeros((P, P)), tri], 1)
    window = np.concatenate([tri, np.where(q + P - k < WINDOW, 0.0, NEG), tri], 1)
    dist = np.concatenate([q - k, q + P - k, q - k], 1)
    before = (np.arange(P)[:, None] < np.arange(P)[None, :]).astype(np.float32)
    upto = (np.arange(P)[:, None] <= np.arange(P)[None, :]).astype(np.float32)
    iota = np.tile(np.arange(SLOTS), (P, 1))
    parts = [np.eye(P), before, np.ones((P, P)), rope, causal, upto, window, dist, iota]
    return np.concatenate([p.astype(np.float32) for p in parts], 1)


KEPT = dict(ident=P, before=P, ones=P, rope=2 * TT * ROT, causal=SPAN)
LATER = dict(upto=P, window=SPAN, dist=SPAN, iota=SLOTS)


def build(nc, t, out):
    with ExitStack() as ctx:
        def sb(name, shape, dt=F32):
            return ctx.enter_context(nc.sbuf_tensor(name, shape, dt))

        class Signal:

            def __init__(self, handle, base=0):
                self.sem, self.base = handle, base

            def __call__(self, n):
                return self.sem, n + self.base

        def sem(name):
            return Signal(ctx.enter_context(nc.semaphore(name)))

        counted_up = {}

        def shared(kind, total):
            if kind not in counted_up:
                counted_up[kind] = [ctx.enter_context(nc.semaphore(kind)), 0]
            signal = Signal(*counted_up[kind])
            counted_up[kind][1] += total
            return signal

        X = sb("X", [P, TT, D])
        hn = sb("hn", [P, TT, D])
        hT = sb("hT", [P, DC, S])
        ring = sb("ring", [P, RING, UNIT])
        A = sb("A", [P, 8192])
        BC = sb("BC", [P, 10240])
        konst = sb("konst", [P, sum(KEPT.values())])
        pT = sb("pT", [P, 2, SPAN])
        stat = sb("stat", [P, 512])
        at = {}
        offset = 0
        for name, width in KEPT.items():
            at[name] = konst[:, offset:offset + width]
            offset += width
        ident, ones, before = at["ident"], at["ones"], at["before"]
        later = {}
        for name, width in LATER.items():
            later[name] = t["constants"][:, offset:offset + width]
            offset += width
        rope_tab = at["rope"].rearrange("p (a t d) -> p a t d", a=2, t=TT)

        gains = sb("gains", [P, 2, 2, DC])
        gains2 = sb("gains2", [P, 2, DC])
        small = sb("small", [P, 64])
        subln, mla_gain = small[:, 0:1], small[:, 1:8]
        ccol, csig = small[:, 8:16], small[:, 16:24]
        sinks = small[:, 24:32]
        f_bias = small[:, 32:40]
        lam = small[:, 40:44]
        cond_c = small[:, 44:52]
        router_w = A[:, 4608:4608 + DC * 72].rearrange("p (c n) -> p c n", c=DC)
        iota = A[:, 2560:2560 + SLOTS]
        router_b = sb("router_b", [P, 2, 72])
        qk_gain = sb("qk_gain", [P, 2, 192])
        gtab = sb("gtab", [P, 2, 2, TT, ROT])
        modc = sb("modc", [P, 4, DC])
        eb = pT[:, :, :].rearrange("p a s -> p (a s)")[:, 0:2 * FF].rearrange("p (b n) -> p b n", b=2)
        modrow = sb("modrow", [P, NB])
        pos_i = A[:, 7168:7168 + (PASSES + 1) * E].bitcast(I32)
        half = sb("half", [P, 16])

        bank = [ctx.enter_context(nc.psum_tensor(f"bank{i}", [P, NB], F32)) for i in range(8)]
        mod_dram = nc.dram_tensor("mod_scratch", (6 * D,), F32, kind="Internal").ap()

        loaded = sem("loaded")
        unit_full = [sem(f"unit_full{i}") for i in range(RING)]
        unit_done = sem("unit_done")
        dve_step, act_step, pool_step = sem("dve_step"), sem("act_step"), sem("pool_step")

        class Steps:

            def __init__(self, signal):
                self.count_sem, self.n, self.eng = signal, 0, None

            def done(self, ins):
                self.n += 1
                ins.then_inc(self.count_sem.sem, 1)
                self.eng.wait_ge(*self.count_sem(self.n))

        dv, ac, po = Steps(dve_step), Steps(act_step), Steps(pool_step)

        units = []

        def plan(view, src):
            units.append((view, src))
            return len(units) - 1

        def slot(u):
            return ring[:, u % RING, :]

        def load_unit(sp, u):
            if u >= RING:
                sp.wait_ge(*unit_done(u - RING + 1))
            view, src = units[u]
            sp.dma_start(view(slot(u)), src).then_inc(unit_full[u % RING].sem, 16)

        def unit_here(pe, u):
            pe.wait_ge(*unit_full[u % RING](16 * (u // RING + 1)))

        class Stage:
            tensor = vector = scalar = gpsimd = sync = staticmethod(lambda eng: None)

        def norm_stage(name, before_stage, gain, shift=None, extra=()):
            st = Stage()
            squares, rooted, scaled = shared("norm_squares", TT), shared("norm_rooted", 1), shared("norm_scaled", TT)
            turned, out_v, out_a = shared("norm_turned", 4), shared("norm_out_v", 4), shared("norm_out_a", 4)
            ssq, rstd = stat[:, 0:TT], stat[:, 2:2 + TT]

            def scalar(act):
                before_stage(act)
                for tt in range(TT):
                    nc.scalar.activation(hT[:, :, :].rearrange("p c s -> p (c s)")[:, tt * D:(tt + 1) * D], X[:, tt, :],
                                         ACT.Square, accum_out=ssq[:, tt:tt + 1]).then_inc(squares.sem, 1)
                for s, v in extra:
                    act.wait_ge(*s(v))
                for f in (1, 3):
                    act.wait_ge(*turned(f + 1))
                    for k in range(2):
                        c = 2 * f + k
                        b = shift[:, c:c + 1] if shift is not None else 0.0
                        nc.scalar.activation(hT[:, c, :], bank[4 + f % 2][:, k * S:(k + 1) * S], ACT.Identity,
                                             scale=gain[:, c:c + 1], bias=b).then_inc(out_a.sem, 1)

            def gpsimd(pool):
                pool.wait_ge(*squares(TT))
                po.done(nc.gpsimd.tensor_scalar(rstd, ssq, 1.0 / D, EPS, ALU.mult, ALU.add))
                nc.gpsimd.tensor_tensor(rstd, rstd, half[:, 0:TT], ALU.pow).then_inc(rooted.sem, 1)

            def vector(dve):
                before_stage(dve)
                dve.wait_ge(*rooted(1))
                for tt in range(TT):
                    nc.vector.tensor_scalar(hn[:, tt, :], X[:, tt, :], rstd[:, tt:tt + 1], None,
                                            ALU.mult).then_inc(scaled.sem, 1)
                dve.wait_ge(*squares(TT))
                for s, v in extra:
                    dve.wait_ge(*s(v))
                for f in (0, 2):
                    dve.wait_ge(*turned(f + 1))
                    for k in range(2):
                        c = 2 * f + k
                        if shift is None:
                            i = nc.vector.tensor_scalar(hT[:, c, :], bank[4][:, k * S:(k + 1) * S],
                                                        gain[:, c:c + 1], None, ALU.mult)
                        else:
                            i = nc.vector.tensor_scalar(hT[:, c, :], bank[4][:, k * S:(k + 1) * S],
                                                        gain[:, c:c + 1], shift[:, c:c + 1], ALU.mult, ALU.add)
                        i.then_inc(out_v.sem, 1)

            def tensor(pe):
                pe.wait_ge(*scaled(TT))
                for f in range(4):
                    if f == 2:
                        pe.wait_ge(*out_v(2))
                    if f == 3:
                        pe.wait_ge(*out_a(2))
                    for k in range(2):
                        for tt in range(TT):
                            i = nc.tensor.transpose(bank[4 + f % 2][:, k * S + tt * P:k * S + (tt + 1) * P],
                                                    hn[:, tt, 2 * f + k:D:DC], ident)
                    i.then_inc(turned.sem, 1)

            def ready(eng):
                eng.wait_ge(*out_v(4))
                eng.wait_ge(*out_a(4))
            st.scalar, st.gpsimd, st.vector, st.tensor, st.ready = scalar, gpsimd, vector, tensor, ready
            return st

        def project_stage(name, ready, lhs, blocks, evac, fold=None, sbanks=(0, 1, 2, 3), first_free=None):
            st = Stage()
            copied = shared("product_copied", TT * len(blocks))

            def ps(n, tt):
                return bank[sbanks[2 * (n % 2) + tt]]

            def last_unit(n):
                return blocks[n][1][-1][0]

            def tensor(pe):
                ready(pe)
                if first_free:
                    first_free(pe)
                for n, (w, parts) in enumerate(blocks):
                    if n >= 2:
                        pe.wait_ge(*copied(2 * (n - 1)))
                    total = sum(p[2] for p in parts)
                    seen = 0
                    for u, view, cn, keep in parts:
                        unit_here(pe, u)
                        for tt in range(TT):
                            for c in range(cn):
                                i = nc.tensor.matmul(ps(n, tt)[:, 0:w], lhs(seen + c, tt), view(slot(u))[:, c, :],
                                                     start=(seen + c == 0), stop=(seen + c == total - 1))
                        seen += cn
                        i.then_inc((unit_done if not keep else kept[0]).sem, 1)

            kept = [sem(name + "_kept")] if any(p[3] for b in blocks for p in b[1]) else [None]
            kept_of = {}
            count = 0
            for n, (w, parts) in enumerate(blocks):
                if parts[-1][3]:
                    count += 1
                    kept_of[n] = count

            def block_ready(eng, n):
                if n in kept_of:
                    eng.wait_ge(*kept[0](kept_of[n]))
                else:
                    eng.wait_ge(*unit_done(last_unit(n) + 1))

            def drain(eng):
                for n, (w, parts) in enumerate(blocks):
                    block_ready(eng, n)
                    for tt in range(TT):
                        evac(eng, n, tt, ps(n, tt)[:, 0:w]).then_inc(copied.sem, 1)
                    if fold:
                        fold(eng, n)
            st.tensor, st.drain, st.copied = tensor, drain, copied
            return st

        def square_units(w, ncols, order="(p c)", kc=DC, per=4, col0=0):
            src = w.rearrange("(p c) n -> p c n", c=kc) if order == "(p c)" else w.rearrange("(c p) n -> p c n", p=P)
            blocks = []
            for n0 in range(0, ncols, NB):
                wd = min(NB, ncols - n0)
                parts = []
                for c0 in range(0, kc, per):
                    cn = min(per, kc - c0)

                    def view(a, wd=wd, cn=cn):
                        return a[:, 0:cn * wd].rearrange("p (c n) -> p c n", c=cn)
                    u = plan(view, src[:, c0:c0 + cn, col0 + n0:col0 + n0 + wd])
                    parts.append((u, view, cn, False))
                blocks.append((wd, parts))
            return blocks

        def loads(first, last):
            def sync(sp):
                for u in range(first, last):
                    load_unit(sp, u)
            return sync

        def turn_stage(name, ready, jobs, scalar_only=False, fill_ready=None, bank0=4):
            st = Stage()
            fills = [jobs[i:i + 2] for i in range(0, len(jobs), 2)]
            by_scalar = [scalar_only or f % 2 == 1 for f in range(len(fills))]
            turned, out_v, out_a = (shared("turn_done", len(fills)), shared("turn_out_v", by_scalar.count(False)),
                                    shared("turn_out_a", by_scalar.count(True)))

            def left(eng, f):
                (eng.wait_ge(*(out_a if by_scalar[f] else out_v)(by_scalar[0:f + 1].count(by_scalar[f]))))

            def tensor(pe):
                ready(pe)
                for f, fill in enumerate(fills):
                    if f >= 2:
                        left(pe, f - 2)
                    if fill_ready:
                        fill_ready(pe, f)
                    for k, (src, w, dst, scale) in enumerate(fill):
                        for tt in range(TT):
                            i = nc.tensor.transpose(bank[bank0 + f % 2][0:w, k * S + tt * P:k * S + (tt + 1) * P],
                                                    src(tt), ident)
                    i.then_inc(turned.sem, 1)

            def evac(eng, scalar):
                for f, fill in enumerate(fills):
                    if by_scalar[f] != scalar:
                        continue
                    eng.wait_ge(*turned(f + 1))
                    for k, (src, w, dst, scale) in enumerate(fill):
                        ps = bank[bank0 + f % 2][0:w, k * S:(k + 1) * S]
                        if scalar and scale is not None:
                            i = nc.scalar.activation(dst, ps, ACT.Identity, scale=scale)
                        elif scalar:
                            i = nc.scalar.activation(dst, ps, ACT.Copy)
                        elif scale is not None:
                            i = nc.vector.tensor_scalar(dst, ps, scale, None, ALU.mult)
                        else:
                            i = nc.vector.tensor_copy(dst, ps)
                    i.then_inc((out_a if scalar else out_v).sem, 1)

            def vector(dve):
                evac(dve, False)

            def scalar(act):
                evac(act, True)

            def done(eng):
                eng.wait_ge(*out_v(by_scalar.count(False)))
                eng.wait_ge(*out_a(by_scalar.count(True)))
            st.tensor, st.vector, st.scalar, st.ready = tensor, vector, scalar, done
            return st

        SC = BC[:, 8192:8192 + 4 * SPAN].rearrange("p (b m s) -> p b m s", b=2, m=2)

        def attention_stage(name, ready, heads, scale, dv_w, bias, filler=None, mix=None, sink=False, squares=None):
            st = Stage()
            n = len(heads)
            maps = len(heads[0][0])
            scored, masked, maxed = (shared("head_scored", maps * n), shared("head_masked", maps * n),
                                     shared("head_maxed", n))
            exped, mixed, turned = (shared("head_exped", n), shared("head_mixed", n if mix else 0),
                                    shared("head_turned", n))
            copied, summed, stored = shared("head_copied", n), shared("head_summed", n), shared("head_stored", n)
            sink_heads = heads if sink is True else []
            nmax = stat[:, 16:24].rearrange("p (b m t) -> p b m t", b=2, m=2)
            den = stat[:, 24:32].rearrange("p (b m t) -> p b m t", b=2, m=2)
            rden = stat[:, 32:40].rearrange("p (b m t) -> p b m t", b=2, m=2)
            dsink = stat[:, 40:44].rearrange("p (b t) -> p b t", b=2)
            obanks = 1 if mix else 2

            def obank(h):
                b = bank[6] if mix else bank[1 + 2 * (h % 2)]
                return b[:, 0:S].rearrange("p (t d) -> p t d", t=TT)
            ranges = [(0, P), (P, SPAN)]

            def tensor(pe):
                ready(pe)

                def score(h):
                    if h >= 2:
                        pe.wait_ge(*masked(maps * (h - 1)))
                    for m in range(maps):
                        ps = bank[(h % 2) * 2 + m]
                        pairs = heads[h][0][m]
                        for tt, (a, b) in enumerate(ranges):
                            for j, (q, k) in enumerate(pairs):
                                i = nc.tensor.matmul(ps[:, a:b], q(tt), k(0, b - a), start=(j == 0),
                                                     stop=(j == len(pairs) - 1))
                        i.then_inc(scored.sem, 1)

                def turn(h):
                    pe.wait_ge(*(mixed if mix else exped)(h + 1))
                    if h >= 2:
                        pe.wait_ge(*copied(h - 1))
                    for j in range(3):
                        i = nc.tensor.transpose(bank[4 + h % 2][:, j * P:(j + 1) * P],
                                                SC[:, h % 2, 0, j * P:(j + 1) * P], ident)
                    i.then_inc(turned.sem, 1)

                def sum_v(h):
                    pe.wait_ge(*copied(h + 1))
                    if h >= obanks:
                        pe.wait_ge(*stored(h - obanks + 1))
                    ps = obank(h)
                    v = heads[h][1]
                    p = pT[:, h % 2, :]
                    nc.tensor.matmul(ps[:, 0, 0:dv_w], p[:, 0:P], v(0), start=True, stop=True)
                    nc.tensor.matmul(ps[:, 1, 0:dv_w], p[:, P:2 * P], v(0), start=True, stop=False)
                    nc.tensor.matmul(ps[:, 1, 0:dv_w], p[:, 2 * P:SPAN], v(1), start=False,
                                     stop=True).then_inc(summed.sem, 1)
                score(0)
                for h in range(n + 1):
                    if h + 1 < n:
                        score(h + 1)
                    if filler and h < n:
                        filler.tensor(pe, h)
                    if h < n:
                        turn(h)
                    if h >= 1:
                        sum_v(h - 1)

            def vector(dve):
                def mask(h):
                    if h >= 2:
                        dve.wait_ge(*turned(h - 1))
                    for m in range(maps):
                        ps = bank[(h % 2) * 2 + m][:, 0:SPAN]
                        b = bias(h)
                        dve.wait_ge(*scored(maps * h + m + 1))
                        nc.vector.scalar_tensor_tensor(out=SC[:, h % 2, m, :], in0=ps, scalar=scale, in1=b,
                                                       op0=ALU.mult, op1=ALU.add).then_inc(masked.sem, 1)
                    dve.wait_ge(*masked(maps * (h + 1)))
                    for m in range(maps):
                        for tt, (a, b) in enumerate(ranges):
                            i = nc.vector.tensor_reduce(nmax[:, h % 2, m, tt:tt + 1], SC[:, h % 2, m, a:b], AX,
                                                        ALU.max, negate=True)
                    if sink and h < HEADS:
                        dv.done(i)
                        i = nc.vector.tensor_scalar(nmax[:, h % 2, 0, :], nmax[:, h % 2, 0, :], nsink[:, h:h + 1],
                                                    None, ALU.min)
                    i.then_inc(maxed.sem, 1)

                def weigh(h):
                    dve.wait_ge(*exped(h + 1))
                    if sink and h < HEADS:
                        dv.done(nc.vector.tensor_tensor(den[:, h % 2, 0, :], den[:, h % 2, 0, :], dsink[:, h % 2, :],
                                                        ALU.add))
                    if h >= 2:
                        dve.wait_ge(*stored(h - 1))
                    dv.done(nc.vector.reciprocal(rden[:, h % 2, 0:maps, :], den[:, h % 2, 0:maps, :]))
                    if mix:
                        dv.done(nc.vector.tensor_scalar(rden[:, h % 2, 1, :], rden[:, h % 2, 1, :], lam[:, 3:4], None,
                                                        ALU.mult))
                        for tt, (a, b) in enumerate(ranges):
                            dv.done(nc.vector.tensor_scalar(SC[:, h % 2, 0, a:b], SC[:, h % 2, 0, a:b],
                                                            rden[:, h % 2, 0, tt:tt + 1], None, ALU.mult))
                            i = nc.vector.scalar_tensor_tensor(out=SC[:, h % 2, 0, a:b], in0=SC[:, h % 2, 1, a:b],
                                                               scalar=rden[:, h % 2, 1, tt:tt + 1],
                                                               in1=SC[:, h % 2, 0, a:b], op0=ALU.mult, op1=ALU.add)
                            if tt == 0:
                                dv.done(i)
                        i.then_inc(mixed.sem, 1)

                def store(h):
                    dve.wait_ge(*summed(h + 1))
                    ps = obank(h)
                    for tt in range(TT):
                        if mix:
                            i = nc.vector.tensor_copy(heads[h][2](tt), ps[:, tt, 0:dv_w])
                        else:
                            i = nc.vector.tensor_scalar(heads[h][2](tt), ps[:, tt, 0:dv_w],
                                                        rden[:, h % 2, 0, tt:tt + 1], None, ALU.mult)
                    i.then_inc(stored.sem, 1)
                mask(0)
                for h in range(n + 1):
                    if h + 1 < n:
                        mask(h + 1)
                    if h < n:
                        weigh(h)
                    if h >= 1:
                        store(h - 1)

            def scalar(act):
                def exps(h):
                    act.wait_ge(*maxed(h + 1))
                    for m in range(maps):
                        for tt, (a, b) in enumerate(ranges):
                            i = nc.scalar.activation(SC[:, h % 2, m, a:b], SC[:, h % 2, m, a:b], ACT.Exp,
                                                     bias=nmax[:, h % 2, m, tt:tt + 1],
                                                     accum_out=den[:, h % 2, m, tt:tt + 1])
                    if sink and h < HEADS:
                        for tt in range(TT):
                            i = nc.scalar.activation(dsink[:, h % 2, tt:tt + 1], sinks[:, h:h + 1], ACT.Exp,
                                                     bias=nmax[:, h % 2, 0, tt:tt + 1])
                    i.then_inc(exped.sem, 1)

                def copy(h):
                    act.wait_ge(*turned(h + 1))
                    if h >= 2:
                        act.wait_ge(*summed(h - 1))
                    nc.scalar.activation(pT[:, h % 2, :], bank[4 + h % 2][:, 0:SPAN], ACT.Copy).then_inc(copied.sem, 1)
                exps(0)
                for h in range(n):
                    if h + 1 < n:
                        exps(h + 1)
                    if filler:
                        filler.scalar(act, h)
                    copy(h)
                    if squares and h >= 1:
                        act.wait_ge(*stored(h))
                        squares(act, h - 1)
                if squares:
                    act.wait_ge(*stored(n))
                    squares(act, n - 1)

            def done(eng):
                eng.wait_ge(*stored(n))
            st.tensor, st.vector, st.scalar, st.ready = tensor, vector, scalar, done
            return st

        order = []

        n_loaded = [0]

        def start_sync(sp):
            def ld(dst, src, signal=loaded):
                sp.dma_start(dst, src).then_inc(signal.sem, 16)
                if signal is loaded:
                    n_loaded[0] += 16
            x = t["x"][0].rearrange("(t p) d -> p t d", p=P)
            for tt in range(TT):
                ld(X[:, tt, :], x[:, tt, :], first)
            ld(ident, t["constants"][:, 0:P], first)
            ld(gains[:, 0, :, :], t["attn_norm"].rearrange("l (p c) -> p l c", c=DC), first)
            ld(gains[:, 1, :, :], t["ffn_norm"].rearrange("l (p c) -> p l c", c=DC), first)
            for u in range(4):
                load_unit(sp, u)
            ld(konst[:, P:], t["constants"][:, P:sum(KEPT.values())])
            ld(BC[:, 384:384 + ROT], t["diff_q_norm"][0].partition_broadcast(P))
            ld(BC[:, 448:448 + ROT], t["diff_k_norm"][0].partition_broadcast(P))
            for k, name in enumerate(("q1", "k1", "q2", "k2")):
                ld(BC[:, k * ROT:(k + 1) * ROT], t["diff_lambda_" + name][0].partition_broadcast(P))
            ld(ccol, t["c_2"].rearrange("a (p c) -> p (a c)", c=DC))
            ld(subln, t["diff_subln"].rearrange("a p -> p a"))
            ld(sinks, t["sinks_2"].partition_broadcast(P))
            ld(qk_gain[:, 0, :], t["mla_q_norm"][0].partition_broadcast(P))
            ld(qk_gain[:, 1, :], t["mla_k_norm"][0].partition_broadcast(P))
            ld(mla_gain[:, 0:3], t["mla_q_a_norm"].rearrange("a (p c) -> p (a c)", c=3))
            ld(mla_gain[:, 3:5], t["mla_kv_a_norm"].rearrange("a (p c) -> p (a c)", c=2))
            ld(mla_gain[:, 5:6], t["mla_q_norm"][0:1, 0:NOPE].rearrange("a p -> p a"))
            ld(mla_gain[:, 6:7], t["mla_k_norm"][0:1, 0:NOPE].rearrange("a p -> p a"))
            for layer in range(2):
                ld(router_b[:, layer, 0:GROUPS], t["moe_b_group"][layer].partition_broadcast(P))
                ld(router_b[:, layer, GROUPS:], t["moe_b_expert"][layer].partition_broadcast(P))
            ld(gains2[:, 0, :], t["g_attn_2"].rearrange("(p c) -> p c", c=DC))
            ld(gains2[:, 1, :], t["g_mlp_2"].rearrange("(p c) -> p c", c=DC))
            ld(f_bias, t["b_f_2"].partition_broadcast(P))
            assert n_loaded[0] == N_SMALL

        N_SMALL = 16 * 23
        N_FIRST = 16 * 5
        first = sem("first")

        def have_first(eng):
            eng.wait_ge(*first(N_FIRST))

        u0 = len(units)
        w_in = t["diff_w_in"][0]
        in_blocks = square_units(w_in, 3072)
        u1 = len(units)
        set_up = sem("set_up")
        lam_exp = sem("lam_exp")
        lam_dot = sem("lam_dot")

        def have_small(eng):
            eng.wait_ge(*loaded(N_SMALL))

        norm1_free = have_first
        n1 = norm_stage("n1", norm1_free, gains[:, 0, 0, :])
        qkv = A[:, 0:TT * 3072].rearrange("p (t n) -> p t n", t=TT)

        def setup_vector(dve):
            have_small(dve)
            l = BC[:, 0:4 * ROT].rearrange("p (k d) -> p k d", k=4)
            pr = BC[:, 4 * ROT:6 * ROT].rearrange("p (k d) -> p k d", k=2)
            for k in range(2):
                dv.done(nc.vector.tensor_tensor(pr[:, k, :], l[:, 2 * k, :], l[:, 2 * k + 1, :], ALU.mult))
            nc.vector.tensor_reduce(lam[:, 0:2], pr, AX, ALU.add).then_inc(lam_dot.sem, 1)
            fold_rope(0)
            dve.wait_ge(*lam_exp(2))
            dv.done(nc.vector.tensor_tensor(lam[:, 2:3], lam[:, 1:2], lam[:, 0:1], ALU.subtract))
            dv.done(nc.vector.tensor_scalar(lam[:, 3:4], lam[:, 2:3], -LAMBDA_INIT, None, ALU.add))
            dv.done(nc.vector.tensor_scalar(csig, csig, 1.0, None, ALU.add))
            dv.done(nc.vector.reciprocal(csig, csig))
            dv.done(nc.vector.tensor_scalar(subln, subln, 1.0 - LAMBDA_INIT, None, ALU.mult))
            dv.done(nc.vector.tensor_scalar(nsink, sinks, -1.0, None, ALU.mult))
            nc.vector.tensor_tensor(cond_c, ccol, csig, ALU.mult).then_inc(set_up.sem, 1)

        nsink = stat[:, 48:56]

        def fold_rope(which):
            for qk in range(2):
                g = BC[:, 384 + 64 * qk:448 + 64 * qk] if which == 0 else qk_gain[:, qk, NOPE:MLA_QK]
                for tt in range(TT):
                    dv.done(nc.vector.tensor_tensor(gtab[:, qk, 0, tt, :], rope_tab[:, 0, tt, :], g, ALU.mult))
                    dv.done(nc.vector.tensor_tensor(gtab[:, qk, 1, tt, 0:32], rope_tab[:, 1, tt, 0:32], g[:, 32:64],
                                                    ALU.mult))
                    dv.done(nc.vector.tensor_tensor(gtab[:, qk, 1, tt, 32:64], rope_tab[:, 1, tt, 32:64], g[:, 0:32],
                                                    ALU.mult))

        def setup_scalar(act):
            have_small(act)
            act.wait_ge(*lam_dot(1))
            nc.scalar.activation(lam[:, 0:2], lam[:, 0:2], ACT.Exp).then_inc(lam_exp.sem, 1)
            nc.scalar.activation(csig, ccol, ACT.Exp, scale=-1.0).then_inc(lam_exp.sem, 1)

        def copy_qkv(eng, n, tt, ps):
            return nc.scalar.activation(qkv[:, tt, n * NB:(n + 1) * NB], ps, ACT.Copy)

        p1_sq, p1_ss, p1_rs = sem("p1_sq"), sem("p1_ss"), sem("p1_rs")
        p1_used = sem("p1_used")
        sq1 = hn[:, 0, :].rearrange("p (b n) -> p b n", b=2)
        rot1 = hn[:, 1, :].rearrange("p (b n) -> p b n", b=2)

        def square_qk(act, n):
            if n >= 4:
                return
            for tt in range(TT):
                j = 2 * n + tt
                act.wait_ge(*p1.copied(j + 1))
                if j >= 2:
                    act.wait_ge(*p1_ss(j - 1))
                nc.scalar.activation(sq1[:, j % 2, :], qkv[:, tt, n * NB:(n + 1) * NB], ACT.Square).then_inc(p1_sq.sem, 1)

        p1 = project_stage("p1", n1.ready, lambda c, tt: hT[:, c, tt * P:(tt + 1) * P], in_blocks, copy_qkv,
                           square_qk)

        def rotate(dve, x, g, w, n_groups, qk, tt, t1, t2):
            cs = gtab[:, qk, 0, tt, :].unsqueeze(1).broadcast_to([P, n_groups, ROT])
            sn0 = gtab[:, qk, 1, tt, 0:32].unsqueeze(1).broadcast_to([P, n_groups, 32])
            sn1 = gtab[:, qk, 1, tt, 32:64].unsqueeze(1).broadcast_to([P, n_groups, 32])
            nc.vector.tensor_tensor(t1, x, cs, ALU.mult)
            nc.vector.tensor_tensor(t2[:, :, 0:32], x[:, :, 32:64], sn0, ALU.mult)
            dv.done(nc.vector.tensor_tensor(t2[:, :, 32:64], x[:, :, 0:32], sn1, ALU.mult))
            dv.done(nc.vector.tensor_tensor(t1, t1, t2, ALU.add))

        p1_qk = sem("p1_qk")

        def rope_vector(dve):
            for n in range(4):
                for tt in range(TT):
                    j = 2 * n + tt
                    x = qkv[:, tt, n * NB:(n + 1) * NB].rearrange("p (g d) -> p g d", d=ROT)
                    dve.wait_ge(*p1_sq(j + 1))
                    nc.vector.tensor_reduce(stat[:, 64 + 8 * (j % 2):72 + 8 * (j % 2)],
                                            sq1[:, j % 2, :].rearrange("p (g d) -> p g d", d=ROT), AX,
                                            ALU.add).then_inc(p1_ss.sem, 1)
                    t1 = rot1[:, 0, :].rearrange("p (g d) -> p g d", d=ROT)
                    t2 = rot1[:, 1, :].rearrange("p (g d) -> p g d", d=ROT)
                    rotate(dve, x, None, ROT, 8, n // 2, tt, t1, t2)
                    dve.wait_ge(*p1_rs(j + 1))
                    r = stat[:, 80 + 8 * (j % 2):88 + 8 * (j % 2)].unsqueeze(2).broadcast_to([P, 8, ROT])
                    dv.done(nc.vector.tensor_tensor(x, t1, r, ALU.mult))
            nc.vector.tensor_copy(stat[:, 8:9], stat[:, 64:65]).then_inc(p1_qk.sem, 1)

        def rope_gpsimd(pool):
            for j in range(8):
                pool.wait_ge(*p1_ss(j + 1))
                a, b = 64 + 8 * (j % 2), 80 + 8 * (j % 2)
                po.done(nc.gpsimd.tensor_scalar(stat[:, 96:104], stat[:, a:a + 8], 1.0 / ROT, EPS, ALU.mult, ALU.add))
                nc.gpsimd.tensor_tensor(stat[:, b:b + 8], stat[:, 96:104], half[:, 0:8], ALU.pow).then_inc(p1_rs.sem, 1)

        qkT = BC[:, 0:8192].rearrange("p (j s) -> p j s", s=S)
        jobs = []
        for h in range(HEADS):
            for qk in range(2):
                jobs.append((lambda tt, c0=qk * D + h * P: qkv[:, tt, c0:c0 + P], P, qkT[:, 2 * h + qk, :], None))

        def t1_ready(pe):
            pe.wait_ge(*p1_qk(1))
        t1 = turn_stage("t1", t1_ready, jobs)

        class Conditioning:

            def __init__(self, g0, g1, heads):
                w = t["w_ada_2"].rearrange("(p c) n -> p c n", c=DC)
                total = g1 - g0
                self.jobs = [[] for _ in range(heads)]
                self.copied = shared("mod_copied", total)
                self.stored = shared("mod_stored", 16 * total)
                self.total, self.g0 = total, g0
                for k in range(total * DC):
                    g, c = g0 + k // DC, k % DC
                    u = plan(lambda a: a, w[:, c, g * UNIT:(g + 1) * UNIT])
                    self.jobs[k * heads // (total * DC)].append((g, c, u))

            def tensor(self, pe, h):
                for g, c, u in self.jobs[h]:
                    if c == 0 and g > self.g0:
                        pe.wait_ge(*self.copied(g - self.g0))
                    unit_here(pe, u)
                    for q in range(4):
                        i = nc.tensor.matmul(bank[7][32 * q:32 * q + 32, :], cond_c[:, c:c + 1].broadcast_to([P, 32]),
                                             slot(u)[:, q * NB:(q + 1) * NB], start=(c == 0), stop=(c == DC - 1))
                    i.then_inc(unit_done.sem, 1)

            def scalar(self, act, h):
                for g, c, u in self.jobs[h]:
                    if c < DC - 1:
                        continue
                    j = g - self.g0
                    act.wait_ge(*unit_done(u + 1))
                    if g > 0:
                        act.wait_ge(*self.stored(16 * j))
                    nc.scalar.activation(modrow[:, :], bank[7][:, :], ACT.Copy).then_inc(self.copied.sem, 1)
                    act.wait_ge(*self.copied(j + 1))
                    act.dma_start(mod_dram[g * UNIT:(g + 1) * UNIT].rearrange("(q n) -> q n", q=4),
                                  modrow[0:P:32, :]).then_inc(self.stored.sem, 16)

            def ready(self, eng):
                eng.wait_ge(*self.stored(16 * self.total))

        cond1 = Conditioning(0, 2, HEADS)
        u2 = len(units)

        def diff_head(h):
            def part(m):
                a, b = m * ROT, (m + 1) * ROT
                return [(lambda tt: qkT[a:b, 2 * h, tt * P:(tt + 1) * P], lambda k0, k1: qkT[a:b, 2 * h + 1, k0:k1])]
            return ([part(0), part(1)], lambda kt: qkv[:, kt, 2 * D + h * P:2 * D + (h + 1) * P],
                    lambda tt: hn[:, tt, h * P:(h + 1) * P])

        n_sq, n_rs, n_out = sem("sub_sq"), sem("sub_rs"), sem("sub_out")
        sub_sq = BC[:, 9728:9728 + TT * P].rearrange("p (t d) -> p t d", t=TT)

        def a1_ready(pe):
            t1.ready(pe)
            pe.wait_ge(*set_up(1))
            pe.wait_ge(*p1.copied(12))
        def sub_squares(act, h):
            if h:
                act.wait_ge(*n_sq(h))
            for tt in range(TT):
                i = nc.scalar.activation(sub_sq[:, tt, :], hn[:, tt, h * P:(h + 1) * P], ACT.Square,
                                         accum_out=stat[:, 64 + 8 * tt + h:65 + 8 * tt + h])
            i.then_inc(n_sq.sem, 1)
        a1 = attention_stage("a1", a1_ready, [diff_head(h) for h in range(HEADS)], ROT ** -0.5, P,
                             lambda h: at["causal"], filler=cond1, mix=True, squares=sub_squares)

        def sub_vector(dve):
            dve.wait_ge(*n_rs(1))
            o = hn[:, :, :].rearrange("p t (h d) -> p t h d", d=P)
            r = stat[:, 80:96].rearrange("p (t h) -> p t h", t=TT)
            for h in range(0, HEADS, 2):
                nc.vector.tensor_tensor(o[:, :, h:h + 2, :], o[:, :, h:h + 2, :],
                                        r[:, :, h:h + 2].unsqueeze(3).broadcast_to([P, TT, 2, P]),
                                        ALU.mult).then_inc(n_out.sem, 1)

        def sub_gpsimd(pool):
            pool.wait_ge(*n_sq(HEADS))
            po.done(nc.gpsimd.tensor_scalar(stat[:, 64:80], stat[:, 64:80], 1.0 / P, EPS, ALU.mult, ALU.add))
            nc.gpsimd.tensor_tensor(stat[:, 80:96], stat[:, 64:80], half[:, 0:16], ALU.pow).then_inc(n_rs.sem, 1)

        def heads_turned(name, ready, scale=None, fill_ready=None):
            return turn_stage(name, ready, [(lambda tt, c=c: hn[:, tt, c * P:(c + 1) * P], P, hT[:, c, :], scale)
                                            for c in range(DC)], fill_ready=fill_ready)
        t2 = heads_turned("t2", a1.ready, subln, lambda pe, f: pe.wait_ge(*n_out(f + 1)))

        def add_x(eng, n, tt, ps):
            xs = X[:, tt, n * NB:(n + 1) * NB]
            return nc.vector.tensor_tensor(xs, xs, ps, ALU.add)

        def hT_lhs(c, tt):
            return hT[:, c, tt * P:(tt + 1) * P]
        out1 = square_units(t["diff_w_out"][0], D, order="(c p)")
        o1 = project_stage("o1", t2.ready, hT_lhs, out1, add_x)

        def o1_done(eng):
            eng.wait_ge(*o1.copied(4))

        def moe(layer, name, x_ready, x_free):
            st = Stage()
            pairs = E // 2
            nrm = norm_stage(name + "_n", x_ready, gains[:, 1, layer, :])
            table_in, logits, gexp, gexp_in = (shared("table_in", 48), shared("logits", 1), shared("gexp", 2),
                                               shared("gexp_in", 1))
            picked, counted, placed, gathered = (shared("picked", 1), shared("counted", 1), shared("placed", 1),
                                                 shared("gathered", DC))
            positioned = shared("positioned", 1)
            gather_banks = (0, 1, 2, 3, 6, 7)
            spread, spread_a = shared("spread_v", DC // 2), shared("spread_a", DC // 2)
            cwt_ready, cw_turned, cw_ready = shared("cwt_ready", 1), shared("cw_turned", 1), shared("cw_ready", 1)
            exped, hid_ready, h_turned = (shared("gate_exped", pairs), shared("hid_ready", pairs),
                                          shared("hid_turned", pairs))
            x_ready_, hT_ready = shared("tokens_ready", pairs + 2), shared("hidT_ready", pairs)
            rows_v, rows_a, rows_turned = shared("rows_v", pairs), shared("rows_a", pairs), shared("rows_turned", pairs)
            first_stored, pair_stored = shared("first_stored", pairs), shared("pair_stored", pairs + 1)
            y_turned, y_out_v, y_out_a = shared("y_turned", 8), shared("y_out_v", 4), shared("y_out_a", 4)
            summed, added, vstep = shared("moe_summed", 4), shared("moe_added", 4), shared("hidden_step", 3 * pairs)
            f_full, f_up, f_exp, f_hid = sem(name + "_f_full"), sem(name + "_f_up"), sem(name + "_f_exp"), sem(name + "_f_hid")
            f_down, f_stored, f_v = sem(name + "_f_down"), sem(name + "_f_stored"), sem(name + "_f_v")
            f_x, f_turned, f_hT = sem(name + "_f_x"), sem(name + "_f_turned"), sem(name + "_f_hT")
            f_rows, f_rturned = sem(name + "_f_rows"), sem(name + "_f_rturned")

            gate_w, up_w, down_w = (t["moe_w_gate"][layer], t["moe_w_up"][layer], t["moe_w_down"][layer])
            base = len(units)
            for _ in range(3 * E):
                units.append(None)
            xsT = BC[:, 0:DC * WIDE].rearrange("p (c s) -> p c s", c=DC)
            ysT = BC[:, DC * WIDE:2 * DC * WIDE].rearrange("p (c s) -> p c s", c=DC)
            place = A[:, 0:TT * SLOTS].rearrange("p (t s) -> p t s", t=TT)
            cwt = A[:, 1024:1024 + TT * SLOTS].rearrange("p (t s) -> p t s", t=TT)
            tmp = A[:, 2048:2560]
            cw = A[:, 6144:6144 + 4 * S].rearrange("p (b s) -> p b s", b=4)
            ys = A[:, 0:4 * D].rearrange("p (b n) -> p b n", b=4)
            lg = A[:, 3072:3072 + TT * 72].rearrange("p (t n) -> p t n", t=TT)
            oh = A[:, 3328:3328 + 2 * TT * E].rearrange("p (k t e) -> p k t e", k=2, t=TT)
            both = A[:, 3584:3584 + TT * E].rearrange("p (t e) -> p t e", t=TT)
            prod = A[:, 3712:3776]
            cnt = A[:, 3776:3840]
            off = A[:, 3840:3904]
            cum = A[:, 3904:3968]
            posf = A[:, 4096:4096 + (PASSES + 1) * E].rearrange("p (j e) -> p j e", j=PASSES + 1)
            r = stat[:, 128:256]
            hid = A[:, 7488:7488 + 2 * FF].rearrange("p (b n) -> p b n", b=2)
            hidT = gtab[:, :, :, :, :].rearrange("p a b t d -> p (a b t d)")[:, 0:2 * 2 * P].rearrange(
                "p (b c n) -> p b c n", b=2, c=2)
            xg = hT[:, :, :].rearrange("p c s -> p (c s)").rearrange("p (b c n) -> p b c n", b=2, c=DC)
            yrow = hn[:, :, :]
            turn_banks = ((6, 7), (4, 5))

            w = A[:, 3968:4096]
            top, slot_of = w[:, 48:50], w[:, 52:56].rearrange("p (k t) -> p k t", k=2)
            equal, seen, e_logits = (w[:, a:a + 16].rearrange("p (t e) -> p t e", t=TT) for a in (0, 16, 32))
            chosen = w[:, 64:80].rearrange("p (t e) -> p t e", t=TT)
            group = w[:, 80:96].rearrange("p (t e) -> p t e", t=TT)
            g_dist = w[:, 96:112].rearrange("p (t e) -> p t e", t=TT)
            e_dist, g_sum, weight_1, weight_2 = (w[:, a:a + 2] for a in (112, 114, 116, 118))
            e_top = w[:, 120:124].rearrange("p (k t) -> p k t", k=2)
            masked = tmp[:, 0:2 * E].rearrange("p (t g e) -> p t g e", t=TT, g=GROUPS)

            def first_of(dst, values, top):
                dv.done(nc.vector.tensor_reduce(top, values, AX, ALU.max))
                dv.done(nc.vector.tensor_tensor(equal, values, top.unsqueeze(2).broadcast_to([P, TT, 8]), ALU.is_equal))
                dv.done(nc.vector.tensor_tensor_scan(w[:, 16:32], restart, w[:, 0:16], 0.0, ALU.mult, ALU.add))
                dv.done(nc.vector.scalar_tensor_tensor(out=dst, in0=seen, scalar=1.0, in1=equal,
                                                       op0=ALU.is_equal, op1=ALU.mult))

            def tensor(pe):
                nrm.tensor(pe)
                nrm.ready(pe)
                pe.wait_ge(*table_in(48))
                for tt in range(TT):
                    for c in range(DC):
                        i = nc.tensor.matmul(bank[0][:, tt * 72:(tt + 1) * 72], hT_lhs(c, tt),
                                             router_w[:, c, :], start=(c == 0), stop=(c == DC - 1))
                i.then_inc(logits.sem, 1)
                pe.wait_ge(*picked(1))
                nc.tensor.matmul(bank[1][:, 0:E], before, both[:, 0, :], start=True, stop=True)
                nc.tensor.matmul(bank[1][:, E:2 * E], ones, both[:, 0, :], start=True, stop=False)
                nc.tensor.matmul(bank[1][:, E:2 * E], before, both[:, 1, :], start=False, stop=True)
                nc.tensor.matmul(bank[1][:, 2 * E:3 * E], ones, both[:, 0, :], start=True, stop=False)
                nc.tensor.matmul(bank[1][:, 2 * E:3 * E], ones, both[:, 1, :], start=False,
                                 stop=True).then_inc(counted.sem, 1)

                def turn_weights():
                    pe.wait_ge(*cwt_ready(1))
                    for b in range(4):
                        for tt in range(TT):
                            i = nc.tensor.transpose(bank[4 + b // 2][:, (b % 2) * S + tt * P:(b % 2) * S + (tt + 1) * P],
                                                    cwt[:, tt, b * P:(b + 1) * P], ident)
                    i.then_inc(cw_turned.sem, 1)

                pe.wait_ge(*placed(1))
                for c in range(DC):
                    if c == 6:
                        turn_weights()
                    if c >= 6:
                        pe.wait_ge(*(spread if c % 2 == 0 else spread_a)((c - 6) // 2 + 1))
                    for tt in range(TT):
                        i = nc.tensor.matmul(bank[gather_banks[c % 6]][:, :], hn[:, tt, c:D:DC], place[:, tt, :], start=(tt == 0),
                                             stop=(tt == TT - 1))
                    i.then_inc(gathered.sem, 1)
                pe.wait_ge(*cw_ready(1))
                pe.wait_ge(*spread(4))
                pe.wait_ge(*spread_a(4))

                def gate_up(k, experts):
                    ps = bank[4 + k]
                    for part in range(2):
                        ws = [slots[part].rearrange("p (c f) -> p c f", c=DC) for slots in experts]
                        for c in range(DC):
                            for q, w in enumerate(ws):
                                i = nc.tensor.matmul(ps[q * CAP:(q + 1) * CAP, part * FF:(part + 1) * FF],
                                                     xg[:, k, c, q * CAP:(q + 1) * CAP], w[:, c, :],
                                                     start=(c == 0), stop=(c == DC - 1))
                        yield i

                def turn_hidden(k, rows):
                    for c in range(2):
                        i = nc.tensor.transpose(bank[6][:, c * P:c * P + rows], hid[0:rows, k, c:FF:2],
                                                ident[0:rows, 0:rows])
                    return i

                def down(k, experts):
                    ws = [w.rearrange("p (c n) -> p c n", c=2) for w in experts]
                    for nb in range(2):
                        for c in range(2):
                            for q, w in enumerate(ws):
                                i = nc.tensor.matmul(bank[2 * k + nb][q * CAP:(q + 1) * CAP, :],
                                                     hidT[:, k, c, q * CAP:(q + 1) * CAP],
                                                     w[:, c, nb * NB:(nb + 1) * NB], start=(c == 0), stop=(c == 1))
                    return i

                def turn_rows(k, rows):
                    for m in range(DC):
                        i = nc.tensor.transpose(bank[turn_banks[k][m // 4]][:, (m % 4) * P:(m % 4) * P + rows],
                                                yrow[0:rows, k, m * P:(m + 1) * P], ident[0:rows, 0:rows])
                    return i

                with pe.Fori(0, E // PER) as turn:
                    def here(k):
                        u = base + k
                        pe.wait_ge(*unit_full[u % RING](turn * 16 + 16 * (u // RING + 1)))

                    for k in range(2):
                        pe.wait_ge(*x_ready_(turn * 2 + k + 1))
                        if k == 0:
                            pe.wait_ge(*pair_stored(turn * 2 + 1))
                        g = gate_up(k, [(slot(base + GATE_AT[2 * k + q]), slot(base + UP_AT[2 * k + q]))
                                        for q in range(2)])
                        here(GATE_AT[2 * k])
                        here(GATE_AT[2 * k + 1])
                        next(g).then_inc(unit_done.sem, 2)
                        here(UP_AT[2 * k])
                        here(UP_AT[2 * k + 1])
                        next(g).then_inc(unit_done.sem, 2)
                    for k in range(2):
                        pe.wait_ge(*hid_ready(turn * 2 + k + 1))
                        turn_hidden(k, P).then_inc(h_turned.sem, 1)
                        pe.wait_ge(*hT_ready(turn * 2 + k + 1))
                        here(DOWN_AT[2 * k])
                        here(DOWN_AT[2 * k + 1])
                        down(k, [slot(base + DOWN_AT[2 * k + q]) for q in range(2)]).then_inc(unit_done.sem, 2)
                    for k in range(2):
                        pe.wait_ge(*rows_v(turn * 2 + k + 1))
                        pe.wait_ge(*rows_a(turn * 2 + k + 1))
                        turn_rows(k, P).then_inc(rows_turned.sem, 1)

                over = pe.value_load(pos_i[0:1, PASSES * E:PASSES * E + 1], min_val=0, max_val=S)
                pe.wait_ge(*pair_stored(E // 2 + 1))
                with pe.If(over > CAP):
                    with pe.Fori(0, (PASSES - 1) * E) as n:
                        pe.wait_ge(*f_x(n + 1))
                        pe.wait_ge(*f_full(n * 48 + 48))
                        g = gate_up(0, [(A[:, 0:2048], A[:, 2048:4096])])
                        next(g)
                        next(g).then_inc(f_up.sem, 1)
                        pe.wait_ge(*f_hid(n + 1))
                        turn_hidden(0, P).then_inc(f_turned.sem, 1)
                        pe.wait_ge(*f_hT(n + 1))
                        down(0, [A[:, 4096:6144]]).then_inc(f_down.sem, 1)
                        pe.wait_ge(*f_rows(n + 1))
                        turn_rows(0, P).then_inc(f_rturned.sem, 1)
                    pe.wait_ge(*f_stored((PASSES - 1) * E + 1))
                for b in range(4):
                    for hf in range(2):
                        j = 2 * b + hf
                        if j >= 2:
                            pe.wait_ge(*(y_out_v if j % 2 == 0 else y_out_a)(j // 2))
                        for m in range(4):
                            i = nc.tensor.transpose(bank[4 + j % 2][:, m * P:(m + 1) * P],
                                                    ysT[:, 4 * hf + m, b * P:(b + 1) * P], ident)
                        i.then_inc(y_turned.sem, 1)
                pe.wait_ge(*y_out_v(4))
                pe.wait_ge(*y_out_a(4))
                for tt in range(TT):
                    for nb in range(2):
                        for b in range(4):
                            i = nc.tensor.matmul(bank[2 * tt + nb][:, :], cw[:, b, tt * P:(tt + 1) * P],
                                                 ys[:, b, nb * NB:(nb + 1) * NB], start=(b == 0), stop=(b == 3))
                        i.then_inc(summed.sem, 1)

            zero64, restart = stat[:, 448:512], stat[:, 432:448]

            def vector(dve):
                nrm.vector(dve)
                have_small(dve)
                nc.vector.memset(zero64, 0.0)
                nc.vector.memset(xsT[:, :, SLOTS:WIDE], 0.0)
                dv.done(nc.vector.memset(restart, 1.0))
                dv.done(nc.vector.memset(restart[:, 0:16:8], 0.0))
                dve.wait_ge(*table_in(48))
                dve.wait_ge(*logits(1))
                dv.done(nc.vector.tensor_tensor(lg, bank[0][:, 0:TT * 72].rearrange("p (t n) -> p t n", t=TT),
                                                router_b[:, layer, :].unsqueeze(1).broadcast_to([P, TT, 72]), ALU.add))
                first_of(group, lg[:, :, 0:8], top)
                g4 = group.unsqueeze(3).broadcast_to([P, TT, 8, 8])
                dv.done(nc.vector.tensor_tensor(masked, lg[:, :, 8:72].rearrange("p t (g e) -> p t g e", g=8), g4, ALU.mult))
                dv.done(nc.vector.tensor_reduce(e_logits, masked.rearrange("p t g e -> p t e g"), AX, ALU.add))
                for k in range(2):
                    if k == 1:
                        dv.done(nc.vector.scalar_tensor_tensor(out=e_logits, in0=chosen, scalar=-3e38,
                                                               in1=e_logits, op0=ALU.mult, op1=ALU.add))
                    first_of(chosen, e_logits, e_top[:, k, :])
                    dv.done(nc.vector.tensor_tensor(oh[:, k, :, :].rearrange("p t (g e) -> p t g e", g=8), g4,
                                                    chosen.unsqueeze(2).broadcast_to([P, TT, 8, 8]), ALU.mult))
                nc.vector.tensor_tensor(both, oh[:, 0, :, :], oh[:, 1, :, :], ALU.add).then_inc(picked.sem, 1)
                nc.vector.tensor_tensor(g_dist, lg[:, :, 0:8], top.unsqueeze(2).broadcast_to([P, TT, 8]), ALU.subtract)
                nc.vector.tensor_tensor(e_dist, e_top[:, 1, :], e_top[:, 0, :], ALU.subtract).then_inc(gexp_in.sem, 1)
                dve.wait_ge(*counted(1))
                dv.done(nc.vector.tensor_copy(cnt, bank[1][:, 2 * E:3 * E]))
                dv.done(nc.vector.tensor_tensor_scan(cum, cnt, zero64, 0.0, ALU.add, ALU.add))
                dv.done(nc.vector.tensor_tensor(off, cum, cnt, ALU.subtract))
                place_in = tmp[:, 0:2 * E].rearrange("p (t e) -> p t e", t=TT)
                of_choice = tmp[:, 2 * E:6 * E].rearrange("p (k t e) -> p k t e", k=2, t=TT)
                dv.done(nc.vector.tensor_tensor(place_in, bank[1][:, 0:2 * E].rearrange("p (t e) -> p t e", t=TT),
                                                off.unsqueeze(1).broadcast_to([P, TT, E]), ALU.add))
                dv.done(nc.vector.tensor_tensor(of_choice, oh, place_in.unsqueeze(1).broadcast_to([P, 2, TT, E]), ALU.mult))
                dv.done(nc.vector.tensor_reduce(slot_of, of_choice, AX, ALU.add))
                for tt in range(TT):
                    dv.done(nc.vector.tensor_scalar(tmp, iota, slot_of[:, 0, tt:tt + 1], None, ALU.is_equal))
                    i = nc.vector.scalar_tensor_tensor(out=place[:, tt, :], in0=iota, scalar=slot_of[:, 1, tt:tt + 1],
                                                       in1=tmp, op0=ALU.is_equal, op1=ALU.add)
                    if tt == 0:
                        dv.done(i)
                i.then_inc(placed.sem, 1)
                dve.wait_ge(*gexp(2))
                dve.wait_ge(*placed(1))
                dv.done(nc.vector.tensor_reduce(g_sum, g_dist, AX, ALU.add))
                dv.done(nc.vector.scalar_tensor_tensor(out=g_sum, in0=e_dist, scalar=1.0, in1=g_sum, op0=ALU.add,
                                                       op1=ALU.mult))
                dv.done(nc.vector.reciprocal(weight_1, g_sum))
                dv.done(nc.vector.tensor_tensor(weight_2, weight_1, e_dist, ALU.mult))
                for tt in range(TT):
                    nc.vector.tensor_scalar(cwt[:, tt, :], iota, slot_of[:, 0, tt:tt + 1], weight_1[:, tt:tt + 1],
                                            ALU.is_equal, ALU.mult)
                    dv.done(nc.vector.tensor_scalar(tmp, iota, slot_of[:, 1, tt:tt + 1], weight_2[:, tt:tt + 1],
                                                    ALU.is_equal, ALU.mult))
                    i = nc.vector.tensor_tensor(cwt[:, tt, :], cwt[:, tt, :], tmp, ALU.add)
                    if tt == 0:
                        dv.done(i)
                i.then_inc(cwt_ready.sem, 1)

                def sort_in(c):
                    dve.wait_ge(*gathered(c + 1))
                    nc.vector.tensor_scalar(xsT[:, c, 0:SLOTS], bank[gather_banks[c % 6]][:, :], gains[:, 1, layer, c:c + 1],
                                            None, ALU.mult).then_inc(spread.sem, 1)
                sort_in(0)
                dv.done(nc.vector.tensor_copy(posf[:, 0, :], off))
                dv.done(nc.vector.tensor_copy(posf[:, PASSES, :], off))
                for j in range(1, PASSES):
                    nc.vector.tensor_scalar(posf[:, j, :], cnt, float(-CAP), float(j * CAP), ALU.add, ALU.min)
                dv.done(nc.vector.tensor_reduce(posf[:, PASSES, 0:1], cnt, AX, ALU.max))
                later_passes = posf[:, 1:PASSES, :]
                dv.done(nc.vector.tensor_tensor(later_passes, later_passes,
                                                off.unsqueeze(1).broadcast_to([P, PASSES - 1, E]), ALU.add))
                dv.done(nc.vector.tensor_scalar(later_passes, later_passes, float(-TRASH), None, ALU.add))
                for j in range(1, PASSES):
                    i = nc.vector.scalar_tensor_tensor(out=posf[:, j, :], in0=cnt, scalar=float(j * CAP),
                                                       in1=posf[:, j, :], op0=ALU.is_gt, op1=ALU.mult)
                dv.done(i)
                dv.done(nc.vector.tensor_scalar(later_passes, later_passes, float(TRASH), None, ALU.add))
                nc.vector.tensor_copy(pos_i[0:1, :], A[0:1, 4096:4096 + (PASSES + 1) * E]).then_inc(positioned.sem, 1)
                sort_in(2)
                sort_in(4)
                dve.wait_ge(*cw_turned(1))
                for b in range(2):
                    i = nc.vector.tensor_copy(cw[:, 2 * b:2 * b + 2, :],
                                              bank[4 + b][:, :].rearrange("p (b s) -> p b s", b=2))
                i.then_inc(cw_ready.sem, 1)
                sort_in(6)

                def tokens(index, dst):
                    where = dve.value_load(pos_i[0:1, index], min_val=0, max_val=TRASH)
                    return nc.vector.tensor_copy(dst, xsT[:, :, bass.ds(where, CAP)])

                def hidden(k, rows, wait):
                    g, u, e = bank[4 + k][0:rows, 0:FF], bank[4 + k][0:rows, FF:2 * FF], eb[0:rows, k, :]
                    wait(nc.vector.tensor_scalar(e, e, 1.0, None, ALU.add))
                    wait(nc.vector.reciprocal(e, e))
                    wait(nc.vector.tensor_tensor(e, g, e, ALU.mult))
                    return nc.vector.tensor_tensor(hid[0:rows, k, :], u, e, ALU.mult)

                dve.wait_ge(*spread(4))
                dve.wait_ge(*spread_a(4))
                dve.wait_ge(*logits(1))
                for k in range(2):
                    for q in range(2):
                        i = tokens(slice(2 * k + q, 2 * k + q + 1), xg[:, k, :, q * CAP:(q + 1) * CAP])
                    i.then_inc(x_ready_.sem, 1)
                with dve.Fori(0, E // PER) as turn:
                    for k in range(2):
                        steps = [3 * k]

                        def wait(ins):
                            steps[0] += 1
                            ins.then_inc(vstep.sem, 1)
                            dve.wait_ge(*vstep(turn * 6 + steps[0]))
                        dve.wait_ge(*exped(turn * 2 + k + 1))
                        hidden(k, P, wait).then_inc(hid_ready.sem, 1)
                        dve.wait_ge(*unit_done(turn * 12 + base + 4 * k + 4))
                        for q in range(2):
                            i = tokens(bass.ds(turn * PER + (PER + 2 * k + q), 1), xg[:, k, :, q * CAP:(q + 1) * CAP])
                        i.then_inc(x_ready_.sem, 1)
                    for k in range(2):
                        dve.wait_ge(*unit_done(turn * 12 + base + 10 + 2 * k))
                        nc.vector.tensor_copy(yrow[:, k, 0:NB], bank[2 * k][:, :]).then_inc(rows_v.sem, 1)

                over = dve.value_load(pos_i[0:1, PASSES * E:PASSES * E + 1], min_val=0, max_val=S)
                with dve.If(over > CAP):
                    with dve.Fori(0, (PASSES - 1) * E) as n:
                        steps = [0]

                        def wait(ins):
                            steps[0] += 1
                            ins.then_inc(f_v.sem, 1)
                            dve.wait_ge(*f_v(n * 3 + steps[0]))
                        dve.wait_ge(*f_stored(n + 1))
                        dve.wait_ge(*pair_stored(E // 2 + 1))
                        tokens(bass.ds(n + E, 1), xg[:, 0, :, 0:CAP]).then_inc(f_x.sem, 1)
                        dve.wait_ge(*f_exp(n + 1))
                        hidden(0, CAP, wait).then_inc(f_hid.sem, 1)
                for j in range(0, 8, 2):
                    dve.wait_ge(*y_turned(j + 1))
                    nc.vector.tensor_copy(ys[:, j // 2, 0:NB], bank[4][:, :]).then_inc(y_out_v.sem, 1)
                for tt in range(TT):
                    for nb in range(2):
                        dve.wait_ge(*summed(2 * tt + nb + 1))
                        xs = X[:, tt, nb * NB:(nb + 1) * NB]
                        nc.vector.tensor_tensor(xs, xs, bank[2 * tt + nb][:, :], ALU.add).then_inc(added.sem, 1)


            def scalar(act):
                nrm.scalar(act)
                act.wait_ge(*gexp_in(1))
                nc.scalar.activation(g_dist, g_dist, ACT.Exp).then_inc(gexp.sem, 1)
                nc.scalar.activation(e_dist, e_dist, ACT.Exp).then_inc(gexp.sem, 1)
                for c in range(1, DC, 2):
                    act.wait_ge(*gathered(c + 1))
                    nc.scalar.activation(xsT[:, c, 0:SLOTS], bank[gather_banks[c % 6]][:, :], ACT.Identity,
                                         scale=gains[:, 1, layer, c:c + 1]).then_inc(spread_a.sem, 1)
                act.wait_ge(*positioned(1))
                nc.scalar.activation(stat[:, 9:10], half[:, 0:1], ACT.Copy).then_inc(pair_stored.sem, 1)
                nc.scalar.activation(stat[:, 11:12], half[:, 0:1], ACT.Copy).then_inc(f_stored.sem, 1)

                def store(index, k, q):
                    where = act.value_load(pos_i[0:1, index], min_val=0, max_val=TRASH)
                    for hf in range(2):
                        i = nc.scalar.activation(
                            ysT[:, 4 * hf:4 * hf + 4, bass.ds(where, CAP)],
                            bank[turn_banks[k][hf]][:, :].rearrange("p (m s) -> p m s", m=4)[:, :, q * CAP:(q + 1) * CAP],
                            ACT.Copy)
                    return i

                def copy_hidden(k, rows):
                    return nc.scalar.activation(hidT[:, k, :, 0:rows],
                                                bank[6][:, 0:2 * P].rearrange("p (c n) -> p c n", c=2)[:, :, 0:rows],
                                                ACT.Copy)

                with act.Fori(0, E // PER) as turn:
                    for k in range(2):
                        act.wait_ge(*unit_done(turn * 12 + base + 4 * k + 4))
                        nc.scalar.activation(eb[:, k, :], bank[4 + k][:, 0:FF], ACT.Exp, scale=-1.0).then_inc(exped.sem, 1)
                    for k in range(2):
                        act.wait_ge(*h_turned(turn * 2 + k + 1))
                        copy_hidden(k, P).then_inc(hT_ready.sem, 1)
                        act.wait_ge(*unit_done(turn * 12 + base + 10 + 2 * k))
                        nc.scalar.activation(yrow[:, k, NB:D], bank[2 * k + 1][:, :], ACT.Copy).then_inc(rows_a.sem, 1)
                    for k in range(2):
                        act.wait_ge(*rows_turned(turn * 2 + k + 1))
                        act.wait_ge(*pair_stored(turn * 2 + k + 1))
                        store(bass.ds(turn * PER + 2 * k, 1), k, 0).then_inc(first_stored.sem, 1)
                        act.wait_ge(*first_stored(turn * 2 + k + 1))
                        store(bass.ds(turn * PER + 2 * k + 1, 1), k, 1).then_inc(pair_stored.sem, 1)
                over = act.value_load(pos_i[0:1, PASSES * E:PASSES * E + 1], min_val=0, max_val=S)
                with act.If(over > CAP):
                    with act.Fori(0, (PASSES - 1) * E) as n:
                        act.wait_ge(*pair_stored(E // 2 + 1))
                        act.wait_ge(*f_stored(n + 1))
                        act.wait_ge(*f_up(n + 1))
                        nc.scalar.activation(eb[0:CAP, 0, :], bank[4][0:CAP, 0:FF], ACT.Exp,
                                             scale=-1.0).then_inc(f_exp.sem, 1)
                        act.wait_ge(*f_turned(n + 1))
                        copy_hidden(0, CAP).then_inc(f_hT.sem, 1)
                        act.wait_ge(*f_down(n + 1))
                        nc.scalar.activation(yrow[0:CAP, 0, 0:NB], bank[0][0:CAP, :], ACT.Copy)
                        nc.scalar.activation(yrow[0:CAP, 0, NB:D], bank[1][0:CAP, :], ACT.Copy).then_inc(f_rows.sem, 1)
                        act.wait_ge(*f_rturned(n + 1))
                        store(bass.ds(n + E, 1), 0, 0).then_inc(f_stored.sem, 1)
                for j in range(1, 8, 2):
                    act.wait_ge(*y_turned(j + 1))
                    nc.scalar.activation(ys[:, j // 2, NB:D], bank[5][:, :], ACT.Copy).then_inc(y_out_a.sem, 1)

            def sync(sp):
                with sp.Fori(0, E // PER) as turn:
                    for k in range(3 * PER):
                        u = base + k
                        sp.wait_ge(*unit_done(turn * 12 + u - RING + 1))
                        w, at_ = next((w, at_) for w, at_ in ((gate_w, GATE_AT), (up_w, UP_AT), (down_w, DOWN_AT))
                                      if k in at_)
                        e = turn * PER + at_.index(k)
                        src = w[bass.ds(e, 1), :, :].rearrange("e (p c) n -> p (e c n)", p=P)
                        sp.dma_start(slot(u), src).then_inc(unit_full[u % RING].sem, 16)

            def gpsimd(pool):
                x_free(pool)
                pool.dma_start(router_w[:, :, 0:GROUPS],
                               t["moe_w_group"][layer].rearrange("(p c) n -> p c n", c=DC)).then_inc(table_in.sem, 16)
                pool.dma_start(router_w[:, :, GROUPS:],
                               t["moe_w_expert"][layer].rearrange("(p c) n -> p c n", c=DC)).then_inc(table_in.sem, 16)
                pool.dma_start(iota, later["iota"]).then_inc(table_in.sem, 16)
                nrm.gpsimd(pool)
                pool.wait_ge(*pair_stored(E // 2 + 1))
                over = pool.value_load(pos_i[0:1, PASSES * E:PASSES * E + 1], min_val=0, max_val=S)
                with pool.If(over > CAP):
                    with pool.Fori(0, PASSES - 1) as ps_:
                        with pool.Fori(0, E) as e:
                            pool.wait_ge(*f_stored(ps_ * E + e + 1))
                            for k, w in enumerate((gate_w, up_w, down_w)):
                                pool.dma_start(A[:, k * 2048:(k + 1) * 2048],
                                               w[bass.ds(e, 1), :, :].rearrange("e (p c) n -> p (e c n)", p=P)
                                               ).then_inc(f_full.sem, 16)

            def done(eng):
                eng.wait_ge(*added(4))
            st.tensor, st.vector, st.scalar, st.gpsimd, st.sync, st.ready = tensor, vector, scalar, gpsimd, sync, done
            return st

        m1_base = len(units)
        m1 = moe(0, "m1", o1_done, a1.ready)
        m1_units = (m1_base, m1_base + 3 * E)

        n2 = norm_stage("n2", m1.ready, gains[:, 0, 1, :])
        A_WIDTH = MLA_Q + MLA_KV + ROT

        def copy_a(eng, n, tt, ps):
            return nc.scalar.activation(hn[:, tt, n * NB:n * NB + ps.shape[1]], ps, ACT.Copy)
        pa = project_stage("pa", n2.ready, hT_lhs, square_units(t["mla_w_a"][0], A_WIDTH), copy_a)
        a_sq, a_rs, a_scaled = sem("a_sq"), sem("a_rs"), sem("a_scaled")
        a_parts = [(0, MLA_Q), (MLA_Q, MLA_Q + MLA_KV)]

        def latent_scalar(act):
            act.wait_ge(*pa.copied(4))
            for k, (a, b) in enumerate(a_parts):
                for tt in range(TT):
                    nc.scalar.activation(BC[:, k * 1024 + tt * 512:k * 1024 + tt * 512 + b - a], hn[:, tt, a:b], ACT.Square,
                                         accum_out=stat[:, 64 + 2 * k + tt:65 + 2 * k + tt]).then_inc(a_sq.sem, 1)

        def latent_gpsimd(pool):
            pool.wait_ge(*a_sq(4))
            for k, (a, b) in enumerate(a_parts):
                po.done(nc.gpsimd.tensor_scalar(stat[:, 68 + 2 * k:70 + 2 * k], stat[:, 64 + 2 * k:66 + 2 * k],
                                                1.0 / (b - a), EPS, ALU.mult, ALU.add))
            nc.gpsimd.tensor_tensor(stat[:, 72:76], stat[:, 68:72], half[:, 0:4], ALU.pow).then_inc(a_rs.sem, 1)

        def latent_vector(dve):
            dve.wait_ge(*a_rs(1))
            for k, (a, b) in enumerate(a_parts):
                for tt in range(TT):
                    i = nc.vector.tensor_scalar(hn[:, tt, a:b], hn[:, tt, a:b], stat[:, 72 + 2 * k + tt:73 + 2 * k + tt],
                                                None, ALU.mult)
            i.then_inc(a_scaled.sem, 1)

        def latent_ready(pe):
            pe.wait_ge(*a_scaled(1))
        cT = BC[:, 8192:8192 + 5 * S].rearrange("p (c s) -> p c s", c=5)
        t3 = turn_stage("t3", latent_ready,
                        [(lambda tt, c=c: hn[:, tt, c:MLA_Q:3], P, cT[:, c, :], mla_gain[:, c:c + 1]) for c in range(3)] +
                        [(lambda tt, c=c: hn[:, tt, MLA_Q + c:MLA_Q + MLA_KV:2], P, cT[:, 3 + c, :],
                          mla_gain[:, 3 + c:4 + c]) for c in range(2)])
        q_l = A[:, 0:3072].rearrange("p (t h d) -> p t h d", t=TT, h=HEADS)
        k_l = A[:, 3072:6144].rearrange("p (t h d) -> p t h d", t=TT, h=HEADS)
        v_l = A[:, 6144:8192].rearrange("p (t h d) -> p t h d", t=TT, h=HEADS)

        def copy_q(eng, n, tt, ps):
            return nc.scalar.activation(A[:, tt * 1536 + n * NB:tt * 1536 + (n + 1) * NB], ps, ACT.Copy)

        def copy_kv(eng, n, tt, ps):
            kv = ps.rearrange("p (h d) -> p h d", h=2)
            nc.scalar.activation(k_l[:, tt, 2 * n:2 * n + 2, 0:NOPE], kv[:, :, 0:NOPE], ACT.Copy)
            return nc.scalar.activation(v_l[:, tt, 2 * n:2 * n + 2, :], kv[:, :, NOPE:], ACT.Copy)
        pq = project_stage("pq", t3.ready, lambda c, tt: cT[:, c, tt * P:(tt + 1) * P],
                           square_units(t["mla_w_qb"][0], 1536, kc=3, per=3), copy_q)
        kv_src = t["mla_w_kvb"][0].rearrange("(p c) n -> p c n", c=2)
        kv_blocks = []
        for n in range(2):
            u = plan(lambda a: a.rearrange("p (c n) -> p c n", c=2), kv_src[:, :, n * 1024:(n + 1) * 1024])
            for hf in range(2):
                kv_blocks.append((NB, [(u, lambda a, hf=hf: a.rearrange("p (c n) -> p c n", c=2)[:, :, hf * NB:(hf + 1) * NB],
                                        2, hf == 0)]))

        def q_left(pe):
            pe.wait_ge(*pq.copied(6))
        pkv = project_stage("pkv", q_left, lambda c, tt: cT[:, 3 + c, tt * P:(tt + 1) * P], kv_blocks, copy_kv)
        l_sq, l_ss, l_rs, l_pe, l_qk = sem("l_sq"), sem("l_ss"), sem("l_rs"), sem("l_pe"), sem("l_qk")
        l_items = [(q_l, 0, 0), (q_l, 0, 1), (k_l, 1, 0), (k_l, 1, 1)]

        l_spare = (hn[:, :, :].rearrange("p t d -> p (t d)"), hT[:, :, :].rearrange("p c s -> p (c s)"))

        def l_squares(j):
            return l_spare[j % 2][:, 0:1536]

        def heads_scalar(act, items):
            for j in items:
                x, qk, tt = l_items[j]
                act.wait_ge(*l_pe(2))
                if j < 2:
                    act.wait_ge(*pq.copied(6))
                else:
                    act.wait_ge(*pkv.copied(8))
                    act.wait_ge(*l_ss(j - 1))
                nc.scalar.activation(l_squares(j), x[:, tt, :, :].rearrange("p h d -> p (h d)"),
                                     ACT.Square).then_inc(l_sq.sem, 1)

        def heads_gpsimd(pool):
            for j in range(4):
                pool.wait_ge(*l_ss(j + 1))
                a, b = 64 + 8 * (j % 2), 80 + 8 * (j % 2)
                po.done(nc.gpsimd.tensor_scalar(stat[:, 96:104], stat[:, a:a + 8], 1.0 / MLA_QK, EPS, ALU.mult, ALU.add))
                nc.gpsimd.tensor_tensor(stat[:, b:b + 8], stat[:, 96:104], half[:, 0:8], ALU.pow).then_inc(l_rs.sem, 1)

        def heads_vector(dve):
            for tt in range(TT):
                nc.vector.tensor_copy(k_l[:, tt, :, NOPE:], hn[:, tt, MLA_Q + MLA_KV:A_WIDTH].unsqueeze(1)
                                      .broadcast_to([P, HEADS, ROT])).then_inc(l_pe.sem, 1)
            dve.wait_ge(*l_pe(2))
            for j, (x, qk, tt) in enumerate(l_items):
                dve.wait_ge(*l_sq(j + 1))
                if j >= 2:
                    dve.wait_ge(*l_rs(j))
                nc.vector.tensor_reduce(stat[:, 64 + 8 * (j % 2):72 + 8 * (j % 2)],
                                        l_squares(j).rearrange("p (h d) -> p h d", h=HEADS), AX, ALU.add).then_inc(l_ss.sem, 1)
                t1_ = l_spare[0][:, 1536:2048].rearrange("p (h d) -> p h d", h=HEADS)
                t2_ = l_spare[1][:, 1536:2048].rearrange("p (h d) -> p h d", h=HEADS)
                rotate(dve, x[:, tt, :, NOPE:], None, ROT, HEADS, qk, tt, t1_, t2_)
                dve.wait_ge(*l_rs(j + 1))
                r = stat[:, 80 + 8 * (j % 2):88 + 8 * (j % 2)].unsqueeze(2)
                nc.vector.tensor_tensor(x[:, tt, :, 0:NOPE], x[:, tt, :, 0:NOPE], r.broadcast_to([P, HEADS, NOPE]),
                                        ALU.mult)
                nc.vector.tensor_tensor(x[:, tt, :, NOPE:], t1_, r.broadcast_to([P, HEADS, ROT]),
                                        ALU.mult).then_inc(l_qk.sem, 1)
                dve.wait_ge(*l_qk(j + 1))

        nopeT = BC[:, 0:16 * S].rearrange("p (h k s) -> p h k s", h=HEADS, k=2)
        peT = BC[:, 16 * S:32 * S].rearrange("p (h k s) -> p h k s", h=HEADS, k=2)

        def l_turn(name, x, k, **how):
            jobs = []
            for h in range(HEADS):
                jobs.append((lambda tt, h=h: x[:, tt, h, 0:NOPE], P, nopeT[:, h, k, :], mla_gain[:, 5 + k:6 + k]))
                jobs.append((lambda tt, h=h: x[:, tt, h, NOPE:], ROT, peT[0:ROT, h, k, :], None))
            return turn_stage(name, lambda pe: pe.wait_ge(*l_qk(2 * k + 2)), jobs, **how)
        t4q = l_turn("t4q", q_l, 0, scalar_only=True)
        t4k = l_turn("t4k", k_l, 1, bank0=6)
        cond2 = Conditioning(2, 3, HEADS)

        def l_turned(pe):
            t4q.ready(pe)
            t4k.ready(pe)

        def latent_head(h):
            pairs = [(lambda tt: nopeT[:, h, 0, tt * P:(tt + 1) * P], lambda k0, k1: nopeT[:, h, 1, k0:k1]),
                     (lambda tt: peT[0:ROT, h, 0, tt * P:(tt + 1) * P], lambda k0, k1: peT[0:ROT, h, 1, k0:k1])]
            return ([pairs], lambda kt: v_l[:, kt, h, :], lambda tt: hn[:, tt, h * P:(h + 1) * P])
        a2 = attention_stage("a2", l_turned, [latent_head(h) for h in range(HEADS)], MLA_QK ** -0.5, P,
                             lambda h: at["causal"], filler=cond2)
        t5 = heads_turned("t5", a2.ready)
        o2 = project_stage("o2", t5.ready, hT_lhs, square_units(t["mla_w_out"][0], D, order="(c p)"), add_x)

        def o2_done(eng):
            eng.wait_ge(*o2.copied(4))
        u3 = len(units)
        m2 = moe(1, "m2", o2_done, a2.ready)
        u4 = len(units)

        mod_in, mod_ready = sem("mod_in"), sem("mod_ready")
        b_cols = stat[:, 256:288].rearrange("p (k c) -> p k c", k=4)
        MOD = (0, 1, 3, 4)

        def conditioning_gpsimd(pool):
            cond1.ready(pool)
            cond2.ready(pool)
            for k, m in enumerate(MOD):
                pool.dma_start(modc[:, k, :], mod_dram[m * D:(m + 1) * D].rearrange("(p c) -> p c", c=DC)
                               ).then_inc(mod_in.sem, 16)
                pool.dma_start(b_cols[:, k, :], t["b_ada_2"][m * D:(m + 1) * D].rearrange("(p c) -> p c", c=DC)
                               ).then_inc(mod_in.sem, 16)

        def conditioning_vector(dve):
            dve.wait_ge(*mod_in(16 * 8))
            dv.done(nc.vector.tensor_tensor(modc[:, :, :], modc[:, :, :], b_cols, ALU.add))
            for k in range(2):
                dv.done(nc.vector.tensor_scalar(modc[:, 2 * k + 1, :], modc[:, 2 * k + 1, :], 1.0, None, ALU.add))
                i = nc.vector.tensor_tensor(modc[:, 2 * k + 1, :], modc[:, 2 * k + 1, :], gains2[:, k, :], ALU.mult)
            i.then_inc(mod_ready.sem, 1)
            dve.wait_ge(*mod_ready(1))

        n3 = norm_stage("n3", m2.ready, modc[:, 1, :], shift=modc[:, 0, :], extra=[(mod_ready, 1)])
        z = A[:, 0:TT * HYB_IN].rearrange("p (t n) -> p t n", t=TT)
        QA, KA, VA, QB, KB, VB, FB = 0, 512, 640, 768, 1280, 1792, 2304
        z_blocks = square_units(t["w_in_2"], HYB_IN - 4 * NB, col0=4 * NB) + square_units(t["w_in_2"], 4 * NB)
        z_at = (4, 0, 1, 2, 3)

        def copy_z(eng, n, tt, ps):
            c0 = z_at[n] * NB
            return nc.scalar.activation(z[:, tt, c0:c0 + ps.shape[1]], ps, ACT.Copy)
        pz = project_stage("pz", n3.ready, hT_lhs, z_blocks, copy_z)
        table = A[:, 4624:4624 + P + 2 * SPAN]
        upto, window, dist = table[:, 0:P], table[:, P:P + SPAN], table[:, P + SPAN:]
        fk = A[:, 5520:5520 + HEADS * S].rearrange("p (h s) -> p h s", h=HEADS)
        hbias = A[:, 7568:7568 + SPAN]
        fox = stat[:, 288:288 + 5 * TT * HEADS].rearrange("p (k t h) -> p k t h", k=5, t=TT)
        f_raw, f_abs, f_log, f_sum, f_low = (fox[:, k, :, :] for k in range(5))
        table3, fx = sem("table3"), sem("fx")
        fx_exp, fx_log, fx_ready, fx_sum, fx_col = sem("fx_exp"), sem("fx_log"), sem("fx_ready"), sem("fx_sum"), sem("fx_col")
        fx_turned, fx_rows, fx_spread, fx_out = sem("fx_turned"), sem("fx_rows"), sem("fx_spread"), sem("fx_out")
        fT = hT[0:HEADS, 0, :]

        def tables_gpsimd(pool):
            m2.ready(pool)
            pool.dma_start(upto, later["upto"]).then_inc(table3.sem, 16)
            pool.dma_start(window, later["window"]).then_inc(table3.sem, 16)
            pool.dma_start(dist, later["dist"]).then_inc(table3.sem, 16)

        def forget_vector(dve):
            dve.wait_ge(*pz.copied(2))
            dv.done(nc.vector.tensor_tensor(f_raw, z[:, :, FB:FB + HEADS],
                                            f_bias.unsqueeze(1).broadcast_to([P, TT, HEADS]), ALU.add))
            nc.vector.tensor_scalar(f_low, f_raw, 0.0, None, ALU.min)
            dv.done(nc.vector.tensor_scalar(f_abs, f_raw, -1.0, None, ALU.mult))
            nc.vector.tensor_tensor(f_abs, f_abs, f_raw, ALU.max).then_inc(fx.sem, 1)
            dve.wait_ge(*fx_exp(1))
            nc.vector.tensor_scalar(f_abs, f_abs, 1.0, None, ALU.add).then_inc(fx.sem, 1)
            dve.wait_ge(*fx_log(1))
            nc.vector.tensor_tensor(f_log, f_low, f_abs, ALU.subtract).then_inc(fx_ready.sem, 1)
            dve.wait_ge(*fx_sum(1))
            nc.vector.tensor_copy(f_sum, bank[7][:, 0:TT * HEADS].rearrange("p (t h) -> p t h", t=TT)).then_inc(fx_col.sem, 1)
            dve.wait_ge(*fx_turned(1))
            nc.vector.tensor_copy(fT, bank[7][0:HEADS, 0:S]).then_inc(fx_rows.sem, 1)
            for b in range(4):
                dve.wait_ge(*fx_spread(b + 1))
                nc.vector.tensor_copy(fk[:, 2 * b:2 * b + 2, :], bank[4 + b][:, :].rearrange("p (h s) -> p h s", h=2)
                                      ).then_inc(fx_out.sem, 1)

        def forget_scalar(act):
            act.wait_ge(*fx(1))
            nc.scalar.activation(f_abs, f_abs, ACT.Exp, scale=-1.0).then_inc(fx_exp.sem, 1)
            act.wait_ge(*fx(2))
            nc.scalar.activation(f_abs, f_abs, ACT.Ln).then_inc(fx_log.sem, 1)

        def forget_tensor(pe):
            pe.wait_ge(*table3(48))
            pe.wait_ge(*fx_ready(1))
            nc.tensor.matmul(bank[7][:, 0:HEADS], upto, f_log[:, 0, :], start=True, stop=True)
            nc.tensor.matmul(bank[7][:, HEADS:2 * HEADS], ones, f_log[:, 0, :], start=True, stop=False)
            nc.tensor.matmul(bank[7][:, HEADS:2 * HEADS], upto, f_log[:, 1, :], start=False,
                             stop=True).then_inc(fx_sum.sem, 1)
            pe.wait_ge(*fx_col(1))
            for tt in range(TT):
                i = nc.tensor.transpose(bank[7][0:HEADS, tt * P:(tt + 1) * P], f_sum[:, tt, :], ident)
            i.then_inc(fx_turned.sem, 1)
            pe.wait_ge(*fx_rows(1))
            for h in range(HEADS):
                i = nc.tensor.matmul(bank[4 + h // 2][:, (h % 2) * S:(h % 2 + 1) * S],
                                     ident[0:HEADS, h:h + 1].broadcast_to([HEADS, P]), fT, start=True, stop=True)
                if h % 2:
                    i.then_inc(fx_spread.sem, 1)

        def z_ready(pe):
            pe.wait_ge(*pz.copied(10))
            pe.wait_ge(*fx_out(4))
        zT = BC[0:ROT, 0:26 * S].rearrange("p (j s) -> p j s", s=S)
        cols = [QA + 64 * h for h in range(8)] + [KA, KA + 64] + [QB + 64 * h for h in range(8)] + \
               [KB + 64 * h for h in range(8)]
        t6 = turn_stage("t6", z_ready, [(lambda tt, c0=c0: z[:, tt, c0:c0 + ROT], ROT, zT[:, j, :], None)
                                        for j, c0 in enumerate(cols)])

        def head3(h):
            if h < HEADS:
                qj, kj, vc, oc = h, 8 + h // 4, VA + 64 * (h // 4), 64 * h
            else:
                qj, kj, vc, oc = 10 + h - 8, 18 + h - 8, VB + 64 * (h - 8), 64 * h
            return ([[(lambda tt: zT[:, qj, tt * P:(tt + 1) * P], lambda k0, k1: zT[:, kj, k0:k1])]],
                    lambda kt: z[:, kt, vc:vc + ROT], lambda tt: hn[:, tt, oc:oc + ROT])

        def bias3(h):
            if h < HEADS:
                slope = 2.0 ** (-8.0 * (h + 1) / HEADS)
                dv.done(nc.vector.scalar_tensor_tensor(out=hbias, in0=dist, scalar=-slope, in1=window, op0=ALU.mult,
                                                       op1=ALU.add))
                return hbias
            for tt, (a, b) in enumerate([(0, P), (P, SPAN)]):
                i = nc.vector.tensor_scalar(hbias[:, a:b], fk[:, h - HEADS, 0:b - a], -1.0,
                                            f_sum[:, tt, h - HEADS:h - HEADS + 1], ALU.mult, ALU.add)
            dv.done(i)
            dv.done(nc.vector.tensor_tensor(hbias, hbias, at["causal"], ALU.add))
            return hbias
        a3 = attention_stage("a3", t6.ready, [head3(h) for h in range(2 * HEADS)], ROT ** -0.5, ROT, bias3, sink=True)
        t7 = heads_turned("t7", a3.ready)

        gate_in = [sem("gate1_in"), sem("gate2_in")]
        gate_rows = [A[:, 0:D], A[:, 5632:5632 + D]]
        gate_bias = [A[:, D:2 * D], A[:, 6656:6656 + D]]
        scratch = [A[:, 2048:3072], BC[:, 7168:8192]]
        gate_ready = [sem("gate1_ready"), sem("gate2_ready")]
        g_fin = A[:, 0:D]
        fin_in = sem("fin_in")

        def gate_gpsimd(pool, k):
            m = (2, 5)[k]
            pool.dma_start(gate_rows[k], mod_dram[m * D:(m + 1) * D].partition_broadcast(P)).then_inc(gate_in[k].sem, 16)
            pool.dma_start(gate_bias[k], t["b_ada_2"][m * D:(m + 1) * D].partition_broadcast(P)).then_inc(gate_in[k].sem, 16)

        def gate_vector(dve, k):
            dve.wait_ge(*gate_in[k](32))
            dv.done(nc.vector.tensor_tensor(gate_rows[k], gate_rows[k], gate_bias[k], ALU.add))

        def gated(k):
            def add(eng, n, tt, ps):
                xs = X[:, tt, n * NB:(n + 1) * NB]
                product = scratch[k][:, tt * NB:(tt + 1) * NB]
                dv.done(nc.vector.tensor_tensor(product, ps, gate_rows[k][:, n * NB:(n + 1) * NB], ALU.mult))
                return nc.vector.tensor_tensor(xs, xs, product, ALU.add)
            return add
        o3 = project_stage("o3", t7.ready, hT_lhs, square_units(t["w_out_2"], D, order="(c p)"), gated(0))

        def o3_done(eng):
            eng.wait_ge(*o3.copied(4))

        n4 = norm_stage("n4", o3_done, modc[:, 3, :], shift=modc[:, 2, :])
        FB_ = DFF // P
        PAIRS = FB_ // 2
        up_src = t["w_up_2"].rearrange("(p c) n -> p c n", c=DC)
        down_src = t["w_down_2"].rearrange("(c p) n -> p c n", p=P)
        up_units = [[plan(lambda a: a.rearrange("p (c n) -> p c n", c=DC), up_src[:, :, c0 + j * 256:c0 + (j + 1) * 256])
                     for c0 in (DFF, 0)] for j in range(PAIRS)]
        down_units = [plan(lambda a: a.rearrange("p (c n) -> p c n", c=2), down_src[:, 2 * j:2 * j + 2, :])
                      for j in range(PAIRS)]
        hidT3 = BC[:, 0:FB_ * S].rearrange("p (b s) -> p b s", b=FB_)
        cw3 = BC[:, 5632:5632 + 4 * 2 * FB_].rearrange("p (k b) -> p k b", k=4)
        cw_rows = BC[0:2 * FB_, 6144:6144 + 4 * P].rearrange("p (k c) -> p k c", k=4)
        cw_in, cw_turned3, cw_out = sem("cw_in"), sem("cw_turned3"), sem("cw_out")
        raw = A[:, 2048:4096].rearrange("p (j h n) -> p j h n", j=2, h=2)
        yv = A[:, 4096:5120].rearrange("p (h b s) -> p h b s", h=2, b=2)
        ev = A[:, 5120:5632].rearrange("p (b s) -> p b s", b=2)
        raw_copied, raw_used, g_conv, g_exp, hid3 = (sem("raw_copied"), sem("raw_used"), sem("g_conv"), sem("g_exp"),
                                                     sem("hid3"))
        down_done, out_added = sem("down_done"), sem("out_added")

        def mlp_gpsimd(pool):
            a3.ready(pool)
            gate_gpsimd(pool, 0)
            for k in range(3):
                pool.dma_start(cw_rows[:, k, :], t["conv_w_2"][k].rearrange("(b p) -> b p", p=P)).then_inc(cw_in.sem, 16)
            pool.dma_start(cw_rows[:, 3, :], t["conv_b_2"].rearrange("(b p) -> b p", p=P)).then_inc(cw_in.sem, 16)
            o3_done(pool)
            gate_gpsimd(pool, 1)
            pool.dma_start(g_fin, t["g_final_2"].partition_broadcast(P)).then_inc(fin_in.sem, 16)

        def mlp_tensor(pe):
            pe.wait_ge(*cw_in(64))
            for k in range(4):
                i = nc.tensor.transpose(bank[6][:, k * 64:k * 64 + 2 * FB_], cw_rows[:, k, :], ident[0:2 * FB_, 0:2 * FB_])
            i.then_inc(cw_turned3.sem, 1)
            n4.ready(pe)
            for j in range(PAIRS):
                for h in range(2):
                    n = 2 * j + h
                    if n >= 4:
                        pe.wait_ge(*raw_copied(n - 3))
                    u = up_units[j][h]
                    unit_here(pe, u)
                    w = units[u][0](slot(u))
                    for b in range(2):
                        for c in range(DC):
                            i = nc.tensor.matmul(bank[n % 4][:, b * S:(b + 1) * S], w[:, c, b * P:(b + 1) * P],
                                                 hT[:, c, :], start=(c == 0), stop=(c == DC - 1))
                    i.then_inc(unit_done.sem, 1)
            pe.wait_ge(*cw_out(1))
            for j in range(PAIRS):
                u = down_units[j]
                pe.wait_ge(*hid3(j + 1))
                unit_here(pe, u)
                w = units[u][0](slot(u))
                for c in range(2):
                    for tt in range(TT):
                        for nb in range(2):
                            i = nc.tensor.matmul(bank[4 + 2 * tt + nb][:, :], hidT3[:, 2 * j + c, tt * P:(tt + 1) * P],
                                                 w[:, c, nb * NB:(nb + 1) * NB], start=(j == 0 and c == 0),
                                                 stop=(j == PAIRS - 1 and c == 1))
                i.then_inc(unit_done.sem, 1)

        def mlp_scalar(act):
            for j in range(PAIRS):
                for h in range(2):
                    n = 2 * j + h
                    act.wait_ge(*unit_done(up_units[j][h] + 1))
                    if j >= 2:
                        act.wait_ge(*raw_used(n - 3))
                    nc.scalar.activation(raw[:, j % 2, h, :], bank[n % 4][:, :], ACT.Copy).then_inc(raw_copied.sem, 1)
                act.wait_ge(*g_conv(j + 1))
                nc.scalar.activation(ev, yv[:, 0, :, :], ACT.Exp, scale=-1.0).then_inc(g_exp.sem, 1)

        def mlp_vector(dve):
            dve.wait_ge(*cw_turned3(1))
            nc.vector.tensor_copy(cw3, bank[6][:, 0:256].rearrange("p (k b) -> p k b", k=4)[:, :, 0:2 * FB_]
                                  ).then_inc(cw_out.sem, 1)
            dve.wait_ge(*cw_out(1))
            for j in range(PAIRS):
                for h in range(2):
                    dve.wait_ge(*raw_copied(2 * j + h + 1))
                    blocks = [((FB_ if h == 0 else 0) + 2 * j + b, raw[:, j % 2, h, b * S:(b + 1) * S], yv[:, h, b, :])
                              for b in range(2)]
                    for ch, x, y in blocks:
                        i = nc.vector.tensor_scalar(y, x, cw3[:, 2, ch:ch + 1], cw3[:, 3, ch:ch + 1], ALU.mult, ALU.add)
                    dv.done(i)
                    for back in (1, 2):
                        for ch, x, y in blocks:
                            i = nc.vector.scalar_tensor_tensor(out=y[:, back:], in0=x[:, 0:S - back],
                                                               scalar=cw3[:, 2 - back, ch:ch + 1], in1=y[:, back:],
                                                               op0=ALU.mult, op1=ALU.add)
                        if back == 1:
                            dv.done(i)
                    i.then_inc(raw_used.sem, 1)
                    if h == 0:
                        dve.wait_ge(*raw_used(2 * j + 1))
                        nc.vector.tensor_copy(stat[:, 14:15], stat[:, 64:65]).then_inc(g_conv.sem, 1)
                dve.wait_ge(*g_exp(j + 1))
                dve.wait_ge(*raw_used(2 * j + 2))
                dv.done(nc.vector.tensor_scalar(ev, ev, 1.0, None, ALU.add))
                dv.done(nc.vector.reciprocal(ev, ev))
                dv.done(nc.vector.tensor_tensor(ev, ev, yv[:, 0, :, :], ALU.mult))
                nc.vector.tensor_tensor(hidT3[:, 2 * j:2 * j + 2, :], ev, yv[:, 1, :, :], ALU.mult).then_inc(hid3.sem, 1)
            gate_vector(dve, 1)
            dve.wait_ge(*unit_done(down_units[-1] + 1))
            for nb in range(2):
                for tt in range(TT):
                    gated(1)(dve, nb, tt, bank[4 + 2 * tt + nb][:, :]).then_inc(out_added.sem, 1)

        last_sq, last_rs, result = sem("last_sq"), sem("last_rs"), sem("result")

        def last_scalar(act):
            act.wait_ge(*out_added(4))
            for tt in range(TT):
                nc.scalar.activation(hT[:, :, :].rearrange("p c s -> p (c s)")[:, tt * D:(tt + 1) * D], X[:, tt, :],
                                     ACT.Square, accum_out=stat[:, tt:tt + 1]).then_inc(last_sq.sem, 1)

        def last_gpsimd(pool):
            pool.wait_ge(*last_sq(TT))
            po.done(nc.gpsimd.tensor_scalar(stat[:, 2:4], stat[:, 0:2], 1.0 / D, EPS, ALU.mult, ALU.add))
            nc.gpsimd.tensor_tensor(stat[:, 2:4], stat[:, 2:4], half[:, 0:TT], ALU.pow).then_inc(last_rs.sem, 1)

        def last_vector(dve):
            dve.wait_ge(*last_rs(1))
            dve.wait_ge(*fin_in(16))
            for tt in range(TT):
                nc.vector.scalar_tensor_tensor(out=hn[:, tt, :], in0=X[:, tt, :], scalar=stat[:, 2 + tt:3 + tt], in1=g_fin,
                                               op0=ALU.mult, op1=ALU.mult).then_inc(result.sem, 1)

        block = ctx.enter_context(nc.Block())
        final_out = sem("final_out")

        @block.sync
        def _(sp):
            def load(first, last):
                for u in range(first, last):
                    load_unit(sp, u)
            start_sync(sp)
            load(4, m1_units[0])
            m1.sync(sp)
            load(m1_units[1], u3)
            m2.sync(sp)
            load(u4, len(units))
            for tt in range(TT):
                sp.wait_ge(*result(tt + 1))
                sp.dma_start(out[0, tt * P:(tt + 1) * P, :], hn[:, tt, :]).then_inc(final_out.sem, 16)
            sp.wait_ge(*final_out(16 * TT))

        @block.gpsimd
        def _(pool):
            po.eng = pool
            po.done(nc.gpsimd.memset(half[:, :], -0.5))
            n1.gpsimd(pool)
            rope_gpsimd(pool)
            sub_gpsimd(pool)
            m1.gpsimd(pool)
            n2.gpsimd(pool)
            latent_gpsimd(pool)
            heads_gpsimd(pool)
            conditioning_gpsimd(pool)
            m2.gpsimd(pool)
            tables_gpsimd(pool)
            n3.gpsimd(pool)
            mlp_gpsimd(pool)
            n4.gpsimd(pool)
            last_gpsimd(pool)

        @block.scalar
        def _(act):
            n1.scalar(act)
            setup_scalar(act)
            p1.drain(act)
            t1.scalar(act)
            a1.scalar(act)
            t2.scalar(act)
            m1.scalar(act)
            n2.scalar(act)
            pa.drain(act)
            latent_scalar(act)
            t3.scalar(act)
            pq.drain(act)
            heads_scalar(act, (0, 1))
            pkv.drain(act)
            heads_scalar(act, (2, 3))
            t4q.scalar(act)
            t4k.scalar(act)
            a2.scalar(act)
            t5.scalar(act)
            m2.scalar(act)
            n3.scalar(act)
            pz.drain(act)
            forget_scalar(act)
            t6.scalar(act)
            a3.scalar(act)
            t7.scalar(act)
            n4.scalar(act)
            mlp_scalar(act)
            last_scalar(act)

        @block.vector
        def _(dve):
            dv.eng = dve
            n1.vector(dve)
            setup_vector(dve)
            rope_vector(dve)
            t1.vector(dve)
            a1.vector(dve)
            sub_vector(dve)
            t2.vector(dve)
            o1.drain(dve)
            m1.vector(dve)
            n2.vector(dve)
            fold_rope(1)
            latent_vector(dve)
            t3.vector(dve)
            heads_vector(dve)
            t4k.vector(dve)
            a2.vector(dve)
            t5.vector(dve)
            o2.drain(dve)
            m2.vector(dve)
            conditioning_vector(dve)
            n3.vector(dve)
            forget_vector(dve)
            t6.vector(dve)
            a3.vector(dve)
            t7.vector(dve)
            gate_vector(dve, 0)
            o3.drain(dve)
            n4.vector(dve)
            mlp_vector(dve)
            last_vector(dve)

        @block.tensor
        def _(pe):
            n1.tensor(pe)
            p1.tensor(pe)
            t1.tensor(pe)
            a1.tensor(pe)
            t2.tensor(pe)
            o1.tensor(pe)
            m1.tensor(pe)
            n2.tensor(pe)
            pa.tensor(pe)
            t3.tensor(pe)
            pq.tensor(pe)
            pkv.tensor(pe)
            t4q.tensor(pe)
            t4k.tensor(pe)
            a2.tensor(pe)
            t5.tensor(pe)
            o2.tensor(pe)
            m2.tensor(pe)
            n3.tensor(pe)
            pz.tensor(pe)
            forget_tensor(pe)
            t6.tensor(pe)
            a3.tensor(pe)
            t7.tensor(pe)
            o3.tensor(pe)
            n4.tensor(pe)
            mlp_tensor(pe)


INPUTS = ["x", "attn_norm", "ffn_norm", "diff_w_in", "diff_q_norm", "diff_k_norm", "diff_lambda_q1",
          "diff_lambda_k1", "diff_lambda_q2", "diff_lambda_k2", "diff_subln", "diff_w_out", "mla_w_a",
          "mla_q_a_norm", "mla_kv_a_norm", "mla_w_qb", "mla_w_kvb", "mla_q_norm", "mla_k_norm", "mla_w_out",
          "moe_w_group", "moe_b_group", "moe_w_expert", "moe_b_expert", "moe_w_gate", "moe_w_up", "moe_w_down",
          "c_2", "w_ada_2", "b_ada_2", "g_attn_2", "w_in_2", "b_f_2", "sinks_2", "w_out_2", "g_mlp_2", "w_up_2",
          "conv_w_2", "conv_b_2", "w_down_2", "g_final_2"]


def kernel(**inputs):
    import concourse.bacc as bacc
    from concourse.bass_utils import run_bass_kernel_spmd

    nc = bacc.Bacc("TRN2", target_bir_lowering=False, num_devices=1)
    arrays, tensors = {}, {}
    for name in INPUTS:
        a = np.ascontiguousarray(inputs[name])
        arrays["in_" + name] = a
        tensors[name] = nc.dram_tensor("in_" + name, a.shape, mybir.dt.from_np(a.dtype), kind="ExternalInput").ap()
    arrays["in_constants"] = shape_constants()
    tensors["constants"] = nc.dram_tensor("in_constants", arrays["in_constants"].shape, F32,
                                          kind="ExternalInput").ap()
    out = nc.dram_tensor("out_0", (1, S, D), F32, kind="ExternalOutput").ap()
    build(nc, tensors, out)
    r = run_bass_kernel_spmd(nc, [arrays], core_ids=[0])
    return r.results[0]["out_0"]
```

```python
import math
from contextlib import ExitStack

import numpy as np

import concourse.bass as bass
from concourse import mybir

ALU = mybir.AluOpType
ACT = mybir.ActivationFunctionType
F32 = mybir.dt.float32
I32 = mybir.dt.int32
AX = mybir.AxisListType.X

P = 128
S = 256
TT = S // P
D = 1024
DC = D // P
EPS = 1e-6
NEG = -1e30
NB = 512

RING = 12
UNIT = 2048

E = 64
GROUPS = 8
FF = 256
CAP = 64
SLOTS = 2 * S
TRASH = SLOTS + CAP
WIDE = TRASH + CAP
PER = 4
PASSES = S // CAP

HEADS = 8
ROT = 64
MLA_Q, MLA_KV, MLA_QK, NOPE = 384, 256, 192, 128
DFF = 2816
LAMBDA_INIT = 0.8 - 0.6 * math.exp(0.0)
WINDOW = 128
HYB_IN = 2312
SPAN = 3 * P

GATE_AT, UP_AT, DOWN_AT = (0, 1, 4, 5), (2, 3, 6, 7), (8, 9, 10, 11)


def shape_constants():
    pos = np.arange(S, dtype=np.float32)
    inv = (1.0 / (np.float32(10000.0) ** (np.arange(0, ROT, 2, dtype=np.float32) / np.float32(ROT)))).astype(np.float32)
    ang = pos[:, None] * inv[None, :]
    cos = np.concatenate([np.cos(ang), np.cos(ang)], 1)
    sin = np.concatenate([-np.sin(ang), np.sin(ang)], 1)
    rope = np.stack([cos, sin], 0).astype(np.float32)
    rope = rope.reshape(2, TT, P, ROT).transpose(2, 0, 1, 3).reshape(P, -1)
    q = np.arange(P)[:, None]
    k = np.arange(P)[None, :]
    tri = np.where(k <= q, 0.0, NEG)
    causal = np.concatenate([tri, np.zeros((P, P)), tri], 1)
    window = np.concatenate([tri, np.where(q + P - k < WINDOW, 0.0, NEG), tri], 1)
    dist = np.concatenate([q - k, q + P - k, q - k], 1)
    before = (np.arange(P)[:, None] < np.arange(P)[None, :]).astype(np.float32)
    upto = (np.arange(P)[:, None] <= np.arange(P)[None, :]).astype(np.float32)
    iota = np.tile(np.arange(SLOTS), (P, 1))
    parts = [np.eye(P), before, np.ones((P, P)), rope, causal, upto, window, dist, iota]
    return np.concatenate([p.astype(np.float32) for p in parts], 1)


KEPT = dict(ident=P, before=P, ones=P, rope=2 * TT * ROT, causal=SPAN)
LATER = dict(upto=P, window=SPAN, dist=SPAN, iota=SLOTS)


def build(nc, t, out):
    with ExitStack() as ctx:
        def sb(name, shape, dt=F32):
            return ctx.enter_context(nc.sbuf_tensor(name, shape, dt))

        class Signal:

            def __init__(self, handle, base=0):
                self.sem, self.base = handle, base

            def __call__(self, n):
                return self.sem, n + self.base

        def sem(name):
            return Signal(ctx.enter_context(nc.semaphore(name)))

        counted_up = {}

        def shared(kind, total):
            if kind not in counted_up:
                counted_up[kind] = [ctx.enter_context(nc.semaphore(kind)), 0]
            signal = Signal(*counted_up[kind])
            counted_up[kind][1] += total
            return signal

        X = sb("X", [P, TT, D])
        hn = sb("hn", [P, TT, D])
        hT = sb("hT", [P, DC, S])
        ring = sb("ring", [P, RING, UNIT])
        A = sb("A", [P, 8192])
        BC = sb("BC", [P, 10240])
        konst = sb("konst", [P, sum(KEPT.values())])
        pT = sb("pT", [P, 2, SPAN])
        stat = sb("stat", [P, 512])
        at = {}
        offset = 0
        for name, width in KEPT.items():
            at[name] = konst[:, offset:offset + width]
            offset += width
        ident, ones, before = at["ident"], at["ones"], at["before"]
        later = {}
        for name, width in LATER.items():
            later[name] = t["constants"][:, offset:offset + width]
            offset += width
        rope_tab = at["rope"].rearrange("p (a t d) -> p a t d", a=2, t=TT)

        gains = sb("gains", [P, 2, 2, DC])
        gains2 = sb("gains2", [P, 2, DC])
        small = sb("small", [P, 64])
        subln, mla_gain = small[:, 0:1], small[:, 1:8]
        ccol, csig = small[:, 8:16], small[:, 16:24]
        sinks = small[:, 24:32]
        f_bias = small[:, 32:40]
        lam = small[:, 40:44]
        cond_c = small[:, 44:52]
        router_w = A[:, 4608:4608 + DC * 72].rearrange("p (c n) -> p c n", c=DC)
        iota = A[:, 2560:2560 + SLOTS]
        router_b = sb("router_b", [P, 2, 72])
        qk_gain = sb("qk_gain", [P, 2, 192])
        gtab = sb("gtab", [P, 2, 2, TT, ROT])
        modc = sb("modc", [P, 4, DC])
        eb = pT[:, :, :].rearrange("p a s -> p (a s)")[:, 0:2 * FF].rearrange("p (b n) -> p b n", b=2)
        modrow = sb("modrow", [P, NB])
        pos_i = A[:, 7168:7168 + (PASSES + 1) * E].bitcast(I32)
        half = sb("half", [P, 16])

        bank = [ctx.enter_context(nc.psum_tensor(f"bank{i}", [P, NB], F32)) for i in range(8)]
        mod_dram = nc.dram_tensor("mod_scratch", (6 * D,), F32, kind="Internal").ap()

        loaded = sem("loaded")
        unit_full = [sem(f"unit_full{i}") for i in range(RING)]
        unit_done = sem("unit_done")
        dve_step, pool_step = sem("dve_step"), sem("pool_step")

        class Steps:

            def __init__(self, signal):
                self.count_sem, self.n, self.eng = signal, 0, None

            def done(self, ins):
                self.n += 1
                ins.then_inc(self.count_sem.sem, 1)
                self.eng.wait_ge(*self.count_sem(self.n))

        dv, po = Steps(dve_step), Steps(pool_step)

        units = []

        def plan(view, src):
            units.append((view, src))
            return len(units) - 1

        def slot(u):
            return ring[:, u % RING, :]

        def load_unit(sp, u):
            if u >= RING:
                sp.wait_ge(*unit_done(u - RING + 1))
            view, src = units[u]
            sp.dma_start(view(slot(u)), src).then_inc(unit_full[u % RING].sem, 16)

        def unit_here(pe, u):
            pe.wait_ge(*unit_full[u % RING](16 * (u // RING + 1)))

        class Stage:
            pass

        def norm_stage(tile_ready, gain, shift=None, extra=()):
            st = Stage()
            squares, rooted, scaled = shared("norm_squares", TT), shared("norm_rooted", TT), shared("norm_scaled", TT)
            turned, out_v, out_a = shared("norm_turned", TT), shared("norm_out_v", TT), shared("norm_out_a", TT)
            ssq, rstd = stat[:, 0:TT], stat[:, 2:2 + TT]

            def square(act, tt):
                tile_ready(act, tt)
                nc.scalar.activation(hn[:, tt, :], X[:, tt, :], ACT.Square,
                                     accum_out=ssq[:, tt:tt + 1]).then_inc(squares.sem, 1)

            def root(pool):
                for tt in range(TT):
                    pool.wait_ge(*squares(tt + 1))
                    ss, r = ssq[:, tt:tt + 1], rstd[:, tt:tt + 1]
                    po.done(nc.gpsimd.tensor_scalar(r, ss, 1.0 / D, EPS, ALU.mult, ALU.add))
                    nc.gpsimd.tensor_tensor(r, r, half[:, 0:1], ALU.pow).then_inc(rooted.sem, 1)

            def scale(dve, tt):
                tile_ready(dve, tt)
                dve.wait_ge(*rooted(tt + 1))
                nc.vector.tensor_scalar(hn[:, tt, :], X[:, tt, :], rstd[:, tt:tt + 1], None,
                                        ALU.mult).then_inc(scaled.sem, 1)

            def turn(pe, tt):
                pe.wait_ge(*scaled(tt + 1))
                for c in range(DC):
                    i = nc.tensor.transpose(bank[4 + 2 * tt + c // 4][:, (c % 4) * P:(c % 4 + 1) * P],
                                            hn[:, tt, c:D:DC], ident)
                i.then_inc(turned.sem, 1)

            def evac(eng, tt, scalar):
                for s, v in extra:
                    eng.wait_ge(*s(v))
                eng.wait_ge(*turned(tt + 1))
                for k in range(4):
                    c = k + 4 * scalar
                    dst, ps = hT[:, c, tt * P:(tt + 1) * P], bank[4 + 2 * tt + scalar][:, k * P:(k + 1) * P]
                    if scalar:
                        i = nc.scalar.activation(dst, ps, ACT.Identity, scale=gain[:, c:c + 1],
                                                 bias=shift[:, c:c + 1] if shift is not None else 0.0)
                    elif shift is None:
                        i = nc.vector.tensor_scalar(dst, ps, gain[:, c:c + 1], None, ALU.mult)
                    else:
                        i = nc.vector.tensor_scalar(dst, ps, gain[:, c:c + 1], shift[:, c:c + 1], ALU.mult, ALU.add)
                i.then_inc((out_a if scalar else out_v).sem, 1)

            def tile(pe, tt):
                if tt == 1:
                    turn(pe, 1)
                pe.wait_ge(*out_v(tt + 1))
                pe.wait_ge(*out_a(tt + 1))
            st.square, st.root, st.scale, st.turn, st.evac, st.tile = square, root, scale, turn, evac, tile
            st.rooted = rooted
            return st

        def close_tensor(pe, products, norm):
            for tt, nb in ((0, 0), (0, 1), (1, 0)):
                products.product(pe, tt, nb)
            norm.turn(pe, 0)
            products.product(pe, 1, 1)

        def close_vector(dve, products, norm):
            products.add(dve, 0, 0)
            products.add(dve, 0, 1)
            norm.scale(dve, 0)
            products.add(dve, 1, 0)
            norm.evac(dve, 0, 0)
            products.add(dve, 1, 1)
            norm.scale(dve, 1)
            norm.evac(dve, 1, 0)

        def close_scalar(act, norm):
            for tt in range(TT):
                norm.square(act, tt)
                norm.evac(act, tt, 1)

        def out_stage(blocks, lhs, add_to):
            st = Stage()
            summed, added = shared("block_summed", 2), shared("block_added", 2 * TT)

            def product(pe, tt, n):
                parts = blocks[n][1]
                seen = 0
                for u, view, cn, _ in parts:
                    unit_here(pe, u)
                    for c in range(cn):
                        i = nc.tensor.matmul(bank[2 * tt + n][:, :], lhs(seen + c, tt), view(slot(u))[:, c, :],
                                             start=(seen + c == 0), stop=(seen + c == DC - 1))
                    seen += cn
                    if tt == 1:
                        i.then_inc(unit_done.sem, 1)
                if tt == 0:
                    i.then_inc(summed.sem, 1)

            def add(dve, tt, n):
                if tt == 0:
                    dve.wait_ge(*summed(n + 1))
                else:
                    dve.wait_ge(*unit_done(blocks[n][1][-1][0] + 1))
                add_to(tt, n, bank[2 * tt + n][:, :]).then_inc(added.sem, 1)

            def ready(eng, tt):
                eng.wait_ge(*added(2 * (tt + 1)))
            st.product, st.add, st.ready = product, add, ready
            return st

        def project_stage(name, ready, lhs, blocks, evac, fold=None, sbanks=(0, 1, 2, 3)):
            st = Stage()
            copied = shared("product_copied", TT * len(blocks))

            def ps(n, tt):
                return bank[sbanks[2 * (n % 2) + tt]]

            def last_unit(n):
                return blocks[n][1][-1][0]

            def tensor(pe):
                for n, (w, parts) in enumerate(blocks):
                    if n >= 2:
                        pe.wait_ge(*copied(2 * (n - 1)))
                    total = sum(p[2] for p in parts)
                    for tiles in ([(0,), (1,)] if n == 0 else [(0, 1)]):
                        if n == 0:
                            ready(pe, tiles[0])
                        seen = 0
                        for u, view, cn, keep in parts:
                            unit_here(pe, u)
                            for tt in tiles:
                                for c in range(cn):
                                    i = nc.tensor.matmul(ps(n, tt)[:, 0:w], lhs(seen + c, tt), view(slot(u))[:, c, :],
                                                         start=(seen + c == 0), stop=(seen + c == total - 1))
                            seen += cn
                            if tiles[-1] == 1:
                                i.then_inc((unit_done if not keep else kept[0]).sem, 1)

            kept = [sem(name + "_kept")] if any(p[3] for b in blocks for p in b[1]) else [None]
            kept_of = {}
            count = 0
            for n, (w, parts) in enumerate(blocks):
                if parts[-1][3]:
                    count += 1
                    kept_of[n] = count

            def block_ready(eng, n):
                if n in kept_of:
                    eng.wait_ge(*kept[0](kept_of[n]))
                else:
                    eng.wait_ge(*unit_done(last_unit(n) + 1))

            def drain(eng):
                for n, (w, parts) in enumerate(blocks):
                    block_ready(eng, n)
                    for tt in range(TT):
                        evac(eng, n, tt, ps(n, tt)[:, 0:w]).then_inc(copied.sem, 1)
                    if fold:
                        fold(eng, n)
            st.tensor, st.drain, st.copied = tensor, drain, copied
            return st

        def square_units(w, ncols, order="(p c)", kc=DC, per=4, col0=0, nb=NB):
            src = w.rearrange("(p c) n -> p c n", c=kc) if order == "(p c)" else w.rearrange("(c p) n -> p c n", p=P)
            blocks = []
            for n0 in range(0, ncols, nb):
                wd = min(nb, ncols - n0)
                parts = []
                for c0 in range(0, kc, per):
                    cn = min(per, kc - c0)

                    def view(a, wd=wd, cn=cn):
                        return a[:, 0:cn * wd].rearrange("p (c n) -> p c n", c=cn)
                    u = plan(view, src[:, c0:c0 + cn, col0 + n0:col0 + n0 + wd])
                    parts.append((u, view, cn, False))
                blocks.append((wd, parts))
            return blocks

        def turn_stage(name, ready, jobs, scalar_only=False, fill_ready=None, bank0=4):
            st = Stage()
            fills = [jobs[i:i + 2] for i in range(0, len(jobs), 2)]
            by_scalar = [scalar_only or f % 2 == 1 for f in range(len(fills))]
            turned, out_v, out_a = (shared("turn_done", len(fills)), shared("turn_out_v", by_scalar.count(False)),
                                    shared("turn_out_a", by_scalar.count(True)))

            def left(eng, f):
                (eng.wait_ge(*(out_a if by_scalar[f] else out_v)(by_scalar[0:f + 1].count(by_scalar[f]))))

            def tensor(pe):
                ready(pe)
                for f, fill in enumerate(fills):
                    if f >= 2:
                        left(pe, f - 2)
                    if fill_ready:
                        fill_ready(pe, f)
                    for k, (src, w, dst, scale) in enumerate(fill):
                        for tt in range(TT):
                            i = nc.tensor.transpose(bank[bank0 + f % 2][0:w, k * S + tt * P:k * S + (tt + 1) * P],
                                                    src(tt), ident)
                    i.then_inc(turned.sem, 1)

            def evac(eng, scalar):
                for f, fill in enumerate(fills):
                    if by_scalar[f] != scalar:
                        continue
                    eng.wait_ge(*turned(f + 1))
                    for k, (src, w, dst, scale) in enumerate(fill):
                        ps = bank[bank0 + f % 2][0:w, k * S:(k + 1) * S]
                        if scalar and scale is not None:
                            i = nc.scalar.activation(dst, ps, ACT.Identity, scale=scale)
                        elif scalar:
                            i = nc.scalar.activation(dst, ps, ACT.Copy)
                        elif scale is not None:
                            i = nc.vector.tensor_scalar(dst, ps, scale, None, ALU.mult)
                        else:
                            i = nc.vector.tensor_copy(dst, ps)
                    i.then_inc((out_a if scalar else out_v).sem, 1)

            def vector(dve):
                evac(dve, False)

            def scalar(act):
                evac(act, True)

            def done(eng):
                eng.wait_ge(*out_v(by_scalar.count(False)))
                eng.wait_ge(*out_a(by_scalar.count(True)))
            st.tensor, st.vector, st.scalar, st.ready = tensor, vector, scalar, done
            return st

        SC = BC[:, 8192:8192 + 4 * SPAN].rearrange("p (b m s) -> p b m s", b=2, m=2)

        def attention_stage(name, ready, heads, scale, dv_w, bias, filler=None, mix=None, sink=False, squares=None):
            st = Stage()
            n = len(heads)
            maps = len(heads[0][0])
            scored, masked, maxed = (shared("head_scored", maps * n), shared("head_masked", maps * n),
                                     shared("head_maxed", n))
            exped, mixed, turned = (shared("head_exped", n), shared("head_mixed", n if mix else 0),
                                    shared("head_turned", n))
            copied, summed, stored = shared("head_copied", n), shared("head_summed", n), shared("head_stored", n)
            nmax = stat[:, 16:24].rearrange("p (b m t) -> p b m t", b=2, m=2)
            den = stat[:, 24:32].rearrange("p (b m t) -> p b m t", b=2, m=2)
            rden = stat[:, 32:40].rearrange("p (b m t) -> p b m t", b=2, m=2)
            dsink = stat[:, 40:44].rearrange("p (b t) -> p b t", b=2)
            obanks = 1 if mix else 2

            def obank(h):
                b = bank[6] if mix else bank[1 + 2 * (h % 2)]
                return b[:, 0:S].rearrange("p (t d) -> p t d", t=TT)
            ranges = [(0, P), (P, SPAN)]

            def tensor(pe):
                ready(pe)

                def score(h):
                    if h >= 2:
                        pe.wait_ge(*masked(maps * (h - 1)))
                    for m in range(maps):
                        ps = bank[(h % 2) * 2 + m]
                        pairs = heads[h][0][m]
                        for tt, (a, b) in enumerate(ranges):
                            for j, (q, k) in enumerate(pairs):
                                i = nc.tensor.matmul(ps[:, a:b], q(tt), k(0, b - a), start=(j == 0),
                                                     stop=(j == len(pairs) - 1))
                        i.then_inc(scored.sem, 1)

                def turn(h):
                    pe.wait_ge(*(mixed if mix else exped)(h + 1))
                    if h >= 2:
                        pe.wait_ge(*copied(h - 1))
                    for j in range(3):
                        i = nc.tensor.transpose(bank[4 + h % 2][:, j * P:(j + 1) * P],
                                                SC[:, h % 2, 0, j * P:(j + 1) * P], ident)
                    i.then_inc(turned.sem, 1)

                def sum_v(h):
                    pe.wait_ge(*copied(h + 1))
                    if h >= obanks:
                        pe.wait_ge(*stored(h - obanks + 1))
                    ps = obank(h)
                    v = heads[h][1]
                    p = pT[:, h % 2, :]
                    nc.tensor.matmul(ps[:, 0, :], p[:, 0:P], v(0), start=True, stop=True)
                    nc.tensor.matmul(ps[:, 1, :], p[:, P:2 * P], v(0), start=True, stop=False)
                    nc.tensor.matmul(ps[:, 1, :], p[:, 2 * P:SPAN], v(1), start=False,
                                     stop=True).then_inc(summed.sem, 1)
                score(0)
                score(1)
                for h in range(n):
                    if h + 2 < n:
                        score(h + 2)
                    if h >= 1:
                        sum_v(h - 1)
                    if filler:
                        filler.tensor(pe, h)
                    turn(h)
                sum_v(n - 1)

            def vector(dve):
                def mask(h):
                    if h >= 2:
                        dve.wait_ge(*turned(h - 1))
                    for m in range(maps):
                        ps = bank[(h % 2) * 2 + m][:, 0:SPAN]
                        b = bias(h, dve)
                        dve.wait_ge(*scored(maps * h + m + 1))
                        nc.vector.scalar_tensor_tensor(out=SC[:, h % 2, m, :], in0=ps, scalar=scale, in1=b,
                                                       op0=ALU.mult, op1=ALU.add).then_inc(masked.sem, 1)
                    dve.wait_ge(*masked(maps * (h + 1)))
                    for m in range(maps):
                        for tt, (a, b) in enumerate(ranges):
                            i = nc.vector.tensor_reduce(nmax[:, h % 2, m, tt:tt + 1], SC[:, h % 2, m, a:b], AX,
                                                        ALU.max, negate=True)
                    if sink and h < HEADS:
                        dv.done(i)
                        i = nc.vector.tensor_scalar(nmax[:, h % 2, 0, :], nmax[:, h % 2, 0, :], nsink[:, h:h + 1],
                                                    None, ALU.min)
                    i.then_inc(maxed.sem, 1)

                def weigh(h):
                    dve.wait_ge(*exped(h + 1))
                    if sink and h < HEADS:
                        dv.done(nc.vector.tensor_tensor(den[:, h % 2, 0, :], den[:, h % 2, 0, :], dsink[:, h % 2, :],
                                                        ALU.add))
                    if h >= 2:
                        dve.wait_ge(*stored(h - 1))
                    dv.done(nc.vector.reciprocal(rden[:, h % 2, 0:maps, :], den[:, h % 2, 0:maps, :]))
                    if mix:
                        dv.done(nc.vector.scalar_tensor_tensor(out=rden[:, h % 2, 1, :], in0=rden[:, h % 2, 1, :],
                                                               scalar=lam[:, 3:4], in1=den[:, h % 2, 0, :],
                                                               op0=ALU.mult, op1=ALU.mult))
                        for tt, (a, b) in enumerate(ranges):
                            i = nc.vector.scalar_tensor_tensor(out=SC[:, h % 2, 0, a:b], in0=SC[:, h % 2, 1, a:b],
                                                               scalar=rden[:, h % 2, 1, tt:tt + 1],
                                                               in1=SC[:, h % 2, 0, a:b], op0=ALU.mult, op1=ALU.add)
                        i.then_inc(mixed.sem, 1)

                def store(h):
                    dve.wait_ge(*summed(h + 1))
                    ps = obank(h)
                    col = dv_w * heads[h][3]
                    for tt in range(TT):
                        i = nc.vector.tensor_scalar(heads[h][2](tt), ps[:, tt, col:col + dv_w],
                                                    rden[:, h % 2, 0, tt:tt + 1], None, ALU.mult)
                    i.then_inc(stored.sem, 1)
                mask(0)
                for h in range(n + 1):
                    if h + 1 < n:
                        mask(h + 1)
                    if h < n:
                        weigh(h)
                    if h >= 1:
                        store(h - 1)

            def scalar(act):
                def exps(h):
                    act.wait_ge(*maxed(h + 1))
                    for m in range(maps):
                        for tt, (a, b) in enumerate(ranges):
                            i = nc.scalar.activation(SC[:, h % 2, m, a:b], SC[:, h % 2, m, a:b], ACT.Exp,
                                                     bias=nmax[:, h % 2, m, tt:tt + 1],
                                                     accum_out=den[:, h % 2, m, tt:tt + 1])
                    if sink and h < HEADS:
                        for tt in range(TT):
                            i = nc.scalar.activation(dsink[:, h % 2, tt:tt + 1], sinks[:, h:h + 1], ACT.Exp,
                                                     bias=nmax[:, h % 2, 0, tt:tt + 1])
                    i.then_inc(exped.sem, 1)

                def copy(h):
                    act.wait_ge(*turned(h + 1))
                    if h >= 2:
                        act.wait_ge(*summed(h - 1))
                    nc.scalar.activation(pT[:, h % 2, :], bank[4 + h % 2][:, 0:SPAN], ACT.Copy).then_inc(copied.sem, 1)
                exps(0)
                for h in range(n):
                    if h + 1 < n:
                        exps(h + 1)
                    if filler:
                        filler.scalar(act, h)
                    copy(h)
                    if squares and h >= 1:
                        act.wait_ge(*stored(h))
                        squares(act, h - 1)
                if squares:
                    act.wait_ge(*stored(n))
                    squares(act, n - 1)

            def done(eng):
                eng.wait_ge(*stored(n))
            st.tensor, st.vector, st.scalar, st.ready, st.masked = tensor, vector, scalar, done, masked
            return st

        n_loaded = [0]

        def start_sync(sp):
            def ld(dst, src, signal=loaded):
                sp.dma_start(dst, src).then_inc(signal.sem, 16)
                if signal is loaded:
                    n_loaded[0] += 16
            x = t["x"][0].rearrange("(t p) d -> p t d", p=P)
            for tt in range(TT):
                ld(X[:, tt, :], x[:, tt, :], x_in[tt])
            ld(ident, t["constants"][:, 0:P], first)
            ld(gains[:, 0, :, :], t["attn_norm"].rearrange("l (p c) -> p l c", c=DC), first)
            ld(gains[:, 1, :, :], t["ffn_norm"].rearrange("l (p c) -> p l c", c=DC), first)
            for u in range(4):
                load_unit(sp, u)
            ld(konst[:, P:], t["constants"][:, P:sum(KEPT.values())])
            ld(BC[:, 384:384 + ROT], t["diff_q_norm"][0].partition_broadcast(P))
            ld(BC[:, 448:448 + ROT], t["diff_k_norm"][0].partition_broadcast(P))
            for k, name in enumerate(("q1", "k1", "q2", "k2")):
                ld(BC[:, k * ROT:(k + 1) * ROT], t["diff_lambda_" + name][0].partition_broadcast(P))
            ld(ccol, t["c_2"].rearrange("a (p c) -> p (a c)", c=DC))
            ld(subln, t["diff_subln"].rearrange("a p -> p a"))
            ld(sinks, t["sinks_2"].partition_broadcast(P))
            ld(qk_gain[:, 0, :], t["mla_q_norm"][0].partition_broadcast(P))
            ld(qk_gain[:, 1, :], t["mla_k_norm"][0].partition_broadcast(P))
            ld(mla_gain[:, 0:3], t["mla_q_a_norm"].rearrange("a (p c) -> p (a c)", c=3))
            ld(mla_gain[:, 3:5], t["mla_kv_a_norm"].rearrange("a (p c) -> p (a c)", c=2))
            ld(mla_gain[:, 5:6], t["mla_q_norm"][0:1, 0:NOPE].rearrange("a p -> p a"))
            ld(mla_gain[:, 6:7], t["mla_k_norm"][0:1, 0:NOPE].rearrange("a p -> p a"))
            for layer in range(2):
                ld(router_b[:, layer, 0:GROUPS], t["moe_b_group"][layer].partition_broadcast(P))
                ld(router_b[:, layer, GROUPS:], t["moe_b_expert"][layer].partition_broadcast(P))
            ld(gains2[:, 0, :], t["g_attn_2"].rearrange("(p c) -> p c", c=DC))
            ld(gains2[:, 1, :], t["g_mlp_2"].rearrange("(p c) -> p c", c=DC))
            ld(f_bias, t["b_f_2"].partition_broadcast(P))
            assert n_loaded[0] == N_SMALL

        N_SMALL = 16 * 23
        first = sem("first")
        N_FIRST = 16 * 3
        x_in = [sem(f"x_in{tt}") for tt in range(TT)]

        w_in = t["diff_w_in"][0]
        in_blocks = square_units(w_in, 3072)
        set_up = sem("set_up")
        lam_exp = sem("lam_exp")
        lam_dot = sem("lam_dot")

        def have_small(eng):
            eng.wait_ge(*loaded(N_SMALL))

        n1 = norm_stage(lambda eng, tt: eng.wait_ge(*x_in[tt](16)), gains[:, 0, 0, :], extra=[(first, N_FIRST)])
        qkv = A[:, 0:TT * 3072].rearrange("p (t n) -> p t n", t=TT)

        def setup_vector(dve):
            have_small(dve)
            l = BC[:, 0:4 * ROT].rearrange("p (k d) -> p k d", k=4)
            pr = BC[:, 4 * ROT:6 * ROT].rearrange("p (k d) -> p k d", k=2)
            for k in range(2):
                dv.done(nc.vector.tensor_tensor(pr[:, k, :], l[:, 2 * k, :], l[:, 2 * k + 1, :], ALU.mult))
            nc.vector.tensor_reduce(lam[:, 0:2], pr, AX, ALU.add).then_inc(lam_dot.sem, 1)
            fold_rope(0)
            dve.wait_ge(*lam_exp(2))
            dv.done(nc.vector.tensor_tensor(lam[:, 2:3], lam[:, 1:2], lam[:, 0:1], ALU.subtract))
            dv.done(nc.vector.tensor_scalar(lam[:, 3:4], lam[:, 2:3], -LAMBDA_INIT, None, ALU.add))
            dv.done(nc.vector.tensor_scalar(csig, csig, 1.0, None, ALU.add))
            dv.done(nc.vector.reciprocal(csig, csig))
            dv.done(nc.vector.tensor_scalar(subln, subln, 1.0 - LAMBDA_INIT, None, ALU.mult))
            dv.done(nc.vector.tensor_scalar(nsink, sinks, -1.0, None, ALU.mult))
            nc.vector.tensor_tensor(cond_c, ccol, csig, ALU.mult).then_inc(set_up.sem, 1)

        nsink = stat[:, 48:56]

        def fold_rope(which):
            for qk in range(2):
                g = BC[:, 384 + 64 * qk:448 + 64 * qk] if which == 0 else qk_gain[:, qk, NOPE:MLA_QK]
                for tt in range(TT):
                    dv.done(nc.vector.tensor_tensor(gtab[:, qk, 0, tt, :], rope_tab[:, 0, tt, :], g, ALU.mult))
                    dv.done(nc.vector.tensor_tensor(gtab[:, qk, 1, tt, 0:32], rope_tab[:, 1, tt, 0:32], g[:, 32:64],
                                                    ALU.mult))
                    dv.done(nc.vector.tensor_tensor(gtab[:, qk, 1, tt, 32:64], rope_tab[:, 1, tt, 32:64], g[:, 0:32],
                                                    ALU.mult))

        def setup_scalar(act):
            have_small(act)
            act.wait_ge(*lam_dot(1))
            nc.scalar.activation(lam[:, 0:2], lam[:, 0:2], ACT.Exp).then_inc(lam_exp.sem, 1)
            nc.scalar.activation(csig, ccol, ACT.Exp, scale=-1.0).then_inc(lam_exp.sem, 1)

        def copy_qkv(eng, n, tt, ps):
            return nc.scalar.activation(qkv[:, tt, n * NB:(n + 1) * NB], ps, ACT.Copy)

        p1_sq, p1_ss, p1_rs = sem("p1_sq"), sem("p1_ss"), sem("p1_rs")
        sq1 = hn[:, 0, :].rearrange("p (b n) -> p b n", b=2)
        rot1 = hn[:, 1, :].rearrange("p (b n) -> p b n", b=2)

        def square_qk(act, n):
            if n >= 4:
                return
            for tt in range(TT):
                j = 2 * n + tt
                act.wait_ge(*p1.copied(j + 1))
                if j >= 2:
                    act.wait_ge(*p1_ss(j - 1))
                nc.scalar.activation(sq1[:, j % 2, :], qkv[:, tt, n * NB:(n + 1) * NB],
                                     ACT.Square).then_inc(p1_sq.sem, 1)

        p1 = project_stage("p1", n1.tile, lambda c, tt: hT[:, c, tt * P:(tt + 1) * P], in_blocks, copy_qkv,
                           square_qk)

        def rotate(dve, x, g, w, n_groups, qk, tt, t1, t2):
            cs = gtab[:, qk, 0, tt, :].unsqueeze(1).broadcast_to([P, n_groups, ROT])
            sn0 = gtab[:, qk, 1, tt, 0:32].unsqueeze(1).broadcast_to([P, n_groups, 32])
            sn1 = gtab[:, qk, 1, tt, 32:64].unsqueeze(1).broadcast_to([P, n_groups, 32])
            nc.vector.tensor_tensor(t1, x, cs, ALU.mult)
            nc.vector.tensor_tensor(t2[:, :, 0:32], x[:, :, 32:64], sn0, ALU.mult)
            dv.done(nc.vector.tensor_tensor(t2[:, :, 32:64], x[:, :, 0:32], sn1, ALU.mult))
            dv.done(nc.vector.tensor_tensor(t1, t1, t2, ALU.add))

        p1_qk = sem("p1_qk")

        def rope_vector(dve):
            for n in range(4):
                for tt in range(TT):
                    j = 2 * n + tt
                    x = qkv[:, tt, n * NB:(n + 1) * NB].rearrange("p (g d) -> p g d", d=ROT)
                    dve.wait_ge(*p1_sq(j + 1))
                    nc.vector.tensor_reduce(stat[:, 64 + 8 * (j % 2):72 + 8 * (j % 2)],
                                            sq1[:, j % 2, :].rearrange("p (g d) -> p g d", d=ROT), AX,
                                            ALU.add).then_inc(p1_ss.sem, 1)
                    t1 = rot1[:, 0, :].rearrange("p (g d) -> p g d", d=ROT)
                    t2 = rot1[:, 1, :].rearrange("p (g d) -> p g d", d=ROT)
                    rotate(dve, x, None, ROT, 8, n // 2, tt, t1, t2)
                    dve.wait_ge(*p1_rs(j + 1))
                    r = stat[:, 80 + 8 * (j % 2):88 + 8 * (j % 2)].unsqueeze(2).broadcast_to([P, 8, ROT])
                    dv.done(nc.vector.tensor_tensor(x, t1, r, ALU.mult))
            nc.vector.tensor_copy(stat[:, 8:9], stat[:, 64:65]).then_inc(p1_qk.sem, 1)

        def rope_gpsimd(pool):
            for j in range(8):
                pool.wait_ge(*p1_ss(j + 1))
                a, b = 64 + 8 * (j % 2), 80 + 8 * (j % 2)
                po.done(nc.gpsimd.tensor_scalar(stat[:, 96:104], stat[:, a:a + 8], 1.0 / ROT, EPS, ALU.mult, ALU.add))
                nc.gpsimd.tensor_tensor(stat[:, b:b + 8], stat[:, 96:104], half[:, 0:8], ALU.pow).then_inc(p1_rs.sem, 1)

        qkT = BC[:, 0:8192].rearrange("p (j s) -> p j s", s=S)
        jobs = []
        for h in range(HEADS):
            for qk in range(2):
                jobs.append((lambda tt, c0=qk * D + h * P: qkv[:, tt, c0:c0 + P], P, qkT[:, 2 * h + qk, :], None))

        def t1_ready(pe):
            pe.wait_ge(*p1_qk(1))
        t1 = turn_stage("t1", t1_ready, jobs)

        class Conditioning:

            def __init__(self, g0, g1, heads):
                w = t["w_ada_2"].rearrange("(p c) n -> p c n", c=DC)
                total = g1 - g0
                self.jobs = [[] for _ in range(heads)]
                self.copied = shared("mod_copied", total)
                self.stored = shared("mod_stored", 16 * total)
                self.total, self.g0 = total, g0
                for k in range(total * DC):
                    g, c = g0 + k // DC, k % DC
                    u = plan(lambda a: a, w[:, c, g * UNIT:(g + 1) * UNIT])
                    self.jobs[k * heads // (total * DC)].append((g, c, u))

            def tensor(self, pe, h):
                for g, c, u in self.jobs[h]:
                    if c == 0 and g > self.g0:
                        pe.wait_ge(*self.copied(g - self.g0))
                    unit_here(pe, u)
                    for q in range(4):
                        i = nc.tensor.matmul(bank[7][32 * q:32 * q + 32, :], cond_c[:, c:c + 1].broadcast_to([P, 32]),
                                             slot(u)[:, q * NB:(q + 1) * NB], start=(c == 0), stop=(c == DC - 1))
                    i.then_inc(unit_done.sem, 1)

            def scalar(self, act, h):
                for g, c, u in self.jobs[h]:
                    if c < DC - 1:
                        continue
                    j = g - self.g0
                    act.wait_ge(*unit_done(u + 1))
                    if g > 0:
                        act.wait_ge(*self.stored(16 * j))
                    nc.scalar.activation(modrow[:, :], bank[7][:, :], ACT.Copy).then_inc(self.copied.sem, 1)
                    act.wait_ge(*self.copied(j + 1))
                    act.dma_start(mod_dram[g * UNIT:(g + 1) * UNIT].rearrange("(q n) -> q n", q=4),
                                  modrow[0:P:32, :]).then_inc(self.stored.sem, 16)

            def bank_read(self, eng):
                eng.wait_ge(*self.copied(self.total))

            def ready(self, eng):
                eng.wait_ge(*self.stored(16 * self.total))

        cond1 = Conditioning(0, 1, HEADS)

        def diff_head(h):
            def part(m):
                a, b = m * ROT, (m + 1) * ROT
                return [(lambda tt: qkT[a:b, 2 * h, tt * P:(tt + 1) * P], lambda k0, k1: qkT[a:b, 2 * h + 1, k0:k1])]
            return ([part(0), part(1)], lambda kt: qkv[:, kt, 2 * D + h * P:2 * D + (h + 1) * P],
                    lambda tt: hn[:, tt, h * P:(h + 1) * P], 0)

        n_sq, n_rs, n_out = sem("sub_sq"), sem("sub_rs"), sem("sub_out")
        sub_sq = BC[:, 9728:9728 + TT * P].rearrange("p (t d) -> p t d", t=TT)

        def a1_ready(pe):
            t1.ready(pe)
            pe.wait_ge(*set_up(1))
            pe.wait_ge(*p1.copied(12))
        def sub_squares(act, h):
            if h:
                act.wait_ge(*n_sq(h))
            for tt in range(TT):
                i = nc.scalar.activation(sub_sq[:, tt, :], hn[:, tt, h * P:(h + 1) * P], ACT.Square,
                                         accum_out=stat[:, 64 + 8 * tt + h:65 + 8 * tt + h])
            i.then_inc(n_sq.sem, 1)
        a1 = attention_stage("a1", a1_ready, [diff_head(h) for h in range(HEADS)], ROT ** -0.5, P,
                             lambda h, dve: at["causal"], filler=cond1, mix=True, squares=sub_squares)

        def sub_vector(dve):
            o = hn[:, :, :].rearrange("p t (h d) -> p t h d", d=P)
            r = stat[:, 80:96].rearrange("p (t h) -> p t h", t=TT)
            for h in range(0, HEADS, 2):
                dve.wait_ge(*n_rs(h + 2))
                nc.vector.tensor_tensor(o[:, :, h:h + 2, :], o[:, :, h:h + 2, :],
                                        r[:, :, h:h + 2].unsqueeze(3).broadcast_to([P, TT, 2, P]),
                                        ALU.mult).then_inc(n_out.sem, 1)

        def sub_gpsimd(pool):
            for h in range(HEADS):
                pool.wait_ge(*n_sq(h + 1))
                ss = stat[:, 64 + h:80:8]
                po.done(nc.gpsimd.tensor_scalar(ss, ss, 1.0 / P, EPS, ALU.mult, ALU.add))
                nc.gpsimd.tensor_tensor(stat[:, 80 + h:96:8], ss, half[:, 0:TT], ALU.pow).then_inc(n_rs.sem, 1)

        def heads_turned(name, ready, scale=None, fill_ready=None):
            return turn_stage(name, ready, [(lambda tt, c=c: hn[:, tt, c * P:(c + 1) * P], P, hT[:, c, :], scale)
                                            for c in range(DC)], fill_ready=fill_ready)
        t2 = heads_turned("t2", a1.ready, subln, lambda pe, f: pe.wait_ge(*n_out(f + 1)))

        def add_x(tt, n, ps):
            xs = X[:, tt, n * NB:(n + 1) * NB]
            return nc.vector.tensor_tensor(xs, xs, ps, ALU.add)

        def hT_lhs(c, tt):
            return hT[:, c, tt * P:(tt + 1) * P]
        o1 = out_stage(square_units(t["diff_w_out"][0], D, order="(c p)"), hT_lhs, add_x)

        def moe(layer, name, x_ready, x_free, filler, after_norm=None):
            st = Stage()
            pairs = E // 2
            nrm = norm_stage(x_ready, gains[:, 1, layer, :])
            st.norm = nrm
            table_in, logits, gexp, gexp_in = (shared("table_in", 48), shared("logits", 1), shared("gexp", 2),
                                               shared("gexp_in", 1))
            picked, counted, placed, gathered = (shared("picked", 1), shared("counted", 1), shared("placed", 1),
                                                 shared("gathered", DC))
            positioned = shared("positioned", 1)
            gather_banks = (0, 1, 2, 3, 6, 7)
            spread, spread_a = shared("spread_v", DC // 2), shared("spread_a", DC // 2)
            cwt_ready, cw_turned, cw_ready = shared("cwt_ready", 1), shared("cw_turned", 1), shared("cw_ready", 1)
            exped, hid_ready, h_turned = (shared("gate_exped", pairs), shared("hid_ready", pairs),
                                          shared("hid_turned", pairs))
            x_ready_, hT_ready = shared("tokens_ready", pairs + 2), shared("hidT_ready", pairs)
            rows_v, rows_a, rows_turned = shared("rows_v", pairs), shared("rows_a", pairs), shared("rows_turned", pairs)
            first_stored, pair_stored = shared("first_stored", pairs), shared("pair_stored", pairs + 1)
            y_turned, y_out_v, y_out_a = shared("y_turned", 8), shared("y_out_v", 4), shared("y_out_a", 4)
            summed, added, vstep = shared("moe_summed", 4), shared("moe_added", 4), shared("hidden_step", 3 * pairs)
            f_full, f_up = sem(name + "_f_full"), sem(name + "_f_up")
            f_exp, f_hid = sem(name + "_f_exp"), sem(name + "_f_hid")
            f_down, f_stored, f_v = sem(name + "_f_down"), sem(name + "_f_stored"), sem(name + "_f_v")
            f_x, f_turned, f_hT = sem(name + "_f_x"), sem(name + "_f_turned"), sem(name + "_f_hT")
            f_rows, f_rturned = sem(name + "_f_rows"), sem(name + "_f_rturned")

            gate_w, up_w, down_w = (t["moe_w_gate"][layer], t["moe_w_up"][layer], t["moe_w_down"][layer])
            base = len(units)
            for _ in range(3 * E):
                units.append(None)
            xsT = BC[:, 0:DC * WIDE].rearrange("p (c s) -> p c s", c=DC)
            ysT = BC[:, DC * WIDE:2 * DC * WIDE].rearrange("p (c s) -> p c s", c=DC)
            place = A[:, 0:TT * SLOTS].rearrange("p (t s) -> p t s", t=TT)
            cwt = A[:, 1024:1024 + TT * SLOTS].rearrange("p (t s) -> p t s", t=TT)
            tmp = A[:, 2048:2560]
            cw = A[:, 6144:6144 + 4 * S].rearrange("p (b s) -> p b s", b=4)
            ys = A[:, 0:4 * D].rearrange("p (b n) -> p b n", b=4)
            lg = A[:, 3072:3072 + TT * 72].rearrange("p (t n) -> p t n", t=TT)
            oh = A[:, 3328:3328 + 2 * TT * E].rearrange("p (k t e) -> p k t e", k=2, t=TT)
            both = A[:, 3584:3584 + TT * E].rearrange("p (t e) -> p t e", t=TT)
            cnt = A[:, 3776:3840]
            off = A[:, 3840:3904]
            cum = A[:, 3904:3968]
            posf = A[:, 4096:4096 + (PASSES + 1) * E].rearrange("p (j e) -> p j e", j=PASSES + 1)
            hid = A[:, 7488:7488 + 2 * FF].rearrange("p (b n) -> p b n", b=2)
            hidT = gtab[:, :, :, :, :].rearrange("p a b t d -> p (a b t d)")[:, 0:2 * 2 * P].rearrange(
                "p (b c n) -> p b c n", b=2, c=2)
            xg = hT[:, :, :].rearrange("p c s -> p (c s)").rearrange("p (b c n) -> p b c n", b=2, c=DC)
            yrow = hn[:, :, :]
            turn_banks = ((6, 7), (4, 5))

            w = A[:, 3968:4096]
            top, slot_of = w[:, 48:50], w[:, 52:56].rearrange("p (k t) -> p k t", k=2)
            equal, seen, e_logits = (w[:, a:a + 16].rearrange("p (t e) -> p t e", t=TT) for a in (0, 16, 32))
            chosen = w[:, 64:80].rearrange("p (t e) -> p t e", t=TT)
            group = w[:, 80:96].rearrange("p (t e) -> p t e", t=TT)
            g_dist = w[:, 96:112].rearrange("p (t e) -> p t e", t=TT)
            e_dist, g_sum, weight_1, weight_2 = (w[:, a:a + 2] for a in (112, 114, 116, 118))
            e_top = w[:, 120:124].rearrange("p (k t) -> p k t", k=2)
            masked = tmp[:, 0:2 * E].rearrange("p (t g e) -> p t g e", t=TT, g=GROUPS)

            def first_of(dst, values, top):
                dv.done(nc.vector.tensor_reduce(top, values, AX, ALU.max))
                dv.done(nc.vector.tensor_tensor(equal, values, top.unsqueeze(2).broadcast_to([P, TT, 8]), ALU.is_equal))
                dv.done(nc.vector.tensor_tensor_scan(w[:, 16:32], restart, w[:, 0:16], 0.0, ALU.mult, ALU.add))
                dv.done(nc.vector.scalar_tensor_tensor(out=dst, in0=seen, scalar=1.0, in1=equal,
                                                       op0=ALU.is_equal, op1=ALU.mult))

            def tensor(pe):
                pe.wait_ge(*table_in(48))
                for tt in range(TT):
                    nrm.tile(pe, tt)
                    for c in range(DC):
                        i = nc.tensor.matmul(bank[0][:, tt * 72:(tt + 1) * 72], hT_lhs(c, tt),
                                             router_w[:, c, :], start=(c == 0), stop=(c == DC - 1))
                i.then_inc(logits.sem, 1)
                filler.tensor(pe, 0)
                pe.wait_ge(*picked(1))
                nc.tensor.matmul(bank[1][:, 0:E], before, both[:, 0, :], start=True, stop=True)
                nc.tensor.matmul(bank[1][:, E:2 * E], ones, both[:, 0, :], start=True, stop=False)
                nc.tensor.matmul(bank[1][:, E:2 * E], before, both[:, 1, :], start=False, stop=True)
                nc.tensor.matmul(bank[1][:, 2 * E:3 * E], ones, both[:, 0, :], start=True, stop=False)
                nc.tensor.matmul(bank[1][:, 2 * E:3 * E], ones, both[:, 1, :], start=False,
                                 stop=True).then_inc(counted.sem, 1)

                def turn_weights():
                    pe.wait_ge(*cwt_ready(1))
                    for b in range(4):
                        for tt in range(TT):
                            i = nc.tensor.transpose(bank[4 + b // 2][:, (b % 2) * S + tt * P:(b % 2) * S + (tt + 1) * P],
                                                    cwt[:, tt, b * P:(b + 1) * P], ident)
                    i.then_inc(cw_turned.sem, 1)

                filler.tensor(pe, 1)
                pe.wait_ge(*placed(1))
                for c in range(DC):
                    if c == 5:
                        filler.bank_read(pe)
                    if c == 6:
                        turn_weights()
                    if c >= 6:
                        pe.wait_ge(*(spread if c % 2 == 0 else spread_a)((c - 6) // 2 + 1))
                    for tt in range(TT):
                        i = nc.tensor.matmul(bank[gather_banks[c % 6]][:, :], hn[:, tt, c:D:DC], place[:, tt, :],
                                             start=(tt == 0), stop=(tt == TT - 1))
                    i.then_inc(gathered.sem, 1)
                pe.wait_ge(*cw_ready(1))
                pe.wait_ge(*spread(4))
                pe.wait_ge(*spread_a(4))

                def gate_up(k, experts):
                    ps = bank[4 + k]
                    for part in range(2):
                        ws = [slots[part].rearrange("p (c f) -> p c f", c=DC) for slots in experts]
                        for c in range(DC):
                            for q, w in enumerate(ws):
                                i = nc.tensor.matmul(ps[q * CAP:(q + 1) * CAP, part * FF:(part + 1) * FF],
                                                     xg[:, k, c, q * CAP:(q + 1) * CAP], w[:, c, :],
                                                     start=(c == 0), stop=(c == DC - 1))
                        yield i

                def turn_hidden(k, rows):
                    for c in range(2):
                        i = nc.tensor.transpose(bank[6][:, c * P:c * P + rows], hid[0:rows, k, c:FF:2],
                                                ident[0:rows, 0:rows])
                    return i

                def down(k, experts):
                    ws = [w.rearrange("p (c n) -> p c n", c=2) for w in experts]
                    for nb in range(2):
                        for c in range(2):
                            for q, w in enumerate(ws):
                                i = nc.tensor.matmul(bank[2 * k + nb][q * CAP:(q + 1) * CAP, :],
                                                     hidT[:, k, c, q * CAP:(q + 1) * CAP],
                                                     w[:, c, nb * NB:(nb + 1) * NB], start=(c == 0), stop=(c == 1))
                    return i

                def turn_rows(k, rows):
                    for m in range(DC):
                        i = nc.tensor.transpose(bank[turn_banks[k][m // 4]][:, (m % 4) * P:(m % 4) * P + rows],
                                                yrow[0:rows, k, m * P:(m + 1) * P], ident[0:rows, 0:rows])
                    return i

                with pe.Fori(0, E // PER) as turn:
                    def here(k):
                        u = base + k
                        pe.wait_ge(*unit_full[u % RING](turn * 16 + 16 * (u // RING + 1)))

                    for k in range(2):
                        pe.wait_ge(*x_ready_(turn * 2 + k + 1))
                        if k == 0:
                            pe.wait_ge(*pair_stored(turn * 2 + 1))
                        g = gate_up(k, [(slot(base + GATE_AT[2 * k + q]), slot(base + UP_AT[2 * k + q]))
                                        for q in range(2)])
                        here(GATE_AT[2 * k])
                        here(GATE_AT[2 * k + 1])
                        next(g).then_inc(unit_done.sem, 2)
                        here(UP_AT[2 * k])
                        here(UP_AT[2 * k + 1])
                        next(g).then_inc(unit_done.sem, 2)
                    for k in range(2):
                        pe.wait_ge(*hid_ready(turn * 2 + k + 1))
                        turn_hidden(k, P).then_inc(h_turned.sem, 1)
                        pe.wait_ge(*hT_ready(turn * 2 + k + 1))
                        here(DOWN_AT[2 * k])
                        here(DOWN_AT[2 * k + 1])
                        down(k, [slot(base + DOWN_AT[2 * k + q]) for q in range(2)]).then_inc(unit_done.sem, 2)
                    for k in range(2):
                        pe.wait_ge(*rows_v(turn * 2 + k + 1))
                        pe.wait_ge(*rows_a(turn * 2 + k + 1))
                        turn_rows(k, P).then_inc(rows_turned.sem, 1)

                over = pe.value_load(pos_i[0:1, PASSES * E:PASSES * E + 1], min_val=0, max_val=S)
                pe.wait_ge(*pair_stored(E // 2 + 1))
                with pe.If(over > CAP):
                    with pe.Fori(0, (PASSES - 1) * E) as n:
                        pe.wait_ge(*f_x(n + 1))
                        pe.wait_ge(*f_full(n * 48 + 48))
                        g = gate_up(0, [(A[:, 0:2048], A[:, 2048:4096])])
                        next(g)
                        next(g).then_inc(f_up.sem, 1)
                        pe.wait_ge(*f_hid(n + 1))
                        turn_hidden(0, P).then_inc(f_turned.sem, 1)
                        pe.wait_ge(*f_hT(n + 1))
                        down(0, [A[:, 4096:6144]]).then_inc(f_down.sem, 1)
                        pe.wait_ge(*f_rows(n + 1))
                        turn_rows(0, P).then_inc(f_rturned.sem, 1)
                    pe.wait_ge(*f_stored((PASSES - 1) * E + 1))
                for b in range(4):
                    for hf in range(2):
                        j = 2 * b + hf
                        if j >= 2:
                            pe.wait_ge(*(y_out_v if j % 2 == 0 else y_out_a)(j // 2))
                        for m in range(4):
                            i = nc.tensor.transpose(bank[4 + j % 2][:, m * P:(m + 1) * P],
                                                    ysT[:, 4 * hf + m, b * P:(b + 1) * P], ident)
                        i.then_inc(y_turned.sem, 1)
                pe.wait_ge(*y_out_v(4))
                pe.wait_ge(*y_out_a(4))

            def product(pe, tt, nb):
                for b in range(4):
                    i = nc.tensor.matmul(bank[2 * tt + nb][:, :], cw[:, b, tt * P:(tt + 1) * P],
                                         ys[:, b, nb * NB:(nb + 1) * NB], start=(b == 0), stop=(b == 3))
                i.then_inc(summed.sem, 1)

            def add(dve, tt, nb):
                dve.wait_ge(*summed(2 * tt + nb + 1))
                xs = X[:, tt, nb * NB:(nb + 1) * NB]
                nc.vector.tensor_tensor(xs, xs, bank[2 * tt + nb][:, :], ALU.add).then_inc(added.sem, 1)

            zero64, restart = stat[:, 448:512], stat[:, 432:448]

            def vector(dve):
                have_small(dve)
                nc.vector.memset(zero64, 0.0)
                nc.vector.memset(xsT[:, :, SLOTS:WIDE], 0.0)
                dv.done(nc.vector.memset(restart, 1.0))
                dv.done(nc.vector.memset(restart[:, 0:16:8], 0.0))
                dve.wait_ge(*table_in(48))
                dve.wait_ge(*logits(1))
                dv.done(nc.vector.tensor_tensor(lg, bank[0][:, 0:TT * 72].rearrange("p (t n) -> p t n", t=TT),
                                                router_b[:, layer, :].unsqueeze(1).broadcast_to([P, TT, 72]), ALU.add))
                first_of(group, lg[:, :, 0:8], top)
                g4 = group.unsqueeze(3).broadcast_to([P, TT, 8, 8])
                dv.done(nc.vector.tensor_tensor(masked, lg[:, :, 8:72].rearrange("p t (g e) -> p t g e", g=8), g4,
                                                ALU.mult))
                dv.done(nc.vector.tensor_reduce(e_logits, masked.rearrange("p t g e -> p t e g"), AX, ALU.add))
                for k in range(2):
                    if k == 1:
                        dv.done(nc.vector.scalar_tensor_tensor(out=e_logits, in0=chosen, scalar=-3e38,
                                                               in1=e_logits, op0=ALU.mult, op1=ALU.add))
                    first_of(chosen, e_logits, e_top[:, k, :])
                    dv.done(nc.vector.tensor_tensor(oh[:, k, :, :].rearrange("p t (g e) -> p t g e", g=8), g4,
                                                    chosen.unsqueeze(2).broadcast_to([P, TT, 8, 8]), ALU.mult))
                nc.vector.tensor_tensor(both, oh[:, 0, :, :], oh[:, 1, :, :], ALU.add).then_inc(picked.sem, 1)
                nc.vector.tensor_tensor(g_dist, lg[:, :, 0:8], top.unsqueeze(2).broadcast_to([P, TT, 8]), ALU.subtract)
                nc.vector.tensor_tensor(e_dist, e_top[:, 1, :], e_top[:, 0, :], ALU.subtract).then_inc(gexp_in.sem, 1)
                dve.wait_ge(*counted(1))
                dv.done(nc.vector.tensor_copy(cnt, bank[1][:, 2 * E:3 * E]))
                dv.done(nc.vector.tensor_tensor_scan(cum, cnt, zero64, 0.0, ALU.add, ALU.add))
                dv.done(nc.vector.tensor_tensor(off, cum, cnt, ALU.subtract))
                place_in = tmp[:, 0:2 * E].rearrange("p (t e) -> p t e", t=TT)
                of_choice = tmp[:, 2 * E:6 * E].rearrange("p (k t e) -> p k t e", k=2, t=TT)
                dv.done(nc.vector.tensor_tensor(place_in, bank[1][:, 0:2 * E].rearrange("p (t e) -> p t e", t=TT),
                                                off.unsqueeze(1).broadcast_to([P, TT, E]), ALU.add))
                dv.done(nc.vector.tensor_tensor(of_choice, oh, place_in.unsqueeze(1).broadcast_to([P, 2, TT, E]),
                                                ALU.mult))
                dv.done(nc.vector.tensor_reduce(slot_of, of_choice, AX, ALU.add))
                for tt in range(TT):
                    dv.done(nc.vector.tensor_scalar(tmp, iota, slot_of[:, 0, tt:tt + 1], None, ALU.is_equal))
                    i = nc.vector.scalar_tensor_tensor(out=place[:, tt, :], in0=iota, scalar=slot_of[:, 1, tt:tt + 1],
                                                       in1=tmp, op0=ALU.is_equal, op1=ALU.add)
                    if tt == 0:
                        dv.done(i)
                i.then_inc(placed.sem, 1)
                dve.wait_ge(*gexp(2))
                dve.wait_ge(*placed(1))
                dv.done(nc.vector.tensor_reduce(g_sum, g_dist, AX, ALU.add))
                dv.done(nc.vector.scalar_tensor_tensor(out=g_sum, in0=e_dist, scalar=1.0, in1=g_sum, op0=ALU.add,
                                                       op1=ALU.mult))
                dv.done(nc.vector.reciprocal(weight_1, g_sum))
                dv.done(nc.vector.tensor_tensor(weight_2, weight_1, e_dist, ALU.mult))
                for tt in range(TT):
                    nc.vector.tensor_scalar(cwt[:, tt, :], iota, slot_of[:, 0, tt:tt + 1], weight_1[:, tt:tt + 1],
                                            ALU.is_equal, ALU.mult)
                    dv.done(nc.vector.tensor_scalar(tmp, iota, slot_of[:, 1, tt:tt + 1], weight_2[:, tt:tt + 1],
                                                    ALU.is_equal, ALU.mult))
                    i = nc.vector.tensor_tensor(cwt[:, tt, :], cwt[:, tt, :], tmp, ALU.add)
                    if tt == 0:
                        dv.done(i)
                i.then_inc(cwt_ready.sem, 1)

                def sort_in(c):
                    dve.wait_ge(*gathered(c + 1))
                    nc.vector.tensor_scalar(xsT[:, c, 0:SLOTS], bank[gather_banks[c % 6]][:, :], gains[:, 1, layer, c:c + 1],
                                            None, ALU.mult).then_inc(spread.sem, 1)
                sort_in(0)
                dv.done(nc.vector.tensor_copy(posf[:, 0, :], off))
                dv.done(nc.vector.tensor_copy(posf[:, PASSES, :], off))
                for j in range(1, PASSES):
                    nc.vector.tensor_scalar(posf[:, j, :], cnt, float(-CAP), float(j * CAP), ALU.add, ALU.min)
                dv.done(nc.vector.tensor_reduce(posf[:, PASSES, 0:1], cnt, AX, ALU.max))
                later_passes = posf[:, 1:PASSES, :]
                dv.done(nc.vector.tensor_tensor(later_passes, later_passes,
                                                off.unsqueeze(1).broadcast_to([P, PASSES - 1, E]), ALU.add))
                dv.done(nc.vector.tensor_scalar(later_passes, later_passes, float(-TRASH), None, ALU.add))
                for j in range(1, PASSES):
                    i = nc.vector.scalar_tensor_tensor(out=posf[:, j, :], in0=cnt, scalar=float(j * CAP),
                                                       in1=posf[:, j, :], op0=ALU.is_gt, op1=ALU.mult)
                dv.done(i)
                dv.done(nc.vector.tensor_scalar(later_passes, later_passes, float(TRASH), None, ALU.add))
                nc.vector.tensor_copy(pos_i[0:1, :], A[0:1, 4096:4096 + (PASSES + 1) * E]).then_inc(positioned.sem, 1)
                sort_in(2)
                sort_in(4)
                dve.wait_ge(*cw_turned(1))
                for b in range(2):
                    i = nc.vector.tensor_copy(cw[:, 2 * b:2 * b + 2, :],
                                              bank[4 + b][:, :].rearrange("p (b s) -> p b s", b=2))
                i.then_inc(cw_ready.sem, 1)
                sort_in(6)

                def tokens(index, dst):
                    where = dve.value_load(pos_i[0:1, index], min_val=0, max_val=TRASH)
                    return nc.vector.tensor_copy(dst, xsT[:, :, bass.ds(where, CAP)])

                def hidden(k, rows, wait):
                    g, u, e = bank[4 + k][0:rows, 0:FF], bank[4 + k][0:rows, FF:2 * FF], eb[0:rows, k, :]
                    wait(nc.vector.tensor_scalar(e, e, 1.0, None, ALU.add))
                    wait(nc.vector.reciprocal(e, e))
                    wait(nc.vector.tensor_tensor(e, g, e, ALU.mult))
                    return nc.vector.tensor_tensor(hid[0:rows, k, :], u, e, ALU.mult)

                dve.wait_ge(*spread(4))
                dve.wait_ge(*spread_a(4))
                dve.wait_ge(*logits(1))
                for k in range(2):
                    for q in range(2):
                        i = tokens(slice(2 * k + q, 2 * k + q + 1), xg[:, k, :, q * CAP:(q + 1) * CAP])
                    i.then_inc(x_ready_.sem, 1)
                with dve.Fori(0, E // PER) as turn:
                    for k in range(2):
                        steps = [3 * k]

                        def wait(ins):
                            steps[0] += 1
                            ins.then_inc(vstep.sem, 1)
                            dve.wait_ge(*vstep(turn * 6 + steps[0]))
                        dve.wait_ge(*exped(turn * 2 + k + 1))
                        hidden(k, P, wait).then_inc(hid_ready.sem, 1)
                        dve.wait_ge(*unit_done(turn * 12 + base + 4 * k + 4))
                        for q in range(2):
                            i = tokens(bass.ds(turn * PER + (PER + 2 * k + q), 1), xg[:, k, :, q * CAP:(q + 1) * CAP])
                        i.then_inc(x_ready_.sem, 1)
                    for k in range(2):
                        dve.wait_ge(*unit_done(turn * 12 + base + 10 + 2 * k))
                        nc.vector.tensor_copy(yrow[:, k, 0:NB], bank[2 * k][:, :]).then_inc(rows_v.sem, 1)

                over = dve.value_load(pos_i[0:1, PASSES * E:PASSES * E + 1], min_val=0, max_val=S)
                with dve.If(over > CAP):
                    with dve.Fori(0, (PASSES - 1) * E) as n:
                        steps = [0]

                        def wait(ins):
                            steps[0] += 1
                            ins.then_inc(f_v.sem, 1)
                            dve.wait_ge(*f_v(n * 3 + steps[0]))
                        dve.wait_ge(*f_stored(n + 1))
                        dve.wait_ge(*pair_stored(E // 2 + 1))
                        tokens(bass.ds(n + E, 1), xg[:, 0, :, 0:CAP]).then_inc(f_x.sem, 1)
                        dve.wait_ge(*f_exp(n + 1))
                        hidden(0, CAP, wait).then_inc(f_hid.sem, 1)
                for j in range(0, 8, 2):
                    dve.wait_ge(*y_turned(j + 1))
                    nc.vector.tensor_copy(ys[:, j // 2, 0:NB], bank[4][:, :]).then_inc(y_out_v.sem, 1)

            def scalar(act):
                act.wait_ge(*gexp_in(1))
                nc.scalar.activation(g_dist, g_dist, ACT.Exp).then_inc(gexp.sem, 1)
                nc.scalar.activation(e_dist, e_dist, ACT.Exp).then_inc(gexp.sem, 1)
                filler.scalar(act, 1)
                for c in range(1, DC, 2):
                    act.wait_ge(*gathered(c + 1))
                    nc.scalar.activation(xsT[:, c, 0:SLOTS], bank[gather_banks[c % 6]][:, :], ACT.Identity,
                                         scale=gains[:, 1, layer, c:c + 1]).then_inc(spread_a.sem, 1)
                act.wait_ge(*positioned(1))
                nc.scalar.activation(stat[:, 9:10], half[:, 0:1], ACT.Copy).then_inc(pair_stored.sem, 1)
                nc.scalar.activation(stat[:, 11:12], half[:, 0:1], ACT.Copy).then_inc(f_stored.sem, 1)

                def store(index, k, q):
                    where = act.value_load(pos_i[0:1, index], min_val=0, max_val=TRASH)
                    for hf in range(2):
                        i = nc.scalar.activation(
                            ysT[:, 4 * hf:4 * hf + 4, bass.ds(where, CAP)],
                            bank[turn_banks[k][hf]][:, :].rearrange("p (m s) -> p m s", m=4)[:, :, q * CAP:(q + 1) * CAP],
                            ACT.Copy)
                    return i

                def copy_hidden(k, rows):
                    return nc.scalar.activation(hidT[:, k, :, 0:rows],
                                                bank[6][:, 0:2 * P].rearrange("p (c n) -> p c n", c=2)[:, :, 0:rows],
                                                ACT.Copy)

                with act.Fori(0, E // PER) as turn:
                    for k in range(2):
                        act.wait_ge(*unit_done(turn * 12 + base + 4 * k + 4))
                        nc.scalar.activation(eb[:, k, :], bank[4 + k][:, 0:FF], ACT.Exp, scale=-1.0).then_inc(exped.sem, 1)
                    for k in range(2):
                        act.wait_ge(*h_turned(turn * 2 + k + 1))
                        copy_hidden(k, P).then_inc(hT_ready.sem, 1)
                        act.wait_ge(*unit_done(turn * 12 + base + 10 + 2 * k))
                        nc.scalar.activation(yrow[:, k, NB:D], bank[2 * k + 1][:, :], ACT.Copy).then_inc(rows_a.sem, 1)
                    for k in range(2):
                        act.wait_ge(*rows_turned(turn * 2 + k + 1))
                        act.wait_ge(*pair_stored(turn * 2 + k + 1))
                        store(bass.ds(turn * PER + 2 * k, 1), k, 0).then_inc(first_stored.sem, 1)
                        act.wait_ge(*first_stored(turn * 2 + k + 1))
                        store(bass.ds(turn * PER + 2 * k + 1, 1), k, 1).then_inc(pair_stored.sem, 1)
                over = act.value_load(pos_i[0:1, PASSES * E:PASSES * E + 1], min_val=0, max_val=S)
                with act.If(over > CAP):
                    with act.Fori(0, (PASSES - 1) * E) as n:
                        act.wait_ge(*pair_stored(E // 2 + 1))
                        act.wait_ge(*f_stored(n + 1))
                        act.wait_ge(*f_up(n + 1))
                        nc.scalar.activation(eb[0:CAP, 0, :], bank[4][0:CAP, 0:FF], ACT.Exp,
                                             scale=-1.0).then_inc(f_exp.sem, 1)
                        act.wait_ge(*f_turned(n + 1))
                        copy_hidden(0, CAP).then_inc(f_hT.sem, 1)
                        act.wait_ge(*f_down(n + 1))
                        nc.scalar.activation(yrow[0:CAP, 0, 0:NB], bank[0][0:CAP, :], ACT.Copy)
                        nc.scalar.activation(yrow[0:CAP, 0, NB:D], bank[1][0:CAP, :], ACT.Copy).then_inc(f_rows.sem, 1)
                        act.wait_ge(*f_rturned(n + 1))
                        store(bass.ds(n + E, 1), 0, 0).then_inc(f_stored.sem, 1)
                for j in range(1, 8, 2):
                    act.wait_ge(*y_turned(j + 1))
                    nc.scalar.activation(ys[:, j // 2, NB:D], bank[5][:, :], ACT.Copy).then_inc(y_out_a.sem, 1)

            def sync(sp):
                with sp.Fori(0, E // PER) as turn:
                    for k in range(3 * PER):
                        u = base + k
                        sp.wait_ge(*unit_done(turn * 12 + u - RING + 1))
                        w, at_ = next((w, at_) for w, at_ in ((gate_w, GATE_AT), (up_w, UP_AT), (down_w, DOWN_AT))
                                      if k in at_)
                        e = turn * PER + at_.index(k)
                        src = w[bass.ds(e, 1), :, :].rearrange("e (p c) n -> p (e c n)", p=P)
                        sp.dma_start(slot(u), src).then_inc(unit_full[u % RING].sem, 16)

            def gpsimd(pool):
                x_free(pool)
                pool.dma_start(router_w[:, :, 0:GROUPS],
                               t["moe_w_group"][layer].rearrange("(p c) n -> p c n", c=DC)).then_inc(table_in.sem, 16)
                pool.dma_start(router_w[:, :, GROUPS:],
                               t["moe_w_expert"][layer].rearrange("(p c) n -> p c n", c=DC)).then_inc(table_in.sem, 16)
                pool.dma_start(iota, later["iota"]).then_inc(table_in.sem, 16)
                nrm.root(pool)
                if after_norm:
                    after_norm(pool)
                pool.wait_ge(*pair_stored(E // 2 + 1))
                over = pool.value_load(pos_i[0:1, PASSES * E:PASSES * E + 1], min_val=0, max_val=S)
                with pool.If(over > CAP):
                    with pool.Fori(0, PASSES - 1) as ps_:
                        with pool.Fori(0, E) as e:
                            pool.wait_ge(*f_stored(ps_ * E + e + 1))
                            for k, w in enumerate((gate_w, up_w, down_w)):
                                pool.dma_start(A[:, k * 2048:(k + 1) * 2048],
                                               w[bass.ds(e, 1), :, :].rearrange("e (p c) n -> p (e c n)", p=P)
                                               ).then_inc(f_full.sem, 16)

            def tile_done(eng, tt):
                eng.wait_ge(*added(2 * (tt + 1)))
            st.tensor, st.vector, st.scalar, st.gpsimd, st.sync = tensor, vector, scalar, gpsimd, sync
            st.product, st.add, st.ready = product, add, tile_done
            return st

        cond2 = Conditioning(1, 2, 2)
        m1_base = len(units)
        m1 = moe(0, "m1", o1.ready, a1.ready, cond2)
        m1_units = (m1_base, m1_base + 3 * E)

        n2 = norm_stage(m1.ready, gains[:, 0, 1, :])
        A_WIDTH = MLA_Q + MLA_KV + ROT

        def copy_a(eng, n, tt, ps):
            return nc.scalar.activation(hn[:, tt, n * NB:n * NB + ps.shape[1]], ps, ACT.Copy)
        pe_zeroed = sem("pe_zeroed")
        a_sq, a_rs, a_scaled = sem("a_sq"), sem("a_rs"), sem("a_scaled")
        a_parts = [(0, MLA_Q), (MLA_Q, MLA_Q + MLA_KV)]

        def latent_scalar(act, k):
            a, b = a_parts[k]
            act.wait_ge(*pa.copied(2 * k + 2))
            for tt in range(TT):
                nc.scalar.activation(BC[:, k * 1024 + tt * 512:k * 1024 + tt * 512 + b - a], hn[:, tt, a:b], ACT.Square,
                                     accum_out=stat[:, 64 + 2 * k + tt:65 + 2 * k + tt]).then_inc(a_sq.sem, 1)
        pa = project_stage("pa", n2.tile, hT_lhs, square_units(t["mla_w_a"][0], A_WIDTH), copy_a, latent_scalar)

        def latent_gpsimd(pool):
            pool.wait_ge(*pe_zeroed(1))
            for k, (a, b) in enumerate(a_parts):
                pool.wait_ge(*a_sq(2 * k + 2))
                r = stat[:, 72 + 2 * k:74 + 2 * k]
                po.done(nc.gpsimd.tensor_scalar(r, stat[:, 64 + 2 * k:66 + 2 * k], 1.0 / (b - a), EPS, ALU.mult, ALU.add))
                nc.gpsimd.tensor_tensor(r, r, half[:, 0:TT], ALU.pow).then_inc(a_rs.sem, 1)

        def latent_vector(dve):
            for k, (a, b) in enumerate(a_parts):
                dve.wait_ge(*a_rs(k + 1))
                for tt in range(TT):
                    i = nc.vector.tensor_scalar(hn[:, tt, a:b], hn[:, tt, a:b], stat[:, 72 + 2 * k + tt:73 + 2 * k + tt],
                                                None, ALU.mult)
                i.then_inc(a_scaled.sem, 1)

        cT = BC[:, 8192:8192 + 5 * S].rearrange("p (c s) -> p c s", c=5)
        t3 = turn_stage("t3", lambda pe: pe.wait_ge(*a_scaled(1)),
                        [(lambda tt, c=c: hn[:, tt, c:MLA_Q:3], P, cT[:, c, :], mla_gain[:, c:c + 1]) for c in range(3)] +
                        [(lambda tt, c=c: hn[:, tt, MLA_Q + c:MLA_Q + MLA_KV:2], P, cT[:, 3 + c, :],
                          mla_gain[:, 3 + c:4 + c]) for c in range(2)],
                        fill_ready=lambda pe, f: pe.wait_ge(*a_scaled(1 if f == 0 else 2)))
        q_l = A[:, 0:3072].rearrange("p (t h d) -> p t h d", t=TT, h=HEADS)
        k_l = A[:, 3072:6144].rearrange("p (t h d) -> p t h d", t=TT, h=HEADS)
        v_l = A[:, 6144:8192].rearrange("p (t h d) -> p t h d", t=TT, h=HEADS)

        def copy_q(eng, n, tt, ps):
            return nc.scalar.activation(q_l[:, tt, 2 * n:2 * n + 2, :], ps.rearrange("p (h d) -> p h d", h=2), ACT.Copy)

        def copy_kv(eng, n, tt, ps):
            kv = ps.rearrange("p (h d) -> p h d", h=2)
            nc.scalar.activation(k_l[:, tt, 2 * n:2 * n + 2, 0:NOPE], kv[:, :, 0:NOPE], ACT.Copy)
            return nc.scalar.activation(v_l[:, tt, 2 * n:2 * n + 2, :], kv[:, :, NOPE:], ACT.Copy)
        pq = project_stage("pq", lambda pe, tt: t3.ready(pe), lambda c, tt: cT[:, c, tt * P:(tt + 1) * P],
                           square_units(t["mla_w_qb"][0], 1536, kc=3, per=3, nb=2 * MLA_QK), copy_q,
                           lambda act, n: heads_scalar(act, (2 * n, 2 * n + 1)))
        kv_src = t["mla_w_kvb"][0].rearrange("(p c) n -> p c n", c=2)
        kv_blocks = []
        for n in range(2):
            u = plan(lambda a: a.rearrange("p (c n) -> p c n", c=2), kv_src[:, :, n * 1024:(n + 1) * 1024])
            for hf in range(2):
                kv_blocks.append((NB, [(u, lambda a, hf=hf: a.rearrange("p (c n) -> p c n", c=2)[:, :, hf * NB:(hf + 1) * NB],
                                        2, hf == 0)]))

        def q_left(pe, tt):
            pe.wait_ge(*pq.copied(8))
        l_sq, l_ss, l_rs, l_pe, l_qk = sem("l_sq"), sem("l_ss"), sem("l_rs"), sem("l_pe"), sem("l_qk")
        l_items = [(x[:, tt, 2 * n:2 * n + 2, :], qk, tt) for qk, x in enumerate((q_l, k_l))
                   for n in range(4) for tt in range(TT)]
        L_HEADS = 2
        l_spare = (hn[:, :, :].rearrange("p t d -> p (t d)"), hT[:, :, :].rearrange("p c s -> p (c s)"))

        def l_squares(j):
            return l_spare[j % 2][:, 0:L_HEADS * MLA_QK].rearrange("p (h d) -> p h d", h=L_HEADS)

        def heads_scalar(act, items):
            for j in items:
                x, qk, tt = l_items[j]
                act.wait_ge(*l_pe(2))
                act.wait_ge(*(pkv if qk else pq).copied(j % 8 // 2 * 2 + 2))
                if j >= 2:
                    act.wait_ge(*l_ss(j - 1))
                nc.scalar.activation(l_squares(j), x, ACT.Square).then_inc(l_sq.sem, 1)
        pkv = project_stage("pkv", q_left, lambda c, tt: cT[:, 3 + c, tt * P:(tt + 1) * P], kv_blocks, copy_kv,
                            lambda act, n: heads_scalar(act, (8 + 2 * n, 9 + 2 * n)))

        def heads_gpsimd(pool):
            for j in range(len(l_items)):
                pool.wait_ge(*l_ss(j + 1))
                a, b, n = 64 + 8 * (j % 2), 80 + 8 * (j % 2), L_HEADS
                mean = stat[:, a + 32:a + 32 + n]
                po.done(nc.gpsimd.tensor_scalar(mean, stat[:, a:a + n], 1.0 / MLA_QK, EPS, ALU.mult, ALU.add))
                nc.gpsimd.tensor_tensor(stat[:, b:b + n], mean, half[:, 0:n], ALU.pow).then_inc(l_rs.sem, 1)

        def heads_vector(dve):
            for tt in range(TT):
                nc.vector.tensor_copy(k_l[:, tt, :, NOPE:], hn[:, tt, MLA_Q + MLA_KV:A_WIDTH].unsqueeze(1)
                                      .broadcast_to([P, HEADS, ROT])).then_inc(l_pe.sem, 1)
            dve.wait_ge(*l_pe(2))
            n = L_HEADS
            t1_, t2_ = (a[:, 1536:1536 + n * ROT].rearrange("p (h d) -> p h d", h=n) for a in l_spare)

            def sums(j):
                dve.wait_ge(*l_sq(j + 1))
                if j >= 2:
                    dve.wait_ge(*l_rs(j - 1))
                nc.vector.tensor_reduce(stat[:, 64 + 8 * (j % 2):64 + 8 * (j % 2) + n], l_squares(j), AX,
                                        ALU.add).then_inc(l_ss.sem, 1)
            for j, (x, qk, tt) in enumerate(l_items):
                if tt == 0:
                    sums(j)
                    sums(j + 1)
                rotate(dve, x[:, :, NOPE:], None, ROT, n, qk, tt, t1_, t2_)
                dve.wait_ge(*l_rs(j + 1))
                r = stat[:, 80 + 8 * (j % 2):80 + 8 * (j % 2) + n].unsqueeze(2)
                nc.vector.tensor_tensor(x[:, :, 0:NOPE], x[:, :, 0:NOPE], r.broadcast_to([P, n, NOPE]), ALU.mult)
                nc.vector.tensor_tensor(x[:, :, NOPE:], t1_, r.broadcast_to([P, n, ROT]),
                                        ALU.mult).then_inc(l_qk.sem, 1)
                dve.wait_ge(*l_qk(j + 1))

        nopeT = BC[:, 0:16 * S].rearrange("p (h k s) -> p h k s", h=HEADS, k=2)
        peT = BC[:, 16 * S:32 * S].rearrange("p (h k s) -> p h k s", h=HEADS, k=2)

        def l_turn(name, x, k, **how):
            jobs = []
            for h in range(HEADS):
                jobs.append((lambda tt, h=h: x[:, tt, h, 0:NOPE], P, nopeT[:, h, k, :], mla_gain[:, 5 + k:6 + k]))
                jobs.append((lambda tt, h=h: x[:, tt, h, NOPE:], ROT, peT[0:ROT, h, k, :], None))
            return turn_stage(name, lambda pe: pe.wait_ge(*l_qk(8 * k + 8)), jobs, **how)
        t4q = l_turn("t4q", q_l, 0, scalar_only=True)
        t4k = l_turn("t4k", k_l, 1, bank0=6)

        def rotary_zero_gpsimd(pool):
            m1.ready(pool, 1)
            pool.wait_ge(*n2.rooted(TT))
            nc.gpsimd.memset(BC[ROT:P, 16 * S:32 * S], 0.0).then_inc(pe_zeroed.sem, 1)

        def l_turned(pe):
            pe.wait_ge(*pe_zeroed(1))
            t4q.ready(pe)
            t4k.ready(pe)

        def latent_head(h):
            pairs = [(lambda tt, x=x: x[:, h, 0, tt * P:(tt + 1) * P], lambda k0, k1, x=x: x[:, h, 1, k0:k1])
                     for x in (nopeT, peT)]
            return ([pairs], lambda kt: v_l[:, kt, h, :], lambda tt: hn[:, tt, h * P:(h + 1) * P], 0)
        a2 = attention_stage("a2", l_turned, [latent_head(h) for h in range(HEADS)], MLA_QK ** -0.5, P,
                             lambda h, dve: at["causal"])
        t5 = heads_turned("t5", a2.ready)
        o2 = out_stage(square_units(t["mla_w_out"][0], D, order="(c p)"), hT_lhs, add_x)
        cond3 = Conditioning(2, 3, 2)
        m2_base = len(units)
        m2 = moe(1, "m2", o2.ready, a2.ready, cond3, lambda pool: conditioning_gpsimd(pool))
        m2_units = (m2_base, m2_base + 3 * E)

        mod_in, mod_ready = sem("mod_in"), sem("mod_ready")
        b_cols = stat[:, 256:288].rearrange("p (k c) -> p k c", k=4)
        MOD = (0, 1, 3, 4)

        def conditioning_gpsimd(pool):
            cond3.ready(pool)
            for k, m in enumerate(MOD):
                pool.dma_start(modc[:, k, :], mod_dram[m * D:(m + 1) * D].rearrange("(p c) -> p c", c=DC)
                               ).then_inc(mod_in.sem, 16)
                pool.dma_start(b_cols[:, k, :], t["b_ada_2"][m * D:(m + 1) * D].rearrange("(p c) -> p c", c=DC)
                               ).then_inc(mod_in.sem, 16)

        def conditioning_vector(dve):
            dve.wait_ge(*mod_in(16 * 8))
            dv.done(nc.vector.tensor_tensor(modc[:, :, :], modc[:, :, :], b_cols, ALU.add))
            for k in range(2):
                dv.done(nc.vector.tensor_scalar(modc[:, 2 * k + 1, :], modc[:, 2 * k + 1, :], 1.0, None, ALU.add))
                i = nc.vector.tensor_tensor(modc[:, 2 * k + 1, :], modc[:, 2 * k + 1, :], gains2[:, k, :], ALU.mult)
            i.then_inc(mod_ready.sem, 1)
            dve.wait_ge(*mod_ready(1))

        n3 = norm_stage(m2.ready, modc[:, 1, :], shift=modc[:, 0, :], extra=[(mod_ready, 1)])
        z = A[:, 0:TT * HYB_IN].rearrange("p (t n) -> p t n", t=TT)
        QA, KA, VA, QB, KB, VB, FB = 0, 512, 640, 768, 1280, 1792, 2304
        in_src = t["w_in_2"].rearrange("(p c) n -> p c n", c=DC)

        def wide_unit(a):
            return a.rearrange("p (c n) -> p c n", c=DC)

        def z_unit(col):
            return plan(wide_unit, in_src[:, :, col:col + 2 * P])
        z_blocks = square_units(t["w_in_2"], 264, col0=VB + 2 * P)
        z_blocks.append((2 * P, [(z_unit(VB), wide_unit, DC, False)]))
        kv_unit = z_unit(KA)
        z_blocks.append((P, [(kv_unit, lambda a: wide_unit(a)[:, :, P:], DC, True)]))
        z_at = (VB + 2 * P, VB, VA)

        def copy_z(eng, n, tt, ps):
            return nc.scalar.activation(z[:, tt, z_at[n]:z_at[n] + ps.shape[1]], ps, ACT.Copy)
        pz = project_stage("pz", n3.tile, hT_lhs, z_blocks, copy_z)
        kT = BC[:, 0:6 * S].rearrange("p (j s) -> p j s", s=S)
        qT = BC[:, 6 * S:22 * S].rearrange("p (j s) -> p j s", s=S)
        q_zeroed = sem("q_zeroed")

        def q_zero_gpsimd(pool):
            m2.ready(pool, 1)
            pool.wait_ge(*n3.rooted(TT))
            po.done(nc.gpsimd.memset(qT[ROT:P, 0:16:2, :], 0.0))
            nc.gpsimd.memset(qT[0:ROT, 1:16:2, :], 0.0).then_inc(q_zeroed.sem, 1)
        turned_units = [kv_unit] + [z_unit(col) for col in (QA, QA + 2 * P, QB, QB + 2 * P, KB, KB + 2 * P)]
        z_out_v, z_out_a = sem("z_out_v"), sem("z_out_a")

        def z_left(eng, f):
            eng.wait_ge(*(z_out_a if f % 2 else z_out_v)(f // 2 + 1))

        def channels_tensor(pe):
            for f, u in enumerate(turned_units):
                if f < 4:
                    pe.wait_ge(*pz.copied(4 if f < 2 else 6))
                else:
                    z_left(pe, f - 4)
                unit_here(pe, u)
                w = wide_unit(slot(u))
                for b in range(1 if f == 0 else 2):
                    for c in range(DC):
                        i = nc.tensor.matmul(bank[(2 + f) % 4][:, b * S:(b + 1) * S], w[:, c, b * P:(b + 1) * P],
                                             hT[:, c, :], start=(c == 0), stop=(c == DC - 1))
                i.then_inc(unit_done.sem, 1)
                if f in (2, 3, 4):
                    (forget_sums, forget_turn, forget_spread)[f - 2](pe)

        def channels_evac(eng, f):
            eng.wait_ge(*unit_done(turned_units[f] + 1))
            ps = bank[(2 + f) % 4]
            copy = (lambda dst, src: nc.scalar.activation(dst, src, ACT.Copy)) if f % 2 else nc.vector.tensor_copy
            pairs = ps[:, :].rearrange("p (j s) -> p j s", j=2)
            if f == 0:
                for kv in range(2):
                    for side in range(2):
                        i = copy(kT[side * ROT:(side + 1) * ROT, kv, :], ps[kv * ROT:(kv + 1) * ROT, 0:S])
            elif f <= 4:
                for side in range(2):
                    rows = slice(side * ROT, (side + 1) * ROT)
                    i = copy(qT[rows, 4 * (f - 1) + side:4 * f:2, :], pairs[rows, :, :])
            else:
                i = copy(kT[:, 2 * (f - 4):2 * (f - 4) + 2, :], pairs)
            i.then_inc((z_out_a if f % 2 else z_out_v).sem, 1)
        table = A[:, 4624:4624 + P + 2 * SPAN]
        upto, window, dist = table[:, 0:P], table[:, P:P + SPAN], table[:, P + SPAN:]
        fk = A[:, 5520:5520 + HEADS * S].rearrange("p (h s) -> p h s", h=HEADS)
        hbias = A[:, 7568:7568 + SPAN]
        fox = stat[:, 288:288 + 5 * TT * HEADS].rearrange("p (k t h) -> p k t h", k=5, t=TT)
        f_raw, f_abs, f_log, f_sum, f_low = (fox[:, k, :, :] for k in range(5))
        table3, fx = sem("table3"), sem("fx")
        fx_exp, fx_log, fx_ready, fx_sum, fx_col = sem("fx_exp"), sem("fx_log"), sem("fx_ready"), sem("fx_sum"), sem("fx_col")
        fx_turned, fx_rows, fx_spread, fx_out = sem("fx_turned"), sem("fx_rows"), sem("fx_spread"), sem("fx_out")
        fT = A[0:HEADS, 7568:7568 + S]

        def tables_gpsimd(pool):
            m2.ready(pool, 1)
            pool.wait_ge(*q_zeroed(1))
            pool.dma_start(upto, later["upto"]).then_inc(table3.sem, 16)
            pool.dma_start(window, later["window"]).then_inc(table3.sem, 16)
            pool.dma_start(dist, later["dist"]).then_inc(table3.sem, 16)

        def forget_vector(dve):
            dve.wait_ge(*pz.copied(2))
            dv.done(nc.vector.tensor_tensor(f_raw, z[:, :, FB:FB + HEADS],
                                            f_bias.unsqueeze(1).broadcast_to([P, TT, HEADS]), ALU.add))
            nc.vector.tensor_scalar(f_low, f_raw, 0.0, None, ALU.min)
            dv.done(nc.vector.tensor_scalar(f_abs, f_raw, -1.0, None, ALU.mult))
            nc.vector.tensor_tensor(f_abs, f_abs, f_raw, ALU.max).then_inc(fx.sem, 1)
            dve.wait_ge(*fx_exp(1))
            nc.vector.tensor_scalar(f_abs, f_abs, 1.0, None, ALU.add).then_inc(fx.sem, 1)
            dve.wait_ge(*fx_log(1))
            nc.vector.tensor_tensor(f_log, f_low, f_abs, ALU.subtract).then_inc(fx_ready.sem, 1)
            channels_evac(dve, 0)
            channels_evac(dve, 2)
            dve.wait_ge(*fx_sum(1))
            nc.vector.tensor_copy(f_sum, bank[7][:, 0:TT * HEADS].rearrange("p (t h) -> p t h", t=TT)).then_inc(fx_col.sem, 1)
            dve.wait_ge(*fx_turned(1))
            nc.vector.tensor_copy(fT, bank[7][0:HEADS, 0:S]).then_inc(fx_rows.sem, 1)
            channels_evac(dve, 4)
            for b in range(4):
                dve.wait_ge(*fx_spread(b + 1))
                nc.vector.tensor_copy(fk[:, 2 * b:2 * b + 2, :], bank[4 + b][:, :].rearrange("p (h s) -> p h s", h=2)
                                      ).then_inc(fx_out.sem, 1)
            channels_evac(dve, 6)

        def forget_scalar(act):
            act.wait_ge(*fx(1))
            nc.scalar.activation(f_abs, f_abs, ACT.Exp, scale=-1.0).then_inc(fx_exp.sem, 1)
            act.wait_ge(*fx(2))
            nc.scalar.activation(f_abs, f_abs, ACT.Ln).then_inc(fx_log.sem, 1)

        def forget_sums(pe):
            pe.wait_ge(*table3(48))
            pe.wait_ge(*fx_ready(1))
            nc.tensor.matmul(bank[7][:, 0:HEADS], upto, f_log[:, 0, :], start=True, stop=True)
            nc.tensor.matmul(bank[7][:, HEADS:2 * HEADS], ones, f_log[:, 0, :], start=True, stop=False)
            nc.tensor.matmul(bank[7][:, HEADS:2 * HEADS], upto, f_log[:, 1, :], start=False,
                             stop=True).then_inc(fx_sum.sem, 1)

        def forget_turn(pe):
            pe.wait_ge(*fx_col(1))
            for tt in range(TT):
                i = nc.tensor.transpose(bank[7][0:HEADS, tt * P:(tt + 1) * P], f_sum[:, tt, :], ident)
            i.then_inc(fx_turned.sem, 1)

        def forget_spread(pe):
            pe.wait_ge(*fx_rows(1))
            for h in range(HEADS):
                i = nc.tensor.matmul(bank[4 + h // 2][:, (h % 2) * S:(h % 2 + 1) * S],
                                     ident[0:HEADS, h:h + 1].broadcast_to([HEADS, P]), fT, start=True, stop=True)
                if h % 2:
                    i.then_inc(fx_spread.sem, 1)

        def z_ready(pe):
            pe.wait_ge(*q_zeroed(1))
            pe.wait_ge(*pz.copied(6))
            z_left(pe, 5)
            z_left(pe, 6)
            pe.wait_ge(*fx_out(4))

        def head3(h):
            i = h % HEADS
            k0 = i // 4 if h < HEADS else 2 + i // 2
            vc, side = (VA, i // 4) if h < HEADS else (VB + P * (i // 2), i % 2)
            return ([[(lambda tt: qT[:, h, tt * P:(tt + 1) * P], lambda k_a, k_b: kT[:, k0, k_a:k_b])]],
                    lambda kt: z[:, kt, vc:vc + P], lambda tt: hn[:, tt, h * ROT:(h + 1) * ROT], side)

        bias_ready = sem("bias_ready")
        hbias = BC[:, 6656:6656 + 2 * SPAN].rearrange("p (b s) -> p b s", b=2)

        def bias_gpsimd(pool):
            pool.wait_ge(*fx_out(4))
            pool.wait_ge(*table3(48))
            for h in range(2 * HEADS):
                if h >= 2:
                    pool.wait_ge(*a3.masked(h - 1))
                b = hbias[:, h % 2, :]
                if h < HEADS:
                    slope = 2.0 ** (-8.0 * (h + 1) / HEADS)
                    po.done(nc.gpsimd.tensor_scalar(b, dist, -slope, None, ALU.mult))
                    nc.gpsimd.tensor_tensor(b, b, window, ALU.add).then_inc(bias_ready.sem, 1)
                    continue
                for tt, (lo, hi) in enumerate([(0, P), (P, SPAN)]):
                    i = nc.gpsimd.tensor_scalar(b[:, lo:hi], fk[:, h - HEADS, 0:hi - lo], -1.0,
                                                f_sum[:, tt, h - HEADS:h - HEADS + 1], ALU.mult, ALU.add)
                po.done(i)
                nc.gpsimd.tensor_tensor(b, b, at["causal"], ALU.add).then_inc(bias_ready.sem, 1)

        def bias3(h, dve):
            dve.wait_ge(*bias_ready(h + 1))
            return hbias[:, h % 2, :]
        a3 = attention_stage("a3", z_ready, [head3(h) for h in range(2 * HEADS)], ROT ** -0.5, ROT, bias3, sink=True)
        t7 = heads_turned("t7", a3.ready)

        gate_in = [sem("gate1_in"), sem("gate2_in")]
        gate_rows = [A[:, 0:D], A[:, 5632:5632 + D]]
        gate_bias = [A[:, D:2 * D], A[:, 6656:6656 + D]]
        scratch = [A[:, 2048:3072], BC[:, 7168:8192]]
        g_fin = A[:, 0:D]
        fin_in = sem("fin_in")

        def gate_gpsimd(pool, k):
            m = (2, 5)[k]
            pool.dma_start(gate_rows[k], mod_dram[m * D:(m + 1) * D].partition_broadcast(P)).then_inc(gate_in[k].sem, 16)
            pool.dma_start(gate_bias[k], t["b_ada_2"][m * D:(m + 1) * D].partition_broadcast(P)).then_inc(gate_in[k].sem, 16)

        def gate_vector(dve, k):
            dve.wait_ge(*gate_in[k](32))
            dv.done(nc.vector.tensor_tensor(gate_rows[k], gate_rows[k], gate_bias[k], ALU.add))

        def gated(k):
            def add(tt, n, ps):
                xs = X[:, tt, n * NB:(n + 1) * NB]
                product = scratch[k][:, n * NB:(n + 1) * NB]
                dv.done(nc.vector.tensor_tensor(product, ps, gate_rows[k][:, n * NB:(n + 1) * NB], ALU.mult))
                return nc.vector.tensor_tensor(xs, xs, product, ALU.add)
            return add
        o3 = out_stage(square_units(t["w_out_2"], D, order="(c p)"), hT_lhs, gated(0))

        n4 = norm_stage(o3.ready, modc[:, 3, :], shift=modc[:, 2, :])
        FB_ = DFF // P
        PAIRS = FB_ // 2
        up_src = t["w_up_2"].rearrange("(p c) n -> p c n", c=DC)
        down_src = t["w_down_2"].rearrange("(c p) n -> p c n", p=P)
        up_units = [[plan(lambda a: a.rearrange("p (c n) -> p c n", c=DC), up_src[:, :, c0 + j * 256:c0 + (j + 1) * 256])
                     for c0 in (DFF, 0)] for j in range(PAIRS)]
        down_units = [plan(lambda a: a.rearrange("p (c n) -> p c n", c=2), down_src[:, 2 * j:2 * j + 2, :])
                      for j in range(PAIRS)]
        hidT3 = BC[:, 0:FB_ * S].rearrange("p (b s) -> p b s", b=FB_)
        cw3 = BC[:, 5632:5632 + 4 * 2 * FB_].rearrange("p (k b) -> p k b", k=4)
        cw_rows = BC[0:2 * FB_, 6144:6144 + 4 * P].rearrange("p (k c) -> p k c", k=4)
        cw_in, cw_turned3, cw_out = sem("cw_in"), sem("cw_turned3"), sem("cw_out")
        raw = A[:, 2048:4096].rearrange("p (j h n) -> p j h n", j=2, h=2)
        yv = A[:, 4096:5120].rearrange("p (h b s) -> p h b s", h=2, b=2)
        ev = A[:, 5120:5632].rearrange("p (b s) -> p b s", b=2)
        raw_copied, raw_used, g_conv, g_exp, hid3 = (sem("raw_copied"), sem("raw_used"), sem("g_conv"), sem("g_exp"),
                                                     sem("hid3"))
        down_done, out_added = sem("down_done"), sem("out_added")

        def gate1_gpsimd(pool):
            a3.ready(pool)
            gate_gpsimd(pool, 0)
            for k in range(3):
                pool.dma_start(cw_rows[:, k, :], t["conv_w_2"][k].rearrange("(b p) -> b p", p=P)).then_inc(cw_in.sem, 16)
            pool.dma_start(cw_rows[:, 3, :], t["conv_b_2"].rearrange("(b p) -> b p", p=P)).then_inc(cw_in.sem, 16)

        def gate2_gpsimd(pool):
            o3.ready(pool, 1)
            gate_gpsimd(pool, 1)
            pool.dma_start(g_fin, t["g_final_2"].partition_broadcast(P)).then_inc(fin_in.sem, 16)

        def mlp_tensor(pe):
            pe.wait_ge(*cw_in(64))
            n4.tile(pe, 0)
            for k in range(4):
                i = nc.tensor.transpose(bank[4][:, k * 64:k * 64 + 2 * FB_], cw_rows[:, k, :], ident[0:2 * FB_, 0:2 * FB_])
            i.then_inc(cw_turned3.sem, 1)
            for j in range(PAIRS):
                for h in range(2):
                    n = 2 * j + h
                    if n >= 4:
                        pe.wait_ge(*raw_copied(n - 3))
                    u = up_units[j][h]
                    unit_here(pe, u)
                    w = units[u][0](slot(u))
                    for t0, t1 in ([(0, P), (P, S)] if n == 0 else [(0, S)]):
                        if n == 0:
                            n4.tile(pe, t0 // P)
                        for b in range(2):
                            for c in range(DC):
                                i = nc.tensor.matmul(bank[n % 4][:, b * S + t0:b * S + t1], w[:, c, b * P:(b + 1) * P],
                                                     hT[:, c, t0:t1], start=(c == 0), stop=(c == DC - 1))
                    i.then_inc(unit_done.sem, 1)
            pe.wait_ge(*cw_out(1))
            for tt in range(TT):
                for nb in ([(0, 1)] if tt == 0 else [(0,), (1,)]):
                    for j in range(PAIRS):
                        u = down_units[j]
                        if tt == 0:
                            pe.wait_ge(*hid3(j + 1))
                            unit_here(pe, u)
                        w = units[u][0](slot(u))
                        for c in range(2):
                            for n in nb:
                                i = nc.tensor.matmul(bank[4 + 2 * tt + n][:, :], hidT3[:, 2 * j + c, tt * P:(tt + 1) * P],
                                                     w[:, c, n * NB:(n + 1) * NB], start=(j == 0 and c == 0),
                                                     stop=(j == PAIRS - 1 and c == 1))
                    i.then_inc(down_done.sem, 1)

        def mlp_scalar(act):
            for j in range(PAIRS):
                for h in range(2):
                    n = 2 * j + h
                    act.wait_ge(*unit_done(up_units[j][h] + 1))
                    if j >= 2:
                        act.wait_ge(*raw_used(n - 3))
                    nc.scalar.activation(raw[:, j % 2, h, :], bank[n % 4][:, :], ACT.Copy).then_inc(raw_copied.sem, 1)
                act.wait_ge(*g_conv(j + 1))
                nc.scalar.activation(ev, yv[:, 0, :, :], ACT.Exp, scale=-1.0).then_inc(g_exp.sem, 1)

        def mlp_vector(dve):
            dve.wait_ge(*cw_turned3(1))
            nc.vector.tensor_copy(cw3, bank[4][:, 0:256].rearrange("p (k b) -> p k b", k=4)[:, :, 0:2 * FB_]
                                  ).then_inc(cw_out.sem, 1)
            dve.wait_ge(*cw_out(1))
            for j in range(PAIRS):
                for h in range(2):
                    dve.wait_ge(*raw_copied(2 * j + h + 1))
                    blocks = [((FB_ if h == 0 else 0) + 2 * j + b, raw[:, j % 2, h, b * S:(b + 1) * S], yv[:, h, b, :])
                              for b in range(2)]
                    for ch, x, y in blocks:
                        i = nc.vector.tensor_scalar(y, x, cw3[:, 2, ch:ch + 1], cw3[:, 3, ch:ch + 1], ALU.mult, ALU.add)
                    dv.done(i)
                    for back in (1, 2):
                        for ch, x, y in blocks:
                            i = nc.vector.scalar_tensor_tensor(out=y[:, back:], in0=x[:, 0:S - back],
                                                               scalar=cw3[:, 2 - back, ch:ch + 1], in1=y[:, back:],
                                                               op0=ALU.mult, op1=ALU.add)
                        if back == 1:
                            dv.done(i)
                    i.then_inc(raw_used.sem, 1)
                    if h == 0:
                        dve.wait_ge(*raw_used(2 * j + 1))
                        nc.vector.tensor_copy(stat[:, 14:15], stat[:, 64:65]).then_inc(g_conv.sem, 1)
                dve.wait_ge(*g_exp(j + 1))
                dve.wait_ge(*raw_used(2 * j + 2))
                dv.done(nc.vector.tensor_scalar(ev, ev, 1.0, None, ALU.add))
                dv.done(nc.vector.reciprocal(ev, ev))
                dv.done(nc.vector.tensor_tensor(ev, ev, yv[:, 0, :, :], ALU.mult))
                nc.vector.tensor_tensor(hidT3[:, 2 * j:2 * j + 2, :], ev, yv[:, 1, :, :], ALU.mult).then_inc(hid3.sem, 1)
            gate_vector(dve, 1)
            dve.wait_ge(*fin_in(16))
            for tt in range(TT):
                for n in range(2):
                    dve.wait_ge(*down_done(tt * (n + 1) + 1))
                    gated(1)(tt, n, bank[4 + 2 * tt + n][:, :]).then_inc(out_added.sem, 1)
                last_scale(dve, tt)

        last_sq, last_rs, result = sem("last_sq"), sem("last_rs"), sem("result")

        def last_scalar(act):
            for tt in range(TT):
                act.wait_ge(*out_added(2 * tt + 2))
                nc.scalar.activation(hn[:, tt, :], X[:, tt, :], ACT.Square,
                                     accum_out=stat[:, tt:tt + 1]).then_inc(last_sq.sem, 1)

        def last_gpsimd(pool):
            for tt in range(TT):
                pool.wait_ge(*last_sq(tt + 1))
                r = stat[:, 2 + tt:3 + tt]
                po.done(nc.gpsimd.tensor_scalar(r, stat[:, tt:tt + 1], 1.0 / D, EPS, ALU.mult, ALU.add))
                nc.gpsimd.tensor_tensor(r, r, half[:, 0:1], ALU.pow).then_inc(last_rs.sem, 1)

        def last_scale(dve, tt):
            dve.wait_ge(*out_added(2 * tt + 2))
            dve.wait_ge(*last_rs(tt + 1))
            nc.vector.scalar_tensor_tensor(out=hn[:, tt, :], in0=X[:, tt, :], scalar=stat[:, 2 + tt:3 + tt], in1=g_fin,
                                           op0=ALU.mult, op1=ALU.mult).then_inc(result.sem, 1)

        block = ctx.enter_context(nc.Block())
        final_out = sem("final_out")

        @block.sync
        def _(sp):
            def load(first, last):
                for u in range(first, last):
                    load_unit(sp, u)
            start_sync(sp)
            load(4, m1_units[0])
            m1.sync(sp)
            load(m1_units[1], m2_units[0])
            m2.sync(sp)
            load(m2_units[1], len(units))
            for tt in range(TT):
                sp.wait_ge(*result(tt + 1))
                sp.dma_start(out[0, tt * P:(tt + 1) * P, :], hn[:, tt, :]).then_inc(final_out.sem, 16)
            sp.wait_ge(*final_out(16 * TT))

        @block.gpsimd
        def _(pool):
            po.eng = pool
            po.done(nc.gpsimd.memset(half[:, :], -0.5))
            n1.root(pool)
            rope_gpsimd(pool)
            sub_gpsimd(pool)
            m1.gpsimd(pool)
            n2.root(pool)
            rotary_zero_gpsimd(pool)
            latent_gpsimd(pool)
            heads_gpsimd(pool)
            m2.gpsimd(pool)
            n3.root(pool)
            q_zero_gpsimd(pool)
            tables_gpsimd(pool)
            bias_gpsimd(pool)
            gate1_gpsimd(pool)
            n4.root(pool)
            gate2_gpsimd(pool)
            last_gpsimd(pool)

        @block.scalar
        def _(act):
            for tt in range(TT):
                n1.square(act, tt)
            for tt in range(TT):
                n1.evac(act, tt, 1)
            setup_scalar(act)
            p1.drain(act)
            t1.scalar(act)
            a1.scalar(act)
            t2.scalar(act)
            close_scalar(act, m1.norm)
            m1.scalar(act)
            close_scalar(act, n2)
            pa.drain(act)
            t3.scalar(act)
            pq.drain(act)
            pkv.drain(act)
            t4q.scalar(act)
            t4k.scalar(act)
            a2.scalar(act)
            t5.scalar(act)
            close_scalar(act, m2.norm)
            m2.scalar(act)
            close_scalar(act, n3)
            pz.drain(act)
            forget_scalar(act)
            for f in (1, 3, 5):
                channels_evac(act, f)
            a3.scalar(act)
            t7.scalar(act)
            close_scalar(act, n4)
            mlp_scalar(act)
            last_scalar(act)

        @block.vector
        def _(dve):
            dv.eng = dve
            for tt in range(TT):
                n1.scale(dve, tt)
            for tt in range(TT):
                n1.evac(dve, tt, 0)
            setup_vector(dve)
            rope_vector(dve)
            t1.vector(dve)
            a1.vector(dve)
            sub_vector(dve)
            t2.vector(dve)
            close_vector(dve, o1, m1.norm)
            m1.vector(dve)
            close_vector(dve, m1, n2)
            fold_rope(1)
            latent_vector(dve)
            t3.vector(dve)
            heads_vector(dve)
            t4k.vector(dve)
            a2.vector(dve)
            t5.vector(dve)
            close_vector(dve, o2, m2.norm)
            m2.vector(dve)
            conditioning_vector(dve)
            close_vector(dve, m2, n3)
            forget_vector(dve)
            a3.vector(dve)
            t7.vector(dve)
            gate_vector(dve, 0)
            close_vector(dve, o3, n4)
            mlp_vector(dve)

        @block.tensor
        def _(pe):
            pe.wait_ge(*first(N_FIRST))
            n1.turn(pe, 0)
            p1.tensor(pe)
            t1.tensor(pe)
            a1.tensor(pe)
            t2.tensor(pe)
            t2.ready(pe)
            close_tensor(pe, o1, m1.norm)
            m1.tensor(pe)
            close_tensor(pe, m1, n2)
            pa.tensor(pe)
            t3.tensor(pe)
            pq.tensor(pe)
            pkv.tensor(pe)
            t4q.tensor(pe)
            t4k.tensor(pe)
            a2.tensor(pe)
            t5.tensor(pe)
            t5.ready(pe)
            close_tensor(pe, o2, m2.norm)
            m2.tensor(pe)
            close_tensor(pe, m2, n3)
            pz.tensor(pe)
            channels_tensor(pe)
            a3.tensor(pe)
            t7.tensor(pe)
            t7.ready(pe)
            close_tensor(pe, o3, n4)
            mlp_tensor(pe)


INPUTS = ["x", "attn_norm", "ffn_norm", "diff_w_in", "diff_q_norm", "diff_k_norm", "diff_lambda_q1",
          "diff_lambda_k1", "diff_lambda_q2", "diff_lambda_k2", "diff_subln", "diff_w_out", "mla_w_a",
          "mla_q_a_norm", "mla_kv_a_norm", "mla_w_qb", "mla_w_kvb", "mla_q_norm", "mla_k_norm", "mla_w_out",
          "moe_w_group", "moe_b_group", "moe_w_expert", "moe_b_expert", "moe_w_gate", "moe_w_up", "moe_w_down",
          "c_2", "w_ada_2", "b_ada_2", "g_attn_2", "w_in_2", "b_f_2", "sinks_2", "w_out_2", "g_mlp_2", "w_up_2",
          "conv_w_2", "conv_b_2", "w_down_2", "g_final_2"]


def kernel(**inputs):
    import concourse.bacc as bacc
    from concourse.bass_utils import run_bass_kernel_spmd

    nc = bacc.Bacc("TRN2", target_bir_lowering=False, num_devices=1)
    arrays, tensors = {}, {}
    for name in INPUTS:
        a = np.ascontiguousarray(inputs[name])
        arrays["in_" + name] = a
        tensors[name] = nc.dram_tensor("in_" + name, a.shape, mybir.dt.from_np(a.dtype), kind="ExternalInput").ap()
    arrays["in_constants"] = shape_constants()
    tensors["constants"] = nc.dram_tensor("in_constants", arrays["in_constants"].shape, F32,
                                          kind="ExternalInput").ap()
    out = nc.dram_tensor("out_0", (1, S, D), F32, kind="ExternalOutput").ap()
    build(nc, tensors, out)
    r = run_bass_kernel_spmd(nc, [arrays], core_ids=[0])
    return r.results[0]["out_0"]
```
